# Optimizing a Trainium2 kernel written in Bass

```python
import math
import jax, jax.numpy as jnp
from jax import lax
import numpy as np

D_MODEL = 1024
BATCH = 1
SEQ = 256
DEPTH = 2

N_MIXERS = 4
EPS = 1e-6
Q_BLOCK = 128
CHUNK = 128

MLA_HEADS = 8
MLA_NOPE = 128
MLA_ROPE = 64
MLA_V = 128
MLA_Q_LORA = 384
MLA_KV_LORA = 256
ROPE_THETA = 10000.0

DIFF_HEADS = 8
DIFF_HD = D_MODEL // (2 * DIFF_HEADS)

MLSTM_HEADS = 8
MLSTM_QK = D_MODEL // 2 // MLSTM_HEADS
MLSTM_V = D_MODEL // MLSTM_HEADS

RET_HEADS = D_MODEL // 256
RET_QK = 256
RET_V = 2 * D_MODEL // RET_HEADS

FFN_HIDDEN = 2816
CONV_W = 3


def n_of(kind):
    return len(range(kind, DEPTH, N_MIXERS))

def rms_norm(x, g):
    xf = x.astype(jnp.float32)
    y = xf * lax.rsqrt(jnp.mean(xf * xf, -1, keepdims=True) + EPS)
    return (y * g.astype(jnp.float32)).astype(x.dtype)

def head_group_norm(x, g):
    xf = x.astype(jnp.float32)
    mu = jnp.mean(xf, -1, keepdims=True)
    xc = xf - mu
    y = xc * lax.rsqrt(jnp.mean(xc * xc, -1, keepdims=True) + EPS)
    return (y * g.astype(jnp.float32)).astype(x.dtype)

def query_blocks(t):
    b, s = t.shape[:2]
    return jnp.moveaxis(t.reshape(b, s // Q_BLOCK, Q_BLOCK, *t.shape[2:]), 1, 0)

def merge_blocks(t):
    t = jnp.moveaxis(t, 0, 1)
    return t.reshape(t.shape[0], -1, *t.shape[3:])

def rope_cos_sin(s, dim):
    inv = ROPE_THETA ** (-jnp.arange(0, dim, 2, dtype=jnp.float32) / dim)
    ang = jnp.arange(s, dtype=jnp.float32)[:, None] * inv[None, :]
    return jnp.cos(ang), jnp.sin(ang)

def apply_rope(x, cos, sin):
    half = x.shape[-1] // 2
    x1, x2 = x[..., :half], x[..., half:]
    cos = cos.astype(x.dtype)
    sin = sin.astype(x.dtype)
    return jnp.concatenate([x1 * cos - x2 * sin, x1 * sin + x2 * cos], -1)

def to_chunks(t):
    b, s = t.shape[:2]
    t = t.reshape(b, s // CHUNK, CHUNK, *t.shape[2:])
    return jnp.moveaxis(jnp.moveaxis(t, 1, 0), 3, 2)

def from_chunks(t):
    t = jnp.moveaxis(jnp.moveaxis(t, 2, 3), 0, 1)
    return t.reshape(t.shape[0], -1, *t.shape[3:])

def mla_mixer(x, w_dq, q_norm_g, w_uq, w_dkv, kv_norm_g, w_ukv, w_o):
    b, s, _ = x.shape
    H = MLA_HEADS
    cq = rms_norm(x @ w_dq, q_norm_g)
    q = (cq @ w_uq).reshape(b, s, H, MLA_NOPE + MLA_ROPE)
    ckv_kr = x @ w_dkv
    ckv = rms_norm(ckv_kr[..., :MLA_KV_LORA], kv_norm_g)
    kv = (ckv @ w_ukv).reshape(b, s, H, MLA_NOPE + MLA_V)
    k_nope, v = kv[..., :MLA_NOPE], kv[..., MLA_NOPE:]
    cos, sin = rope_cos_sin(s, MLA_ROPE)
    q_nope = q[..., :MLA_NOPE]
    q_rope = apply_rope(q[..., MLA_NOPE:], cos[:, None, :], sin[:, None, :])
    k_rope = apply_rope(ckv_kr[..., MLA_KV_LORA:], cos, sin)
    scale = (MLA_NOPE + MLA_ROPE) ** -0.5

    def block(args):
        qn, qr = args
        sc = (jnp.einsum('bqhd,bkhd->bhqk', qn, k_nope).astype(jnp.float32)
              + jnp.einsum('bqhr,bkr->bhqk', qr, k_rope).astype(jnp.float32)) * scale
        p = jax.nn.softmax(sc, -1).astype(v.dtype)
        return jnp.einsum('bhqk,bkhd->bqhd', p, v)

    o = merge_blocks(lax.map(block, (query_blocks(q_nope), query_blocks(q_rope))))
    return o.reshape(b, s, H * MLA_V) @ w_o

def diff_mixer(x, w_qkv, lam_p, subln_g, w_o, layer_idx):
    b, s, _ = x.shape
    H, d = DIFF_HEADS, DIFF_HD
    qkv = x @ w_qkv
    q = qkv[..., :2 * H * d].reshape(b, s, H, 2, d)
    k = qkv[..., 2 * H * d:4 * H * d].reshape(b, s, H, 2, d)
    v = qkv[..., 4 * H * d:].reshape(b, s, H, 2 * d)
    lam_init = 0.8 - 0.6 * math.exp(-0.3 * layer_idx)
    lp = lam_p.astype(jnp.float32)
    lam = jnp.exp(jnp.sum(lp[0] * lp[1])) - jnp.exp(jnp.sum(lp[2] * lp[3])) + lam_init
    slopes = 2.0 ** (-8.0 * jnp.arange(1, H + 1, dtype=jnp.float32) / H)
    pos = jnp.arange(s, dtype=jnp.int32)
    scale = d ** -0.5

    def block(args):
        qb, qpos = args
        sc = jnp.einsum('bqhjd,bkhjd->bhjqk', qb, k).astype(jnp.float32) * scale
        dist = jnp.abs(qpos[:, None] - pos[None, :]).astype(jnp.float32)
        sc = sc - slopes[None, :, None, None, None] * dist[None, None, None]
        p = jax.nn.softmax(sc, -1)
        a = (p[:, :, 0] - lam * p[:, :, 1]).astype(v.dtype)
        return jnp.einsum('bhqk,bkhd->bqhd', a, v)

    o = merge_blocks(lax.map(block, (query_blocks(q), pos.reshape(-1, Q_BLOCK))))
    o = rms_norm(o, subln_g) * (1.0 - lam_init)
    return o.reshape(b, s, H * 2 * d) @ w_o

def mlstm_chunkwise(q, k, v, i_pre, log_f):
    b, s, H, dk = q.shape
    dv = v.shape[-1]
    f32 = jnp.float32
    xs = (to_chunks(q.astype(f32)), to_chunks(k.astype(f32)), to_chunks(v.astype(f32)),
          to_chunks(i_pre), to_chunks(log_f))
    tri = jnp.tril(jnp.ones((CHUNK, CHUNK), bool))

    def step(carry, inp):
        C, n, m = carry
        qc, kc, vc, ic, fc = inp
        bcum = jnp.cumsum(fc, -1)
        dmat = jnp.where(tri, bcum[..., :, None] - bcum[..., None, :] + ic[..., None, :], -jnp.inf)
        m_inter = bcum + m[..., None]
        m_t = jnp.maximum(jnp.max(dmat, -1), m_inter)
        w_intra = jnp.exp(dmat - m_t[..., None])
        w_inter = jnp.exp(m_inter - m_t)
        sqk = jnp.einsum('bhtd,bhsd->bhts', qc, kc) * w_intra
        num = (w_inter[..., None] * jnp.einsum('bhtd,bhde->bhte', qc, C)
               + jnp.einsum('bhts,bhse->bhte', sqk, vc))
        den = w_inter * jnp.einsum('bhtd,bhd->bht', qc, n) + jnp.sum(sqk, -1)
        h = num / jnp.maximum(jnp.abs(den), jnp.exp(-m_t))[..., None]
        b_last = bcum[..., -1]
        g_s = b_last[..., None] - bcum + ic
        m_new = jnp.maximum(b_last + m, jnp.max(g_s, -1))
        w_s = jnp.exp(g_s - m_new[..., None])
        decay = jnp.exp(b_last + m - m_new)
        C_new = decay[..., None, None] * C + jnp.einsum('bhs,bhsd,bhse->bhde', w_s, kc, vc)
        n_new = decay[..., None] * n + jnp.einsum('bhs,bhsd->bhd', w_s, kc)
        return (C_new, n_new, m_new), h

    init = (jnp.zeros((b, H, dk, dv), f32), jnp.zeros((b, H, dk), f32), jnp.zeros((b, H), f32))
    _, hs = lax.scan(step, init, xs)
    return from_chunks(hs).astype(v.dtype)

def mlstm_mixer(x, w_in, b_gates, norm_g, w_out):
    b, s, _ = x.shape
    H, dk, dv = MLSTM_HEADS, MLSTM_QK, MLSTM_V
    proj = x @ w_in
    o1, o2, o3, o4 = H * dk, 2 * H * dk, 2 * H * dk + H * dv, 2 * H * dk + 2 * H * dv
    q = proj[..., :o1].reshape(b, s, H, dk)
    k = proj[..., o1:o2].reshape(b, s, H, dk) * (dk ** -0.5)
    v = proj[..., o2:o3].reshape(b, s, H, dv)
    o_gate = jax.nn.sigmoid(proj[..., o3:o4])
    g = (proj[..., o4:] + b_gates).astype(jnp.float32).reshape(b, s, 4, H)
    h_f = mlstm_chunkwise(q, k, v, g[:, :, 0], jax.nn.log_sigmoid(g[:, :, 1]))
    fl = lambda t: jnp.flip(t, 1)
    h_b = fl(mlstm_chunkwise(fl(q), fl(k), fl(v), fl(g[:, :, 2]), jax.nn.log_sigmoid(fl(g[:, :, 3]))))
    h = head_group_norm(h_f + h_b, norm_g.reshape(H, dv))
    return (h.reshape(b, s, H * dv) * o_gate) @ w_out

def retention_chunkwise(q, k, v, log_gamma):
    b, s, H, dk = q.shape
    dv = v.shape[-1]
    f32 = jnp.float32
    idx = jnp.arange(CHUNK, dtype=f32)
    rel = idx[:, None] - idx[None, :]
    dmask = jnp.exp(jnp.maximum(rel, 0.0)[None] * log_gamma[:, None, None]) * (rel >= 0)[None]
    xi = jnp.exp((idx[None] + 1.0) * log_gamma[:, None])
    zeta = jnp.exp((CHUNK - 1.0 - idx[None]) * log_gamma[:, None])
    g_chunk = jnp.exp(CHUNK * log_gamma)
    xs = (to_chunks(q.astype(f32)), to_chunks(k.astype(f32)), to_chunks(v.astype(f32)))

    def step(R, inp):
        qc, kc, vc = inp
        inner = jnp.einsum('bhts,bhse->bhte', jnp.einsum('bhtd,bhsd->bhts', qc, kc) * dmask, vc)
        cross = jnp.einsum('bhtd,bhde->bhte', qc, R) * xi[None, :, :, None]
        R_new = g_chunk[None, :, None, None] * R + jnp.einsum('bhsd,bhse->bhde', kc * zeta[None, :, :, None], vc)
        return R_new, inner + cross

    _, ys = lax.scan(step, jnp.zeros((b, H, dk, dv), f32), xs)
    return from_chunks(ys).astype(v.dtype)

def retention_mixer(x, w_in, decay_logit, norm_g, w_o):
    b, s, _ = x.shape
    H, dk, dv = RET_HEADS, RET_QK, RET_V
    proj = x @ w_in
    o1, o2, o3 = H * dk, 2 * H * dk, 2 * H * dk + H * dv
    q = proj[..., :o1].reshape(b, s, H, dk)
    k = proj[..., o1:o2].reshape(b, s, H, dk) * (dk ** -0.5)
    v = proj[..., o2:o3].reshape(b, s, H, dv)
    gate = proj[..., o3:]
    lg = jax.nn.log_sigmoid(decay_logit.astype(jnp.float32))
    fl = lambda t: jnp.flip(t, 1)
    y = retention_chunkwise(q, k, v, lg[0]) + fl(retention_chunkwise(fl(q), fl(k), fl(v), lg[1]))
    y = head_group_norm(y, norm_g.reshape(H, dv)).reshape(b, s, H * dv)
    return (jax.nn.silu(gate) * y) @ w_o

def conv_ffn(x, w_up, conv_w, conv_b, w_down):
    u = x @ w_up
    s = u.shape[1]
    half = CONV_W // 2
    up = jnp.pad(u, ((0, 0), (half, half), (0, 0)))
    c = conv_b
    for j in range(CONV_W):
        c = c + conv_w[j] * up[:, j:j + s]
    g, val = c[..., :FFN_HIDDEN], c[..., FFN_HIDDEN:]
    return (jax.nn.gelu(g) * val) @ w_down

def first_inputs(seed: int = 0) -> dict:
    key = jax.random.key(seed)
    ks = iter(jax.random.split(key, 40))
    D = D_MODEL
    nA, nB, nC, nD = n_of(0), n_of(1), n_of(2), n_of(3)

    def w(shape, fan_in):
        return jax.random.normal(next(ks), shape, jnp.float32) * (fan_in ** -0.5)

    def gain(shape):
        return 1.0 + 0.02 * jax.random.normal(next(ks), shape, jnp.float32)

    inp = {}
    inp['x'] = jax.random.normal(next(ks), (BATCH, SEQ, D), jnp.float32)
    inp['norm_g'] = gain((DEPTH, 4, D))
    inp['ffn_w_up'] = w((DEPTH, D, 2 * FFN_HIDDEN), D)
    inp['ffn_conv_w'] = w((DEPTH, CONV_W, 2 * FFN_HIDDEN), CONV_W)
    inp['ffn_conv_b'] = 0.01 * jax.random.normal(next(ks), (DEPTH, 2 * FFN_HIDDEN), jnp.float32)
    inp['ffn_w_down'] = w((DEPTH, FFN_HIDDEN, D), FFN_HIDDEN)
    inp['mla_w_dq'] = w((nA, D, MLA_Q_LORA), D)
    inp['mla_q_norm_g'] = gain((nA, MLA_Q_LORA))
    inp['mla_w_uq'] = w((nA, MLA_Q_LORA, MLA_HEADS * (MLA_NOPE + MLA_ROPE)), MLA_Q_LORA)
    inp['mla_w_dkv'] = w((nA, D, MLA_KV_LORA + MLA_ROPE), D)
    inp['mla_kv_norm_g'] = gain((nA, MLA_KV_LORA))
    inp['mla_w_ukv'] = w((nA, MLA_KV_LORA, MLA_HEADS * (MLA_NOPE + MLA_V)), MLA_KV_LORA)
    inp['mla_w_o'] = w((nA, MLA_HEADS * MLA_V, D), MLA_HEADS * MLA_V)
    inp['diff_w_qkv'] = w((nB, D, 3 * D), D)
    inp['diff_lambda'] = 0.1 * jax.random.normal(next(ks), (nB, 4, DIFF_HD), jnp.float32)
    inp['diff_subln_g'] = gain((nB, 2 * DIFF_HD))
    inp['diff_w_o'] = w((nB, D, D), D)
    H = MLSTM_HEADS
    inp['mlstm_w_in'] = w((nC, D, 2 * H * MLSTM_QK + 2 * H * MLSTM_V + 4 * H), D)
    i_bias = 0.1 * jax.random.normal(next(ks), (nC, 2, H), jnp.float32)
    f_bias = jnp.linspace(3.0, 6.0, H, dtype=jnp.float32)[None, None] + 0.1 * jax.random.normal(next(ks), (nC, 2, H), jnp.float32)
    inp['mlstm_b_gates'] = jnp.stack([i_bias[:, 0], f_bias[:, 0], i_bias[:, 1], f_bias[:, 1]], 1).reshape(nC, 4 * H)
    inp['mlstm_norm_g'] = gain((nC, H * MLSTM_V))
    inp['mlstm_w_out'] = w((nC, H * MLSTM_V, D), H * MLSTM_V)
    Hr = RET_HEADS
    inp['ret_w_in'] = w((nD, D, 2 * Hr * RET_QK + 2 * Hr * RET_V), D)
    eps_h = 2.0 ** (-5.0 - np.arange(Hr, dtype=np.float32))
    base_logit = jnp.asarray(np.log((1.0 - eps_h) / eps_h), jnp.float32)
    inp['ret_decay_logit'] = base_logit[None, None] + 0.1 * jax.random.normal(next(ks), (nD, 2, Hr), jnp.float32)
    inp['ret_norm_g'] = gain((nD, Hr * RET_V))
    inp['ret_w_o'] = w((nD, Hr * RET_V, D), Hr * RET_V)
    return inp

def first_block(x, norm_g, ffn_w_up, ffn_conv_w, ffn_conv_b, ffn_w_down,
              mla_w_dq, mla_q_norm_g, mla_w_uq, mla_w_dkv, mla_kv_norm_g, mla_w_ukv, mla_w_o,
              diff_w_qkv, diff_lambda, diff_subln_g, diff_w_o,
              mlstm_w_in, mlstm_b_gates, mlstm_norm_g, mlstm_w_out,
              ret_w_in, ret_decay_logit, ret_norm_g, ret_w_o):
    h = x
    for i in range(DEPTH):
        kind, j = i % N_MIXERS, i // N_MIXERS
        a = rms_norm(h, norm_g[i, 0])
        if kind == 0:
            a = mla_mixer(a, mla_w_dq[j], mla_q_norm_g[j], mla_w_uq[j], mla_w_dkv[j],
                          mla_kv_norm_g[j], mla_w_ukv[j], mla_w_o[j])
        elif kind == 1:
            a = diff_mixer(a, diff_w_qkv[j], diff_lambda[j], diff_subln_g[j], diff_w_o[j], i)
        elif kind == 2:
            a = mlstm_mixer(a, mlstm_w_in[j], mlstm_b_gates[j], mlstm_norm_g[j], mlstm_w_out[j])
        else:
            a = retention_mixer(a, ret_w_in[j], ret_decay_logit[j], ret_norm_g[j], ret_w_o[j])
        h = h + rms_norm(a, norm_g[i, 1])
        f = conv_ffn(rms_norm(h, norm_g[i, 2]), ffn_w_up[i], ffn_conv_w[i], ffn_conv_b[i], ffn_w_down[i])
        h = h + rms_norm(f, norm_g[i, 3])
    return h


DEPTH_2 = 1

D_MIX = D_MODEL
NEG = -1e30
FORCE = 1e6
F_FLOOR = 1e-30
NSA_HEADS = 8
NSA_KV_GROUPS = 2
NSA_HD = 64
CMP_LEN = 32
CMP_STRIDE = 16
CMP_HID = 256
SEL_BLOCK = 64
SEL_TOPK = 16
SEL_QBLOCK = 32
WINDOW = 512
WIN_QBLOCK = 128
HG_HEADS = 4
HG_DK = 128
HG_DV = 128
HG_CHUNK = 64
D_FF = 2752

NSA_WIDTH = NSA_HEADS * NSA_HD
HG_WIDTH = HG_HEADS * HG_DV
KV_W = NSA_KV_GROUPS * NSA_HD
IN_SIZES = (NSA_WIDTH, KV_W, KV_W, KV_W, KV_W, KV_W, KV_W, NSA_HEADS * 3,
            HG_HEADS * HG_DK, HG_HEADS * HG_DK, HG_WIDTH, HG_WIDTH)
IN_COLS = sum(IN_SIZES)
IN_SPLITS = tuple(int(v) for v in np.cumsum(IN_SIZES)[:-1])


def rms_norm_2(x, g):
    xf = x.astype(jnp.float32)
    y = xf * lax.rsqrt(jnp.mean(xf * xf, axis=-1, keepdims=True) + EPS)
    return (y * g.astype(jnp.float32)).astype(x.dtype)

def swiglu(x, w_gu, w_down):
    gate, up = jnp.split(x @ w_gu, 2, axis=-1)
    return (jax.nn.silu(gate) * up) @ w_down

def alibi_slopes(n):
    return jnp.asarray([2.0 ** (-8.0 * (i + 1) / n) for i in range(n)], dtype=jnp.float32)

def compress(kv, pos_emb, w1, w2):
    B, S, G, dk = kv.shape
    chunks = kv.reshape(B, S // CMP_STRIDE, CMP_STRIDE, G, dk)
    blocks = jnp.concatenate([chunks[:, :-1], chunks[:, 1:]], axis=2) + pos_emb[:, None, :]
    nb = blocks.shape[1]
    flat = blocks.transpose(0, 1, 3, 2, 4).reshape(B, nb, G, CMP_LEN * dk)
    return jax.nn.gelu(flat @ w1) @ w2

def nsa_group(q, k_c, v_c, k_s, v_s, k_w, v_w, gate_logits,
              cmp_pos_k, cmp_pos_v, cmp_k_w1, cmp_k_w2, cmp_v_w1, cmp_v_w2):
    B, S = q.shape[:2]
    G, Hg, dk = NSA_KV_GROUPS, NSA_HEADS // NSA_KV_GROUPS, NSA_HD
    scale = dk ** -0.5
    slopes = alibi_slopes(NSA_HEADS).reshape(G, Hg)
    q5 = q.reshape(B, S, G, Hg, dk)
    kv4 = lambda t: t.reshape(B, S, G, dk)
    pos = jnp.arange(S, dtype=jnp.int32)

    kc = compress(kv4(k_c), cmp_pos_k, cmp_k_w1, cmp_k_w2)
    vc = compress(kv4(v_c), cmp_pos_v, cmp_v_w1, cmp_v_w2)
    nb = kc.shape[1]
    blk_end = jnp.arange(nb, dtype=jnp.int32) * CMP_STRIDE + (CMP_LEN - 1)
    dist_c = pos[:, None] - blk_end[None, :]
    s_c = jnp.einsum('bsgnd,bcgd->bsgnc', q5, kc).astype(jnp.float32) * scale
    s_c = s_c - slopes[:, :, None] * dist_c.astype(jnp.float32)[:, None, None, :]
    s_c = jnp.where((dist_c >= 0)[:, None, None, :], s_c, NEG)
    p_c = jax.nn.softmax(s_c, axis=-1)
    p_c = jnp.where((pos >= CMP_LEN - 1)[:, None, None, None], p_c, 0.0)
    o_cmp = jnp.einsum('bsgnc,bcgd->bsgnd', p_c.astype(vc.dtype), vc)

    imp = p_c.sum(axis=3)
    padded = jnp.pad(imp, ((0, 0), (0, 0), (0, 0), (1, 1)))
    chunk_imp = padded[..., :-1] + padded[..., 1:]
    ns = S // SEL_BLOCK
    p_slc = chunk_imp.reshape(B, S, G, ns, SEL_BLOCK // CMP_STRIDE).sum(-1)
    blk = jnp.arange(ns, dtype=jnp.int32)
    cur = pos // SEL_BLOCK
    forced = (blk[None] == 0) | (blk[None] == cur[:, None]) | (blk[None] == cur[:, None] - 1)
    causal = blk[None] * SEL_BLOCK <= pos[:, None]
    score = jnp.where(forced[:, None], FORCE, jnp.where(causal[:, None], p_slc, NEG))
    n_sel = min(SEL_TOPK, ns)
    _, sel_idx = lax.top_k(score, n_sel)

    k_blocks = kv4(k_s).reshape(B, ns, SEL_BLOCK, G, dk).transpose(0, 3, 1, 2, 4)
    v_blocks = kv4(v_s).reshape(B, ns, SEL_BLOCK, G, dk).transpose(0, 3, 1, 2, 4)
    nq = S // SEL_QBLOCK
    b_ix = jnp.arange(B)[:, None, None, None]
    g_ix = jnp.arange(G)[None, None, :, None]
    l_ar = jnp.arange(SEL_BLOCK, dtype=jnp.int32)

    def sel_step(args):
        qb, idx, qi = args
        kg = k_blocks[b_ix, g_ix, idx]
        vg = v_blocks[b_ix, g_ix, idx]
        s = jnp.einsum('btgnd,btgkld->btgnkl', qb, kg).astype(jnp.float32) * scale
        qpos = qi * SEL_QBLOCK + jnp.arange(SEL_QBLOCK, dtype=jnp.int32)
        kpos = idx[..., None] * SEL_BLOCK + l_ar
        dist = qpos[None, :, None, None, None] - kpos
        s = s - slopes[None, None, :, :, None, None] * dist.astype(jnp.float32)[:, :, :, None]
        s = jnp.where((dist >= 0)[:, :, :, None], s, NEG)
        p = jax.nn.softmax(s.reshape(s.shape[:4] + (-1,)), axis=-1).reshape(s.shape)
        return jnp.einsum('btgnkl,btgkld->btgnd', p.astype(vg.dtype), vg)

    o_sel = lax.map(sel_step, (q5.reshape(B, nq, SEL_QBLOCK, G, Hg, dk).swapaxes(0, 1),
                               sel_idx.reshape(B, nq, SEL_QBLOCK, G, n_sel).swapaxes(0, 1),
                               jnp.arange(nq, dtype=jnp.int32)))
    o_sel = o_sel.swapaxes(0, 1).reshape(B, S, G, Hg, dk)

    nwq = S // WIN_QBLOCK
    n_kb = WINDOW // WIN_QBLOCK + 1
    kw_len = n_kb * WIN_QBLOCK

    def band(t):
        tp = jnp.pad(kv4(t), ((0, 0), (WINDOW, 0), (0, 0), (0, 0)))
        tp = tp.reshape(B, nwq + WINDOW // WIN_QBLOCK, WIN_QBLOCK, G, dk)
        return jnp.concatenate([tp[:, j:j + nwq] for j in range(n_kb)], axis=2).swapaxes(0, 1)

    def win_step(args):
        qb, kb, vb, qi = args
        s = jnp.einsum('btgnd,bkgd->btgnk', qb, kb).astype(jnp.float32) * scale
        qpos = qi * WIN_QBLOCK + jnp.arange(WIN_QBLOCK, dtype=jnp.int32)
        kpos = qi * WIN_QBLOCK - WINDOW + jnp.arange(kw_len, dtype=jnp.int32)
        dist = qpos[:, None] - kpos[None, :]
        valid = (dist >= 0) & (dist < WINDOW) & (kpos >= 0)[None, :]
        s = s - slopes[None, None, :, :, None] * dist.astype(jnp.float32)[None, :, None, None, :]
        s = jnp.where(valid[None, :, None, None, :], s, NEG)
        p = jax.nn.softmax(s, axis=-1)
        return jnp.einsum('btgnk,bkgd->btgnd', p.astype(vb.dtype), vb)

    o_win = lax.map(win_step, (q5.reshape(B, nwq, WIN_QBLOCK, G, Hg, dk).swapaxes(0, 1),
                               band(k_w), band(v_w), jnp.arange(nwq, dtype=jnp.int32)))
    o_win = o_win.swapaxes(0, 1).reshape(B, S, G, Hg, dk)

    g = jax.nn.sigmoid(gate_logits.astype(jnp.float32)).reshape(B, S, G, Hg, 3)
    o = (g[..., 0:1] * o_cmp.astype(jnp.float32) + g[..., 1:2] * o_sel.astype(jnp.float32)
         + g[..., 2:3] * o_win.astype(jnp.float32))
    return o.reshape(B, S, NSA_WIDTH).astype(q.dtype)

def hgrn2_group(q, f_logit, i_in, g_in, lower_bound, out_norm):
    B, S = q.shape[:2]
    H, dk, dv, C = HG_HEADS, HG_DK, HG_DV, HG_CHUNK
    qf = jax.nn.silu(q.astype(jnp.float32)).reshape(B, S, H, dk)
    lb = lower_bound.astype(jnp.float32)
    z = f_logit.astype(jnp.float32)
    f = lb + (1.0 - lb) * jax.nn.sigmoid(z)
    logf = jnp.log(jnp.maximum(f, F_FLOOR)).reshape(B, S, H, dk)
    kf = ((1.0 - lb) * jax.nn.sigmoid(-z)).reshape(B, S, H, dk)
    vf = i_in.astype(jnp.float32).reshape(B, S, H, dv)
    nc = S // C
    to_chunks = lambda t: t.reshape(B, nc, C, H, t.shape[-1]).transpose(1, 0, 3, 2, 4)
    tril = jnp.tril(jnp.ones((C, C), dtype=bool))

    def step(state, inp):
        qc, kc, vc, lf = inp
        b = jnp.cumsum(lf, axis=2)
        decay = b[:, :, :, None, :] - b[:, :, None, :, :]
        decay = jnp.exp(jnp.where(tril[:, :, None], decay, NEG))
        a = jnp.einsum('bhtd,bhtsd,bhsd->bhts', qc, decay, kc)
        o_intra = jnp.einsum('bhts,bhsv->bhtv', a, vc)
        o_inter = jnp.einsum('bhtd,bhdv->bhtv', qc * jnp.exp(b), state)
        b_last = b[:, :, -1]
        new_state = (jnp.exp(b_last)[..., None] * state
                     + jnp.einsum('bhsd,bhsv->bhdv', kc * jnp.exp(b_last[:, :, None] - b), vc))
        return new_state, o_intra + o_inter

    state0 = jnp.zeros((B, H, dk, dv), jnp.float32)
    _, o = lax.scan(step, state0, (to_chunks(qf), to_chunks(kf), to_chunks(vf), to_chunks(logf)))
    o = o.transpose(1, 0, 3, 2, 4).reshape(B, S, H, dv)
    o = o * lax.rsqrt(jnp.mean(o * o, axis=-1, keepdims=True) + EPS) * out_norm.astype(jnp.float32)
    o = o.reshape(B, S, HG_WIDTH) * jax.nn.silu(g_in.astype(jnp.float32))
    return o.astype(q.dtype)

def hybrid_mixer(h, w_in, cmp_pos_k, cmp_pos_v, cmp_k_w1, cmp_k_w2, cmp_v_w1, cmp_v_w2,
                 lower_bound, hg_norm, w_out):
    parts = jnp.split(h @ w_in, IN_SPLITS, axis=-1)
    nq, k_c, v_c, k_s, v_s, k_w, v_w, gl, hq, hf, hi, hg = parts
    o_nsa = nsa_group(nq, k_c, v_c, k_s, v_s, k_w, v_w, gl,
                      cmp_pos_k, cmp_pos_v, cmp_k_w1, cmp_k_w2, cmp_v_w1, cmp_v_w2)
    o_hg = hgrn2_group(hq, hf, hi, hg, lower_bound, hg_norm)
    return jnp.concatenate([o_nsa, o_hg], axis=-1) @ w_out

def second_inputs(seed: int = 0) -> dict:
    key = jax.random.key(seed)
    ks = jax.random.split(key, 20)
    nrm = lambda k, shape, s: jax.random.normal(k, shape, jnp.float32) * s
    gain = lambda k, shape: 1.0 + 0.02 * jax.random.normal(k, shape, jnp.float32)
    L = DEPTH_2
    return {
        "x": jax.random.normal(ks[0], (BATCH, SEQ, D_MODEL), jnp.float32),
        "ffn1_norm": gain(ks[1], (L, D_MODEL)),
        "ffn1_w_gu": nrm(ks[2], (L, D_MODEL, 2 * D_FF), D_MODEL ** -0.5),
        "ffn1_w_down": nrm(ks[3], (L, D_FF, D_MODEL), D_FF ** -0.5),
        "mix_norm": gain(ks[4], (L, D_MODEL)),
        "w_in": nrm(ks[5], (L, D_MODEL, IN_COLS), D_MODEL ** -0.5),
        "cmp_pos_k": nrm(ks[6], (L, CMP_LEN, NSA_HD), 0.02),
        "cmp_pos_v": nrm(ks[7], (L, CMP_LEN, NSA_HD), 0.02),
        "cmp_k_w1": nrm(ks[8], (L, CMP_LEN * NSA_HD, CMP_HID), (CMP_LEN * NSA_HD) ** -0.5),
        "cmp_k_w2": nrm(ks[9], (L, CMP_HID, NSA_HD), CMP_HID ** -0.5),
        "cmp_v_w1": nrm(ks[10], (L, CMP_LEN * NSA_HD, CMP_HID), (CMP_LEN * NSA_HD) ** -0.5),
        "cmp_v_w2": nrm(ks[11], (L, CMP_HID, NSA_HD), CMP_HID ** -0.5),
        "hgrn_lower_bound": nrm(ks[12], (L, HG_HEADS * HG_DK), 0.1),
        "hgrn_out_norm": gain(ks[13], (L, HG_DV)),
        "w_out": nrm(ks[14], (L, D_MIX, D_MODEL), D_MIX ** -0.5),
        "ffn2_norm": gain(ks[15], (L, D_MODEL)),
        "ffn2_w_gu": nrm(ks[16], (L, D_MODEL, 2 * D_FF), D_MODEL ** -0.5),
        "ffn2_w_down": nrm(ks[17], (L, D_FF, D_MODEL), D_FF ** -0.5),
        "final_norm": gain(ks[18], (D_MODEL,)),
    }

def second_block(x, ffn1_norm, ffn1_w_gu, ffn1_w_down, mix_norm, w_in, cmp_pos_k, cmp_pos_v,
              cmp_k_w1, cmp_k_w2, cmp_v_w1, cmp_v_w2, hgrn_lower_bound, hgrn_out_norm, w_out,
              ffn2_norm, ffn2_w_gu, ffn2_w_down, final_norm):
    lb_sm = jax.nn.softmax(hgrn_lower_bound.astype(jnp.float32), axis=0)
    lower_bounds = jnp.cumsum(lb_sm, axis=0) - lb_sm[0]
    h = x
    for l in range(DEPTH_2):
        h = h + 0.5 * swiglu(rms_norm_2(h, ffn1_norm[l]), ffn1_w_gu[l], ffn1_w_down[l])
        h = h + hybrid_mixer(rms_norm_2(h, mix_norm[l]), w_in[l], cmp_pos_k[l], cmp_pos_v[l],
                             cmp_k_w1[l], cmp_k_w2[l], cmp_v_w1[l], cmp_v_w2[l],
                             lower_bounds[l], hgrn_out_norm[l], w_out[l])
        h = h + 0.5 * swiglu(rms_norm_2(h, ffn2_norm[l]), ffn2_w_gu[l], ffn2_w_down[l])
    return rms_norm_2(h, final_norm)


def setup_inputs(seed=0):
    out = dict(first_inputs(seed))
    for name, value in second_inputs(seed + 1).items():
        if name != "x":
            out[name + "_2"] = value
    return out


def reference(
    x, norm_g, ffn_w_up, ffn_conv_w, ffn_conv_b, ffn_w_down, mla_w_dq, mla_q_norm_g, mla_w_uq,
    mla_w_dkv, mla_kv_norm_g, mla_w_ukv, mla_w_o, diff_w_qkv, diff_lambda, diff_subln_g,
    diff_w_o, mlstm_w_in, mlstm_b_gates, mlstm_norm_g, mlstm_w_out, ret_w_in, ret_decay_logit,
    ret_norm_g, ret_w_o, ffn1_norm_2, ffn1_w_gu_2, ffn1_w_down_2, mix_norm_2, w_in_2,
    cmp_pos_k_2, cmp_pos_v_2, cmp_k_w1_2, cmp_k_w2_2, cmp_v_w1_2, cmp_v_w2_2,
    hgrn_lower_bound_2, hgrn_out_norm_2, w_out_2, ffn2_norm_2, ffn2_w_gu_2, ffn2_w_down_2,
    final_norm_2,
):
    x = first_block(
        x, norm_g, ffn_w_up, ffn_conv_w, ffn_conv_b, ffn_w_down, mla_w_dq, mla_q_norm_g,
        mla_w_uq, mla_w_dkv, mla_kv_norm_g, mla_w_ukv, mla_w_o, diff_w_qkv, diff_lambda,
        diff_subln_g, diff_w_o, mlstm_w_in, mlstm_b_gates, mlstm_norm_g, mlstm_w_out, ret_w_in,
        ret_decay_logit, ret_norm_g, ret_w_o,
    )
    return second_block(
        x, ffn1_norm_2, ffn1_w_gu_2, ffn1_w_down_2, mix_norm_2, w_in_2, cmp_pos_k_2,
        cmp_pos_v_2, cmp_k_w1_2, cmp_k_w2_2, cmp_v_w1_2, cmp_v_w2_2, hgrn_lower_bound_2,
        hgrn_out_norm_2, w_out_2, ffn2_norm_2, ffn2_w_gu_2, ffn2_w_down_2, final_norm_2,
    )


_drawn_inputs = setup_inputs


def setup_inputs(seed=0):
    import zlib

    import numpy as np

    out = dict(_drawn_inputs(seed))
    spreads = {}
    factors = {'ffn_conv_b': 4.419,
     'mla_q_norm_g': 2.781,
     'diff_subln_g': 4.915,
     'ffn1_norm_2': 8.0,
     'mix_norm_2': 8.0,
     'cmp_pos_k_2': 52.769,
     'cmp_pos_v_2': 64.0,
     'cmp_k_w1_2': 3.693,
     'cmp_k_w2_2': 3.65,
     'hgrn_out_norm_2': 25.18,
     'ffn2_norm_2': 32.57,
     'final_norm_2': 7.715}
    for name, (base, spread) in spreads.items():
        noise = np.random.default_rng([zlib.crc32(name.encode()), seed]).standard_normal(out[name].shape)
        drawn = base * np.exp(spread * noise) if base else spread * noise
        out[name] = __import__('jax').numpy.asarray(drawn.astype(out[name].dtype))
    for name, factor in factors.items():
        out[name] = (out[name] * factor).astype(out[name].dtype)
    return out
```

```python
import math
from contextlib import ExitStack

import numpy as np

import concourse.bass as bass
from concourse import mybir

F32 = mybir.dt.float32
F32R = mybir.dt.float32r
BF16 = mybir.dt.bfloat16
U32 = mybir.dt.uint32
ACT = mybir.ActivationFunctionType
ALU = mybir.AluOpType
AX = mybir.AxisListType.X

P = 128
SEQ = 256
TT = SEQ // P
D = 1024
KC = D // P
EPS = 1e-6
BANK = 512

H = 8
NOPE, ROPE, VD = 128, 64, 128
QL, KVL = 384, 256
F1, F2 = 2816, 2752
FT = 22
LAM_INIT = 0.8 - 0.6 * math.exp(-0.3)
NSA_Q, HG = 512, 512
HD = 64
CMP = 32
STRIDE = 16
NB = SEQ // STRIDE - 1
HGH = 4
MASKED = 1e30

V_NORM = 0
V_FFN1 = V_NORM + 64
V_MIX = V_FFN1 + 8
V_FFN2 = V_MIX + 8
V_QN = V_FFN2 + 8
V_KVN = V_QN + 3
V_LB = V_KVN + 2
V_SUB = V_LB + 4
V_POSK = V_SUB + 1
V_POSV = V_POSK + 16
V_CW = V_POSV + 16
V_CB = V_CW + 264
V_ALL = V_CB + 88

C_Q, C_KC, C_VC, C_KS, C_VS, C_KW, C_VW, C_GL = 0, 512, 640, 768, 896, 1024, 1152, 1280
C_HQ, C_HF, C_HI = 1304, 1816, 2328

U_DQ = 0
U_DKV = U_DQ + 2
U_UQ = U_DKV + 2
U_UKV = U_UQ + 4
U_MO = U_UKV + 2
U_F0 = U_MO + 4
U_QK = U_F0 + FT
U_V = U_QK + 8
U_DO = U_V + 4
U_F1 = U_DO + 4
U_F2 = U_F1 + FT
U_NQ = U_F2 + FT
U_NC = U_NQ + 2
U_NS = U_NC + 1
U_NW = U_NS + 1
U_NG = U_NW + 1
U_HQ = U_NG + 1
U_HF = U_HQ + 2
U_HI = U_HF + 2
U_CK = U_HI + 4
U_CV = U_CK + 2
U_WO = U_CV + 2
U_F3 = U_WO + 4
U_END = U_F3 + FT
U_OF_FFN = [U_F0, U_F1, U_F2, U_F3]
LOOPED = 9

N_MLA, N_F0, N_DIFF, N_F1, N_F2, N_MIX, N_F3, N_FINAL = range(8)


def constants():
    pos = np.arange(SEQ, dtype=np.float32)
    q = pos.reshape(TT, P).T[:, :, None]
    dist = np.abs(q - pos[None, None, :]).astype(np.float32)
    signed = q - pos[None, None, :]
    causal = np.where(signed >= 0, signed, MASKED).astype(np.float32)
    causal = np.concatenate([causal[:, 0, :P], causal[:, 1, :]], axis=1)
    ends = (np.arange(NB) * STRIDE + CMP - 1).astype(np.float32)
    cmp = q - ends[None, None, :]
    cmp = np.where(cmp >= 0, cmp, MASKED).astype(np.float32)
    rows = (q[:, :, 0] >= CMP - 1).astype(np.float32)
    inv = (np.float32(10000.0) ** (-np.arange(0, ROPE, 2, dtype=np.float32) / np.float32(ROPE))).astype(np.float32)
    ang = pos[:, None] * inv[None, :]
    cos, sin = np.cos(ang).astype(np.float32), np.sin(ang).astype(np.float32)
    cos2 = np.concatenate([cos, cos], 1)
    sin2 = np.concatenate([sin, -sin], 1)
    tok = lambda a: np.ascontiguousarray(a.reshape(TT, P, -1).transpose(1, 0, 2))
    s = np.arange(P)[:, None]
    t = np.arange(P)[None, :]
    masks = np.zeros((P, 8, P), np.float32)
    masks[:, 0, :] = s == t
    for i in range(7):
        m = 1 << i
        masks[:, i + 1, :] = (s // (2 * m) == t // (2 * m)) & (s % (2 * m) < m) & (t % (2 * m) >= m)
    return {
        "ident": np.eye(P, dtype=np.float32), "dist": dist.reshape(P, -1), "causal": causal,
        "cdist": cmp.reshape(P, -1), "crows": rows,
        "ropek": np.concatenate([tok(cos2), tok(sin2)], 1).reshape(P, -1),
        "ropeq": np.concatenate([cos2.T, sin2.T], 1), "masks": masks.reshape(P, -1),
    }


(R_MLA, R_CQ, R_P0, R_F0, R_P1, R_DIFF, R_SUB, R_P2, R_F1, R_P3, R_F2, R_MIX, R_HG, R_F3, R_FINAL,
 R_END) = range(16)
R_N = {R_CQ: 4, R_SUB: 16, R_HG: 8}
R_OF_NORM = [R_MLA, R_F0, R_DIFF, R_F1, R_F2, R_MIX, R_F3, R_FINAL]
R_OF_POST = [R_P0, R_P1, R_P2, R_P3]
V_OF_NORM = [V_NORM, V_NORM + 16, V_NORM + 32, V_NORM + 48, V_FFN1, V_MIX, V_FFN2]
M_SCALE = (NOPE + ROPE) ** -0.5
D_SCALE = HD ** -0.5
N_PARTS = [(768, NB), (768 + NB, NB), (0, P), (P, 2 * P), (3 * P, P), (4 * P, 2 * P)]


class Chain:

    def __init__(self, eng, sem):
        self.eng, self.sem, self.n = eng, sem, 0

    def put(self, ins):
        ins.then_inc(self.sem, 1)
        self.n += 1
        return self.n

    def wait(self, n=None):
        self.eng.wait_ge(self.sem, self.n if n is None else n)

    def link(self, ins):
        self.put(ins)
        self.wait()


def program(nc, a, out):
    ctx = ExitStack()
    sems = {}

    def S(name):
        if name not in sems:
            sems[name] = ctx.enter_context(nc.semaphore(name))
        return sems[name]

    def sb(name, shape, dt=F32):
        return ctx.enter_context(nc.sbuf_tensor(name, shape, dt))

    with ctx:
        psum = ctx.enter_context(nc.psum_tensor("psum", [P, 8, BANK], F32))

        resid = sb("resid", [P, TT, D])
        normed = sb("normed", [P, TT, D])
        act_hi = sb("act_hi", [P, KC, SEQ], F32R)
        act_lo = sb("act_lo", [P, KC, SEQ], F32R)
        raw_u = sb("raw_u", [P, 2, 2048])
        hi_u = sb("hi_u", [P, 2, 2048], F32R)
        lo_u = sb("lo_u", [P, 2, 2048], F32R)
        raw_d = sb("raw_d", [P, 2, 1024])
        hi_d = sb("hi_d", [P, 2, 1024], F32R)
        lo_d = sb("lo_d", [P, 2, 1024], F32R)
        hid_hi = sb("hid_hi", [P, 2, SEQ], F32R)
        hid_lo = sb("hid_lo", [P, 2, SEQ], F32R)
        gain_row = sb("gain_row", [P, 2, D])
        vecs = sb("vecs", [P, V_ALL])
        ident = sb("ident", [P, P])
        zeros = sb("zeros", [P, BANK], BF16)
        half = sb("half", [P, 16])
        st = sb("st", [P, R_END, 16])
        junk = sb("junk", [P, D])
        soft = sb("soft", [P, 8, 4, 8])
        lam = sb("lam", [P, 272])
        junk_d = sb("junk_d", [P, P])
        bound = sb("bound", [P, 6, 4])
        top = sb("top", [P, 8])
        masks = sb("masks", [P, 8, P])
        cdist = sb("cdist", [P, TT, NB])
        crows = sb("crows", [P, TT])
        w2k = sb("w2k", [P, 2, HD])
        w2v = sb("w2v", [P, 2, HD])
        hgain = sb("hgain", [P, P])
        dist = sb("dist", [P, TT, SEQ])
        causal = sb("causal", [P, 3, P])
        arena = sb("arena", [P, 12288])

        def ar(at, *shape, p=P):
            n = int(np.prod(shape))
            v = arena[0:p, at:at + n]
            if len(shape) == 2:
                v = v.rearrange("p (a b) -> p a b", a=shape[0])
            if len(shape) == 3:
                v = v.rearrange("p (a b c) -> p a b c", a=shape[0], b=shape[1])
            return v

        vrows = ar(0, 6, P)
        VROWS = [(V_NORM, 98), (V_POSK, 32), (V_CW, 88), (V_CW + 88, 88), (V_CW + 176, 88), (V_CB, 88)]
        cg, cv, gg, hf = (ar(512 * i, 2, SEQ) for i in range(4))

        def u_slot(t, u):
            return t[:, u % 2, :]

        def cols(w, c0, n):
            return w[:, c0:c0 + n].rearrange("(k p) n -> p k n", p=P)

        def rows(w, k0, n):
            return w[k0 * P:(k0 + n) * P, :].rearrange("(k p) n -> p k n", p=P)

        w_up, w_down = a["ffn_w_up"], a["ffn_w_down"]
        gu = [None, None, a["ffn1_w_gu_2"][0], a["ffn2_w_gu_2"][0]]
        dn = [w_down[0], w_down[1], a["ffn1_w_down_2"][0], a["ffn2_w_down_2"][0]]
        gu[0], gu[1] = w_up[0], w_up[1]
        FW = [F1, F1, F2, F2]
        units = {}
        w_in = a["w_in_2"][0]
        for i in range(2):
            units[U_DQ + i] = rows(a["mla_w_dq"][0], 4 * i, 4)
            units[U_DKV + i] = rows(a["mla_w_dkv"][0], 4 * i, 4)
            units[U_UKV + i] = cols(a["mla_w_ukv"][0], 1024 * i, 1024)
            units[U_NQ + i] = cols(w_in, C_Q + 256 * i, 256)
            units[U_HQ + i] = cols(w_in, C_HQ + 256 * i, 256)
            units[U_HF + i] = cols(w_in, C_HF + 256 * i, 256)
            units[U_CK + i] = rows(a["cmp_k_w1_2"][0], 8 * i, 8)
            units[U_CV + i] = rows(a["cmp_v_w1_2"][0], 8 * i, 8)
        for i in range(4):
            units[U_UQ + i] = cols(a["mla_w_uq"][0], 384 * i, 384)
            units[U_MO + i] = rows(a["mla_w_o"][0], 2 * i, 2)
            units[U_V + i] = rows(a["diff_w_qkv"][0][:, 2048:3072], 2 * i, 2)
            units[U_DO + i] = rows(a["diff_w_o"][0], 2 * i, 2)
            units[U_HI + i] = rows(w_in[:, C_HI:C_HI + 1024], 2 * i, 2)
            units[U_WO + i] = rows(a["w_out_2"][0], 2 * i, 2)
        for i in range(8):
            units[U_QK + i] = cols(a["diff_w_qkv"][0], 256 * i, 256)
        units[U_NC] = cols(w_in, C_KC, 256)
        units[U_NS] = cols(w_in, C_KS, 256)
        units[U_NW] = cols(w_in, C_KW, 256)
        units[U_NG] = cols(w_in, C_GL, 24)

        def width(f, t):
            return min(P, FW[f] - t * P) if isinstance(t, int) else P

        def unit_view(t, u):
            if isinstance(u, int) and u in units:
                k, n = units[u].shape[1], units[u].shape[2]
                return u_slot(t, u)[:, 0:k * n].rearrange("p (k n) -> p k n", k=k)
            return u_slot(t, u)

        def up_view(t, slot, s, n):
            return t[:, slot, 1024 * s:1024 * s + 1024].rearrange("p (k n) -> p k n", k=KC)[:, :, 0:n]

        m_q = ar(0, H, SEQ)
        m_qr = ar(2048, H, SEQ, p=ROPE)
        m_k = ar(4096, H, SEQ)
        m_v = ar(6144, TT, H, VD)
        m_kr = ar(8192, SEQ, p=ROPE)
        ropek = ar(8448, 2, TT, ROPE)
        ropeq = ar(8704, 2, SEQ, p=ROPE)
        m_p = ar(9216, 3, TT, SEQ)
        m_pt = ar(10752, 2, 2, SEQ)
        cq = normed[:].rearrange("p a b -> p (a b)")[:, 0:768].rearrange("p (t n) -> p t n", t=TT)
        ck = normed[:].rearrange("p a b -> p (a b)")[:, 768:1280].rearrange("p (t n) -> p t n", t=TT)
        kr3 = normed[:].rearrange("p a b -> p (a b)")[:, 1280:1664].rearrange("p (a t n) -> p a t n", a=3, t=TT)
        qr2 = normed[0:ROPE, :, :].rearrange("p a (b t) -> p a b t", b=4)[:, :, 0:2, :]
        d_q = ar(0, H, SEQ)
        d_k = ar(2048, H, SEQ)
        d_v = ar(4096, TT, D)
        d_x = ar(6144, 3, 4, SEQ)
        d_a = ar(9216, 2, TT, SEQ)
        d_at = ar(10240, 2, 2, SEQ)
        d_o = normed[:].rearrange("p t (h d) -> p t h d", h=H)
        n_q = ar(0, 4, SEQ)
        n_k = ar(1024, 4, SEQ)
        n_vs = ar(2048, TT, P)
        n_vw = ar(2304, TT, P)
        n_g = ar(2560, TT, 24)
        h_q = ar(2624, HGH, SEQ)
        h_f = ar(3648, HGH, SEQ)
        h_k = ar(4672, HGH, SEQ)
        h_v = ar(5696, TT, 512)
        h_g = ar(6720, TT, 512)
        h_a = ar(7744, 8, P)
        h_ax = ar(8768, HGH, P)
        h_e = ar(9280, 1024)
        n_x = ar(10304, 2, 800)
        c_x = normed[:].rearrange("p a b -> p (a b)")[:, 0:960].rearrange("p (v i c) -> p v i c", v=2, i=16)
        c_h = ar(7744, 2, 256, p=30)
        c_ht = ar(8256, 4, 30)
        c_k = ar(11904, 2, NB)
        c_v = ar(11936, 2, HD, p=NB)
        n_pt = normed[:]
        h_o = ar(0, TT, HGH, P)

        h_sq = ar(10304, 8, P)

        def decay_of(m):
            if m == 1:
                return h_f.rearrange("p h t -> p (h t)")
            at = 1024 - 2048 // m
            return h_e[:, at:at + 1024 // m]

        block = ctx.enter_context(nc.Block())

        @block.sync
        def _(sp):
            def load_unit(u):
                if u >= 2:
                    sp.wait_ge(S("hi_u_done"), u - 1)
                    sp.wait_ge(S("lo_u_done"), u - 1)
                k = units[u].shape[1]
                for k0, k1 in ((0, k // 2), (k // 2, k)):
                    sp.dma_start(unit_view(raw_u, u)[:, k0:k1], units[u][:, k0:k1]).then_inc(S(f"raw_u{u % 2}"), 16)

            def load_up(f, t, slot, n):
                u = t + U_OF_FFN[f]
                sp.wait_ge(S("hi_u_done"), u - 1)
                sp.wait_ge(S("lo_u_done"), u - 1)
                for s in range(2):
                    src = gu[f][:, bass.ds(t * P + s * FW[f], n)].rearrange("(k p) n -> p k n", p=P)
                    sp.dma_start(up_view(raw_u, slot, s, n), src).then_inc(S(f"raw_u{slot}"), 16)

            def load_down(f, t, slot, n):
                d = t + FT * f
                if f or not isinstance(t, int) or t >= 2:
                    sp.wait_ge(S("hi_d_done"), d - 1)
                    sp.wait_ge(S("lo_d_done"), d - 1)
                sp.dma_start(raw_d[0:n, slot, :], dn[f][bass.ds(t * P, n), :]).then_inc(S(f"raw_d{slot}"), 16)

            def ffn(f):
                for t in range(2):
                    load_up(f, t, t, P)
                    load_down(f, t, t, P)
                with sp.Fori(1, LOOPED + 1) as b:
                    for t in range(2):
                        load_up(f, b * 2 + t, t, P)
                        load_down(f, b * 2 + t, t, P)
                for t in range(2 * LOOPED + 2, FT):
                    load_up(f, t, t % 2, width(f, t))
                    load_down(f, t, t % 2, width(f, t))

            def load_gain(i):
                g = a["norm_g"]
                src = [g[0, 1], g[0, 3], g[1, 1], g[1, 3], a["final_norm_2"]][i]
                if i >= 2:
                    sp.wait_ge(S("resid_ready"), 2 * (i - 1))
                sp.dma_start(gain_row[:, i % 2, :], src.partition_broadcast(P)).then_inc(S(f"gain{i % 2}"), 16)

            sp.dma_start(resid[:], a["x"][0].rearrange("(t p) d -> p t d", p=P)).then_inc(S("x_in"), 16)
            sp.dma_start(ident[:], a["ident"]).then_inc(S("ident_in"), 16)
            rows_in = S("vrows_in")
            sp.dma_start(vrows[0:64, 0, :], a["norm_g"].rearrange("l n (k p) -> (l n k) p", p=P)).then_inc(rows_in, 16)
            at = 64
            for name, n in (("ffn1_norm_2", 8), ("mix_norm_2", 8), ("ffn2_norm_2", 8), ("mla_q_norm_g", 3),
                            ("mla_kv_norm_g", 2), ("hgrn_lower_bound_2", 4), ("diff_subln_g", 1)):
                sp.dma_start(vrows[at:at + n, 0, :],
                             a[name].rearrange("l (k p) -> (l k) p", p=P)).then_inc(rows_in, 16)
                at += n
            for i, name in enumerate(("cmp_pos_k_2", "cmp_pos_v_2")):
                sp.dma_start(vrows[16 * i:16 * i + 16, 1, :],
                             a[name][0].rearrange("(i l) d -> i (l d)", l=2)).then_inc(rows_in, 16)
            cw = a["ffn_conv_w"].rearrange("l j (k p) -> (l j k) p", p=P)
            for i in range(3):
                sp.dma_start(vrows[0:88, 2 + i, :], cw[88 * i:88 * i + 88, :]).then_inc(rows_in, 16)
            sp.dma_start(vrows[0:88, 5, :], a["ffn_conv_b"].rearrange("l (k p) -> (l k) p", p=P)).then_inc(rows_in, 16)
            for u in range(2):
                load_unit(u)
            sp.dma_start(ropek, a["ropek"].rearrange("p (a t r) -> p a t r", a=2, t=TT)).then_inc(S("rope_in"), 16)
            sp.dma_start(ropeq, a["ropeq"].rearrange("p (a t) -> p a t", a=2)).then_inc(S("rope_in"), 16)
            load_gain(0)
            for u in range(2, U_F0):
                load_unit(u)
            load_gain(1)
            ffn(0)
            sp.dma_start(dist[:], a["dist"].rearrange("p (t k) -> p t k", t=TT)).then_inc(S("tables_in"), 16)
            sp.dma_start(causal[:], a["causal"].rearrange("p (t k) -> p t k", t=3)).then_inc(S("tables_in"), 16)
            sp.dma_start(lam[:, 0:256], a["diff_lambda"].rearrange("l a d -> (l a d)").partition_broadcast(P)).then_inc(S("tables_in"), 16)
            sp.dma_start(masks[:], a["masks"].rearrange("p (t k) -> p t k", t=8)).then_inc(S("tables_in"), 16)
            sp.dma_start(cdist[:], a["cdist"].rearrange("p (t k) -> p t k", t=TT)).then_inc(S("tables_in"), 16)
            sp.dma_start(crows[:], a["crows"]).then_inc(S("tables_in"), 16)
            sp.dma_start(w2k[:], a["cmp_k_w2_2"][0].rearrange("(c p) d -> p c d", p=P)).then_inc(S("tables_in"), 16)
            sp.dma_start(w2v[:], a["cmp_v_w2_2"][0].rearrange("(c p) d -> p c d", p=P)).then_inc(S("tables_in"), 16)
            sp.dma_start(hgain[:], a["hgrn_out_norm_2"][0].partition_broadcast(P)).then_inc(S("tables_in"), 16)
            load_gain(2)
            for u in range(U_QK, U_F1):
                load_unit(u)
            load_gain(3)
            ffn(1)
            load_gain(4)
            ffn(2)
            for u in range(U_NQ, U_F3):
                load_unit(u)
            ffn(3)
            sp.wait_ge(S("final"), 2)
            sp.dma_start(out[0].rearrange("(t p) d -> p t d", p=P), normed[:]).then_inc(S("stored"), 16)
            sp.wait_ge(S("stored"), 16)

        @block.gpsimd
        def _(pool):
            pool.memset(half[:], -0.5).then_inc(S("half_set"), 1)
            pool.wait_ge(S("half_set"), 1)

            def rsqrt(r):
                n = R_N.get(r, 2)
                pool.wait_ge(S("ms"), r + 1)
                pool.tensor_tensor(st[:, r, 0:n], st[:, r, 0:n], half[:, 0:n], ALU.pow).then_inc(S("rstd"), 1)

            def hgrn():
                for l in range(1, 8):
                    m = 1 << (l - 1)
                    pool.wait_ge(S("h_level"), l + 1)
                    if l >= 2:
                        pool.wait_ge(S("h_e"), l - 1)
                        pool.wait_ge(S("h_k_upd"), l - 1)
                    e = decay_of(m).rearrange("p (n s) -> p n s", s=2)
                    left = h_k.rearrange("p h t -> p (h t)").rearrange("p (n s m) -> p n s m", s=2, m=m)[:, :, 0, :]
                    pool.tensor_tensor(left, left, e[:, :, 1:2].broadcast_to([P, 512 // m, m]), ALU.mult)\
                        .then_inc(S("h_k_upd"), 1)

            for r in range(R_HG):
                rsqrt(r)
            hgrn()
            for r in range(R_HG, R_END):
                rsqrt(r)

        @block.tensor
        def _(pe):
            def mm3(o, s_hi, s_lo, m_hi, m_lo, start, stop):
                pe.matmul(o, s_hi, m_hi, start=start, stop=False)
                pe.matmul(o, s_hi, m_lo, start=False, stop=False)
                return pe.matmul(o, s_lo, m_hi, start=False, stop=stop)

            def unit_ready(u):
                pe.wait_ge(S("hi_u_done"), u + 1)
                pe.wait_ge(S("lo_u_done"), u + 1)

            def tok(t):
                return slice(t * P, t * P + P)

            def norm_transposes(i):
                pe.wait_ge(S("normed"), 2 * i + 2)
                for b in range(4):
                    for k in range(2):
                        for t in range(TT):
                            mm = pe.transpose(psum[:, 4 + b, k * SEQ + t * P:k * SEQ + t * P + P],
                                              normed[:, t, (2 * b + k) * P:(2 * b + k + 1) * P], ident[:])
                    mm.then_inc(S("norm_tr"), 1)

            def tokens_out(o, u, k0, w0, n, first, last, i=None):
                hi, lo = unit_view(hi_u, u), unit_view(lo_u, u)
                for k in range(hi.shape[1]):
                    if i is not None:
                        pe.wait_ge(S("act_lo"), 8 * i + k0 + k + 1)
                    for t in range(TT):
                        mm = mm3(o(t), act_hi[:, k0 + k, tok(t)], act_lo[:, k0 + k, tok(t)],
                                 hi[:, k, w0:w0 + n], lo[:, k, w0:w0 + n],
                                 first and k == 0, last and k == hi.shape[1] - 1)
                return mm

            def features_out(o, u, w0, n, c0=0, i=None):
                hi, lo = unit_view(hi_u, u), unit_view(lo_u, u)
                kn = hi.shape[1]
                for k in range(kn):
                    if i is not None:
                        pe.wait_ge(S("act_lo"), 8 * i + k + 1)
                    mm = mm3(o, hi[:, k, w0:w0 + n], lo[:, k, w0:w0 + n], act_hi[:, c0 + k, :], act_lo[:, c0 + k, :],
                             k == 0, k == kn - 1)
                return mm

            def wide(u0, chunk_ready):
                for i in range(4):
                    unit_ready(u0 + i)
                    hi, lo = unit_view(hi_u, u0 + i), unit_view(lo_u, u0 + i)
                    for k in range(2):
                        chunk_ready(2 * i + k)
                        for t in range(TT):
                            for n in range(2):
                                mm = mm3(psum[:, 2 * t + n, :], act_hi[:, 2 * i + k, tok(t)],
                                         act_lo[:, 2 * i + k, tok(t)], hi[:, k, n * BANK:n * BANK + BANK],
                                         lo[:, k, n * BANK:n * BANK + BANK],
                                         i == 0 and k == 0, i == 3 and k == 1)
                    mm.then_inc(S("used_u"), 1)

            def ffn(f):
                i = [N_F0, N_F1, N_F2, N_F3][f]

                def up(t, slot, n, first=False):
                    g, u = t + FT * f, t + U_OF_FFN[f]
                    unit_ready(u)
                    if not isinstance(t, int) or t >= 2:
                        if f < 2:
                            pe.wait_ge(S("tap_b"), g * 2 - 2)
                        else:
                            pe.wait_ge(S("hid_hi_done"), g - 1)
                    for s in range(2):
                        hi, lo = up_view(hi_u, slot, s, n), up_view(lo_u, slot, s, n)
                        for k in range(KC):
                            if first and s == 0:
                                pe.wait_ge(S("act_lo"), 8 * i + max(k, 1) + 1)
                            mm = mm3(psum[0:n, 4 + 2 * slot + s, 0:SEQ], hi[:, k, :], lo[:, k, :],
                                     act_hi[:, k, :], act_lo[:, k, :], k == 0, k == KC - 1)
                        mm.then_inc(S("gate_up" if s == 0 else "used_u"), 1)

                def down(t, slot, n, last=False):
                    g = t + FT * f
                    pe.wait_ge(S("hi_d_done"), g + 1)
                    pe.wait_ge(S("lo_d_done"), g + 1)
                    pe.wait_ge(S("hid_lo_done"), g + 1)
                    for tk in range(TT):
                        for c in range(2):
                            w = slice(c * BANK, c * BANK + BANK)
                            mm = mm3(psum[:, 2 * tk + c, :], hid_hi[0:n, slot, tok(tk)], hid_lo[0:n, slot, tok(tk)],
                                     hi_d[0:n, slot, w], lo_d[0:n, slot, w], False, last)
                    mm.then_inc(S("used_d"), 1)

                up(0, 0, P, True)
                pe.wait_ge(S("zeros_set"), 1)
                for b in range(4):
                    pe.matmul(psum[:, b, :], zeros[:, 0:P], zeros[:], start=True, stop=False)
                up(1, 1, P)
                down(0, 0, P)
                with pe.Fori(0, LOOPED) as b:
                    up(b * 2 + 2, 0, P)
                    down(b * 2 + 1, 1, P)
                    up(b * 2 + 3, 1, P)
                    down(b * 2 + 2, 0, P)
                up(20, 0, P)
                down(19, 1, P)
                up(21, 1, width(f, 21))
                down(20, 0, P)
                down(21, 1, width(f, 21), True)

            def mla():
                for i in range(2):
                    unit_ready(U_DQ + i)
                    mm = tokens_out(lambda t: psum[:, t, 0:QL], U_DQ + i, 4 * i, 0, QL, i == 0, i == 1, N_MLA)
                    mm.then_inc(S("used_u"), 1)
                for i in range(2):
                    unit_ready(U_DKV + i)
                    mm = tokens_out(lambda t: psum[:, 2 + t, 0:KVL + ROPE], U_DKV + i, 4 * i, 0, KVL + ROPE,
                                    i == 0, i == 1)
                    mm.then_inc(S("used_u"), 1)
                pe.wait_ge(S("latents"), 2)
                for c in range(3):
                    for t in range(TT):
                        pe.transpose(psum[:, 4 + c // 2, (c % 2) * SEQ + t * P:(c % 2) * SEQ + t * P + P],
                                     cq[:, t, c * P:c * P + P], ident[:])
                pe.wait_ge(S("latents"), 4)
                for c in range(2):
                    for t in range(TT):
                        pe.transpose(psum[:, 6, c * SEQ + t * P:c * SEQ + t * P + P],
                                     ck[:, t, c * P:c * P + P], ident[:])
                pe.wait_ge(S("k_roped"), 1)
                for t in range(TT):
                    mm = pe.transpose(psum[0:ROPE, 7, t * P:t * P + P], kr3[:, 2, t, :], ident[:])
                mm.then_inc(S("latent_tr"), 1)
                pe.wait_ge(S("latent_lo"), 5)
                for i in range(4):
                    u = U_UQ + i
                    unit_ready(u)
                    b = 2 * (i % 2)
                    if i >= 2:
                        pe.wait_ge(S("m_q_out"), i - 1)
                        pe.wait_ge(S("m_qr_read"), i - 1)
                    for h in range(2):
                        mm = features_out(psum[:, b, h * SEQ:h * SEQ + SEQ], u, h * 192, NOPE)
                    mm.then_inc(S("m_q_up"), 1)
                    for h in range(2):
                        mm = features_out(psum[0:ROPE, b + 1, h * SEQ:h * SEQ + SEQ], u, h * 192 + NOPE, ROPE)
                    mm.then_inc(S("used_u"), 1)
                for i in range(2):
                    u = U_UKV + i
                    unit_ready(u)
                    hi, lo = unit_view(hi_u, u), unit_view(lo_u, u)
                    if i:
                        pe.wait_ge(S("m_k_out"), 1)
                        pe.wait_ge(S("m_v_out"), 1)
                    for h in range(4):
                        mm = features_out(psum[:, 4 + h // 2, (h % 2) * SEQ:(h % 2) * SEQ + SEQ], u, h * 256, NOPE, 3)
                    mm.then_inc(S("m_k_up"), 1)
                    for t in range(TT):
                        for k in range(2):
                            v_hi, v_lo = (x[:, k, :].rearrange("p (h n) -> p h n", h=4)[:, :, NOPE:] for x in (hi, lo))
                            mm = mm3(psum[:, 6 + t, :], act_hi[:, 3 + k, tok(t)], act_lo[:, 3 + k, tok(t)],
                                     v_hi, v_lo, k == 0, k == 1)
                    mm.then_inc(S("used_u"), 1)

                def scores(h):
                    if h >= 3:
                        pe.wait_ge(S("m_exp"), 2 * (h - 2))
                    for t in range(TT):
                        o = psum[:, h % 3, t * SEQ:t * SEQ + SEQ]
                        pe.matmul(o, m_q[:, h, tok(t)], m_k[:, h, :], start=True, stop=False)
                        mm = pe.matmul(o, m_qr[:, h, tok(t)], m_kr, start=False, stop=True)
                    mm.then_inc(S("m_scores"), 1)

                def turn(h):
                    pe.wait_ge(S("m_probs"), 2 * h + 2)
                    if h >= 2:
                        pe.wait_ge(S("m_pt"), h - 1)
                    for k in range(2):
                        for t in range(TT):
                            mm = pe.transpose(psum[:, 3 + h % 2, k * SEQ + t * P:k * SEQ + t * P + P],
                                              m_p[:, h % 3, t, k * P:k * P + P], ident[:])
                    mm.then_inc(S("m_turned"), 1)

                def values(h):
                    pe.wait_ge(S("m_pt"), h + 1)
                    if h >= 2:
                        pe.wait_ge(S("m_o_lo"), h - 1)
                    for k in range(2):
                        mm = pe.matmul(psum[:, 5 + h % 2, 0:SEQ], m_v[:, k, h, :], m_pt[:, h % 2, k, :],
                                       start=k == 0, stop=k == 1)
                    mm.then_inc(S("m_values"), 1)

                pe.wait_ge(S("m_q_out"), 4)
                pe.wait_ge(S("m_qr_out"), 4)
                pe.wait_ge(S("m_k_out"), 2)
                pe.wait_ge(S("m_v_out"), 2)
                for i in range(H + 3):
                    if i < H:
                        scores(i)
                    if 0 <= i - 2 < H:
                        turn(i - 2)
                    if i >= 3:
                        values(i - 3)
                wide(U_MO, lambda c: pe.wait_ge(S("m_o_lo"), c + 1))

            def diff():
                for i in range(8):
                    u = U_QK + i
                    unit_ready(u)
                    if i >= 4:
                        pe.wait_ge(S("d_qk_out"), i - 3)
                    for h in range(2):
                        mm = features_out(psum[:, i % 4, h * SEQ:h * SEQ + SEQ], u, h * P, P,
                                          i=N_DIFF if i == 0 and h == 0 else None)
                    mm.then_inc(S("used_u"), 1)
                for i in range(4):
                    u = U_V + i
                    unit_ready(u)
                    for n in range(2):
                        mm = tokens_out(lambda t: psum[:, 4 + 2 * t + n, :], u, 2 * i, n * BANK, BANK, i == 0, i == 3)
                    mm.then_inc(S("used_u"), 1)

                def scores(h):
                    if h >= 2:
                        pe.wait_ge(S("d_biased"), 2 * (h - 1))
                    for j in range(2):
                        r = slice(j * HD, j * HD + HD)
                        for t in range(TT):
                            mm = pe.matmul(psum[:, 2 * (h % 2) + j, t * SEQ:t * SEQ + SEQ], d_q[r, h, tok(t)],
                                           d_k[r, h, :], start=True, stop=True)
                        mm.then_inc(S("d_scores"), 1)

                def turn(h):
                    pe.wait_ge(S("d_maps"), 2 * h + 2)
                    if h >= 2:
                        pe.wait_ge(S("d_at"), h - 1)
                    for k in range(2):
                        for t in range(TT):
                            mm = pe.transpose(psum[:, 4 + h % 2, k * SEQ + t * P:k * SEQ + t * P + P],
                                              d_a[:, h % 2, t, k * P:k * P + P], ident[:])
                    mm.then_inc(S("d_turned"), 1)

                def values(h):
                    pe.wait_ge(S("d_at"), h + 1)
                    if h >= 2:
                        pe.wait_ge(S("d_o_out"), h - 1)
                    for t in range(TT):
                        for k in range(2):
                            mm = pe.matmul(psum[:, 6 + h % 2, t * P:t * P + P], d_at[:, h % 2, k, tok(t)],
                                           d_v[:, k, h * P:h * P + P], start=k == 0, stop=k == 1)
                    mm.then_inc(S("d_values"), 1)

                pe.wait_ge(S("d_qk_out"), 8)
                pe.wait_ge(S("d_v_out"), 2)
                for i in range(H + 3):
                    if i < H:
                        scores(i)
                    if 0 <= i - 2 < H:
                        turn(i - 2)
                    if i >= 3:
                        values(i - 3)
                pe.wait_ge(S("d_normed"), 2)
                for b in range(4):
                    for k in range(2):
                        for t in range(TT):
                            mm = pe.transpose(psum[:, 4 + b, k * SEQ + t * P:k * SEQ + t * P + P],
                                              d_o[:, t, 2 * b + k, :], ident[:])
                    mm.then_inc(S("d_tr"), 1)
                wide(U_DO, lambda c: pe.wait_ge(S("d_lo"), c // 2 + 1))

            def mix():
                for i in range(2):
                    unit_ready(U_NQ + i)
                    for h in range(2):
                        mm = features_out(psum[:, i, h * SEQ:h * SEQ + SEQ], U_NQ + i, h * P, P,
                                          i=N_MIX if i == 0 and h == 0 else None)
                    mm.then_inc(S("used_u"), 1)
                unit_ready(U_NC)
                for v in range(2):
                    mm = features_out(psum[:, 2, v * SEQ:v * SEQ + SEQ], U_NC, v * P, P)
                mm.then_inc(S("used_u"), 1)
                for i, u in enumerate((U_NS, U_NW)):
                    unit_ready(u)
                    features_out(psum[:, 3 + 2 * i, 0:SEQ], u, 0, P)
                    for t in range(TT):
                        hi, lo = unit_view(hi_u, u), unit_view(lo_u, u)
                        for k in range(KC):
                            mm = mm3(psum[:, 4 + 2 * i, t * P:t * P + P], act_hi[:, k, tok(t)], act_lo[:, k, tok(t)],
                                     hi[:, k, P:2 * P], lo[:, k, P:2 * P], k == 0, k == KC - 1)
                    mm.then_inc(S("used_u"), 1)
                unit_ready(U_NG)
                hi, lo = unit_view(hi_u, U_NG), unit_view(lo_u, U_NG)
                for t in range(TT):
                    for k in range(KC):
                        mm = mm3(psum[:, 7, t * 24:t * 24 + 24], act_hi[:, k, tok(t)], act_lo[:, k, tok(t)],
                                 hi[:, k, :], lo[:, k, :], k == 0, k == KC - 1)
                mm.then_inc(S("used_u"), 1)
                pe.wait_ge(S("n_q_out"), 2)
                for i in range(2):
                    unit_ready(U_HQ + i)
                    for h in range(2):
                        mm = features_out(psum[:, i, h * SEQ:h * SEQ + SEQ], U_HQ + i, h * P, P)
                    mm.then_inc(S("used_u"), 1)
                pe.wait_ge(S("c_x_done"), 16)
                pe.wait_ge(S("n_k_out"), 8)
                for i in range(2):
                    unit_ready(U_HF + i)
                    for h in range(2):
                        mm = features_out(psum[:, 2 + i, h * SEQ:h * SEQ + SEQ], U_HF + i, h * P, P)
                    mm.then_inc(S("used_u"), 1)
                pe.wait_ge(S("n_v_out"), 2)
                pe.wait_ge(S("n_gates"), 1)
                for i in range(4):
                    u = U_HI + i
                    unit_ready(u)
                    for n in range(2):
                        mm = tokens_out(lambda t: psum[:, 4 + 2 * t + n, :], u, 2 * i, n * BANK, BANK, i == 0, i == 3)
                    mm.then_inc(S("used_u"), 1)
                pe.wait_ge(S("h_q_out"), 2)
                for v in range(2):
                    x_hi, x_lo = (x[:, 2 * v:2 * v + 2, :].rearrange("p a b -> p (a b)")[:, 0:480]
                                  .rearrange("p (i c) -> p i c", i=16) for x in (act_hi, act_lo))
                    pe.wait_ge(S("c_lo"), v + 1)
                    for i in range(2):
                        u = (U_CK, U_CV)[v] + i
                        unit_ready(u)
                        hi, lo = unit_view(hi_u, u), unit_view(lo_u, u)
                        for k in range(8):
                            mm = mm3(psum[0:30, v, 0:256], x_hi[:, 8 * i + k, :], x_lo[:, 8 * i + k, :],
                                     hi[:, k, :], lo[:, k, :], i == 0 and k == 0, i == 1 and k == 7)
                        mm.then_inc(S("used_u"), 1)
                pe.wait_ge(S("h_fk_out"), 4)
                pe.wait_ge(S("c_h_out"), 2)
                for v in range(2):
                    for c in range(2):
                        mm = pe.transpose(psum[:, 2, (2 * v + c) * 30:(2 * v + c) * 30 + 30],
                                          c_h[:, v, c * P:c * P + P], ident[0:30, 0:30])
                mm.then_inc(S("c_h_tr"), 1)
                pe.wait_ge(S("c_ht_out"), 1)
                for e in range(2):
                    for g in range(2):
                        for c in range(2):
                            mm = pe.matmul(psum[e * HD:e * HD + HD, 3, g * NB:g * NB + NB], w2k[:, c, :],
                                           c_ht[:, c, g * NB:g * NB + NB], start=c == 0, stop=c == 1)
                for g in range(2):
                    for c in range(2):
                        mm = pe.matmul(psum[0:NB, 0, g * HD:g * HD + HD], c_ht[:, 2 + c, g * NB:g * NB + NB],
                                       w2v[:, c, :], start=c == 0, stop=c == 1)
                mm.then_inc(S("c_kv"), 1)

                def scores(h):
                    b, r, j, g = 2 * (h % 2), slice((h % 2) * HD, (h % 2) * HD + HD), h // 2, h // 4
                    if h >= 2:
                        pe.wait_ge(S("n_biased"), 3 * (h - 1))
                    for br in range(2):
                        k = n_k[r, 2 * br + g, :]
                        pe.matmul(psum[:, b + br, 0:P], n_q[r, j, tok(0)], k[:, 0:P], start=True, stop=True)
                        mm = pe.matmul(psum[:, b + br, P:3 * P], n_q[r, j, tok(1)], k, start=True, stop=True)
                        if br == 0:
                            for t in range(TT):
                                pe.matmul(psum[:, b, 3 * P + t * NB:3 * P + t * NB + NB], n_q[r, j, tok(t)],
                                          c_k[r, g, :], start=True, stop=True)
                    mm.then_inc(S("n_scores"), 1)

                def turn(h):
                    pe.wait_ge(S("n_probs"), 6 * h + 6)
                    if h >= 1:
                        pe.wait_ge(S("n_pt_a"), 2 * h)
                        pe.wait_ge(S("n_pt_b"), 2 * h)
                    x = n_x[:, h % 2, :]
                    for br in range(2):
                        for c in range(3):
                            pe.transpose(psum[:, 4 + br, c * P:c * P + P], x[:, (3 * br + c) * P:(3 * br + c + 1) * P],
                                         ident[:])
                        mm = pe.transpose(psum[0:NB, 4 + br, 3 * P:4 * P], x[:, 768 + br * NB:768 + br * NB + NB], ident[:])
                    mm.then_inc(S("n_turned"), 1)

                def values(h):
                    r, j, g = slice((h % 2) * HD, (h % 2) * HD + HD), h // 2, h // 4
                    pe.wait_ge(S("n_pt_a"), 2 * h + 2)
                    pe.wait_ge(S("n_pt_b"), 2 * h + 2)
                    if j >= 2:
                        pe.wait_ge(S("n_o_lo"), j - 1)
                    o, pt, gs = psum[r, 6 + j % 2, 0:SEQ], n_pt[:, h % 2, :], slice(g * HD, g * HD + HD)
                    pe.matmul(o, c_v[:, g, :], pt[0:NB, 768:1024], start=True, stop=False)
                    pe.matmul(o, n_vs[:, 0, gs], pt[:, 0:256], start=False, stop=False)
                    pe.matmul(o, n_vw[:, 0, gs], pt[:, 384:640], start=False, stop=False)
                    pe.matmul(o[:, P:], n_vs[:, 1, gs], pt[:, 256:384], start=False, stop=False)
                    pe.matmul(o[:, P:], n_vw[:, 1, gs], pt[:, 640:768], start=False, stop=True)\
                        .then_inc(S("n_values"), 1)

                pe.wait_ge(S("c_kv_out"), 2)
                pe.wait_ge(S("h_v_out"), 2)
                pe.wait_ge(S("h_g_out"), 2)
                for i in range(H + 2):
                    if i < H:
                        scores(i)
                    if i >= 2:
                        values(i - 2)
                    if 1 <= i <= H:
                        turn(i - 1)

                pe.wait_ge(S("h_ready"), 1)
                for l in range(8):
                    b = 2 * (l % 2)
                    if l >= 1:
                        pe.wait_ge(S("h_q_upd"), l)
                    if l >= 2:
                        pe.wait_ge(S("h_k_upd"), l - 1)
                        pe.wait_ge(S("h_a_done"), l - 1)
                    for x in range(8):
                        t, h = x // 4, x % 4
                        mm = pe.matmul(psum[:, b + t, h * P:h * P + P], h_k[:, h, tok(t)], h_q[:, h, tok(t)],
                                       start=True, stop=True)
                    mm.then_inc(S("h_level"), 1)
                pe.wait_ge(S("h_q_upd"), 8)
                pe.wait_ge(S("h_k_upd"), 7)
                for h in range(HGH):
                    mm = pe.matmul(psum[:, 4, h * P:h * P + P], h_k[:, h, tok(0)], h_q[:, h, tok(1)],
                                   start=True, stop=True)
                mm.then_inc(S("h_level"), 1)
                pe.wait_ge(S("n_o_lo"), 4)
                pe.wait_ge(S("h_a_done"), 8)
                pe.wait_ge(S("h_ax_out"), 1)
                for h in range(HGH):
                    v = [h_v[:, t, h * P:h * P + P] for t in range(TT)]
                    pe.matmul(psum[:, 6, h * P:h * P + P], h_a[:, h, :], v[0], start=True, stop=True)
                    pe.matmul(psum[:, 7, h * P:h * P + P], h_ax[:, h, :], v[0], start=True, stop=False)
                    mm = pe.matmul(psum[:, 7, h * P:h * P + P], h_a[:, 4 + h, :], v[1], start=False, stop=True)
                mm.then_inc(S("h_out"), 1)
                pe.wait_ge(S("h_gated"), 2)
                for h in range(HGH):
                    for t in range(TT):
                        mm = pe.transpose(psum[:, 4 + h // 2, (h % 2) * SEQ + t * P:(h % 2) * SEQ + t * P + P],
                                          h_o[:, t, h, :], ident[:])
                    if h % 2:
                        mm.then_inc(S("h_tr"), 1)
                wide(U_WO, lambda c: pe.wait_ge(S("n_o_lo"), c + 1) if c < 4 else pe.wait_ge(S("h_lo"), (c - 2) // 2))

            pe.wait_ge(S("ident_in"), 16)
            pe.wait_ge(S("vrows_in"), 16 * 14)
            for i, (at, n) in enumerate(VROWS):
                mm = pe.transpose(psum[:, 3, at:at + n], vrows[0:n, i, :], ident[0:n, 0:n])
            mm.then_inc(S("vecs_tr"), 1)
            norm_transposes(N_MLA)
            mla()
            norm_transposes(N_F0)
            ffn(0)
            norm_transposes(N_DIFF)
            diff()
            norm_transposes(N_F1)
            ffn(1)
            norm_transposes(N_F2)
            ffn(2)
            norm_transposes(N_MIX)
            mix()
            norm_transposes(N_F3)
            ffn(3)

        @block.scalar
        def _(act):
            def split_u(u):
                if isinstance(u, int):
                    if u >= U_END:
                        return
                    act.wait_ge(S(f"raw_u{u % 2}"), 32 * (u // 2 + 1))
                    if u >= 2:
                        act.wait_ge(S("used_u"), u - 1)
                    act.activation(unit_view(hi_u, u), unit_view(raw_u, u), ACT.Copy).then_inc(S("hi_u_done"), 1)

            def split_u_looped(b, u0):
                act.wait_ge(S(f"raw_u{u0 % 2}"), b * 32 + 32 * (u0 // 2 + 1))
                act.wait_ge(S("used_u"), b * 2 + (u0 - 1))
                act.activation(u_slot(hi_u, u0), u_slot(raw_u, u0), ACT.Copy).then_inc(S("hi_u_done"), 1)

            def split_d(d, b=None):
                act.wait_ge(S(f"raw_d{d % 2}"), 16 * (d // 2 + 1) if b is None else b * 16 + 16 * (d // 2 + 1))
                if b is not None:
                    act.wait_ge(S("used_d"), b * 2 + (d - 1))
                elif d >= 2:
                    act.wait_ge(S("used_d"), d - 1)
                act.activation(hi_d[:, d % 2, :], raw_d[:, d % 2, :], ACT.Copy).then_inc(S("hi_d_done"), 1)

            def square_sums(r, ready):
                for t in range(TT):
                    ready(t)
                    if t == 0 and r == R_MLA:
                        pass
                    act.activation(junk[:], resid[:, t, :], ACT.Square, accum_out=st[:, r, t:t + 1])\
                        .then_inc(S("row_sums"), 1)
                    act.wait_ge(S("row_sums"), 2 * R_OF_NORM.index(r) + t + 1)

            def norm(i):
                if i == N_MLA:
                    square_sums(R_MLA, lambda t: act.wait_ge(S("x_in"), 16))
                else:
                    square_sums(R_OF_NORM[i], lambda t: act.wait_ge(S("resid_ready"), 2 * (i - 1) + t + 1))
                if i == N_MLA:
                    act.wait_ge(S("vecs_tr"), 1)
                    act.activation(vecs[:], psum[:, 3, 0:V_ALL], ACT.Copy).then_inc(S("vecs_ready"), 1)
                    act.wait_ge(S("vecs_ready"), 1)
                if i == N_FINAL:
                    return
                for k in range(KC):
                    act.wait_ge(S("norm_tr"), 4 * i + k // 2 + 1)
                    act.activation(act_hi[:, k, :], psum[:, 4 + k // 2, (k % 2) * SEQ:(k % 2) * SEQ + SEQ], ACT.Copy,
                                   scale=vecs[:, V_OF_NORM[i] + k:V_OF_NORM[i] + k + 1]).then_inc(S("act_hi"), 1)

            def post_sums(j, name, n):
                act.wait_ge(S(name), n)
                for t in range(TT):
                    act.activation(junk[:].rearrange("p (a b) -> p a b", a=2), psum[:, 2 * t:2 * t + 2, :], ACT.Square,
                                   accum_out=st[:, R_OF_POST[j], t:t + 1]).then_inc(S("post_sums"), 1)
                    act.wait_ge(S("post_sums"), 2 * j + t + 1)

            def ffn(f):
                def tile(t, slot, n, b=None):
                    at = (lambda x: x) if b is None else (lambda x: b * 2 + x)
                    g, u = FT * f + t, U_OF_FFN[f] + t
                    looped_or_late = b is not None or g >= 2
                    act.wait_ge(S("gate_up"), at(g + 1))
                    if f < 2:
                        if looped_or_late:
                            act.wait_ge(S("hid_lo_done"), at(g - 1))
                        for s, buf in ((0, cg), (1, cv)):
                            if s:
                                act.wait_ge(S("used_u"), at(u + 1))
                            w = at(V_CW + (f * 3 + 1) * 44 + s * FT + t)
                            c = at(V_CB + f * 44 + s * FT + t)
                            act.activation(buf[0:n, slot, :], psum[0:n, 4 + 2 * slot + s, 0:SEQ], ACT.Identity,
                                           scale=vecs[0:n, bass.ds(w, 1)], bias=vecs[0:n, bass.ds(c, 1)])\
                                .then_inc(S("conv_mid"), 1)
                    else:
                        act.wait_ge(S("hid_hi_done"), at(g - 1))
                        act.activation(gg[0:n, slot, :], psum[0:n, 4 + 2 * slot, 0:SEQ], ACT.Silu)\
                            .then_inc(S("gated"), 1)
                    if b is None:
                        split_u(u + 2)
                    else:
                        split_u_looped(b, u + 2)
                    if f < 2:
                        act.wait_ge(S("tap_b"), b * 4 + 2 * g + 1 if b is not None else 2 * g + 1)
                        act.activation(gg[0:n, slot, :], cg[0:n, slot, :], ACT.Gelu_apprx_tanh).then_inc(S("gated"), 1)
                    if b is not None or t + 1 < FT:
                        split_d(g + 1, b)

                split_d(FT * f)
                tile(0, 0, P)
                tile(1, 1, P)
                with act.Fori(0, LOOPED) as b:
                    tile(2, 0, P, b)
                    tile(3, 1, P, b)
                tile(20, 0, P)
                tile(21, 1, width(f, 21))

            def mla():
                for u in range(2, 4):
                    split_u(u)
                ch = Chain(act, S("act_chain_mla"))
                act.wait_ge(S("used_u"), U_DQ + 2)
                for t in range(TT):
                    ch.link(act.activation(junk[:, 0:QL], psum[:, t, 0:QL], ACT.Square, accum_out=st[:, R_CQ, t:t + 1]))
                act.wait_ge(S("used_u"), U_DKV + 2)
                for t in range(TT):
                    ins = act.activation(junk[:, 0:KVL], psum[:, 2 + t, 0:KVL], ACT.Square,
                                         accum_out=st[:, R_CQ, 2 + t:3 + t])
                    if t == 0:
                        ch.link(ins)
                ins.then_inc(S("latent_sums"), 1)
                for u in range(4, 6):
                    split_u(u)
                act.wait_ge(S("latent_tr"), 1)
                for c in range(5):
                    b, o = (4 + c // 2, c % 2) if c < 3 else (6, c - 3)
                    v = V_QN + c if c < 3 else V_KVN + c - 3
                    act.activation(act_hi[:, c, :], psum[:, b, o * SEQ:o * SEQ + SEQ], ACT.Copy,
                                   scale=vecs[:, v:v + 1]).then_inc(S("latent_hi"), 1)
                act.activation(m_kr, psum[0:ROPE, 7, 0:SEQ], ACT.Copy).then_inc(S("m_kr_out"), 1)
                for i in range(4):
                    act.wait_ge(S("m_q_up"), i + 1)
                    act.activation(m_q[:, 2 * i:2 * i + 2, :], psum[:, 2 * (i % 2), :].rearrange("p (h t) -> p h t", h=2),
                                   ACT.Copy).then_inc(S("m_q_out"), 1)
                    split_u(U_UQ + i + 2)
                for i in range(2):
                    act.wait_ge(S("m_k_up"), i + 1)
                    act.activation(m_k[:, 4 * i:4 * i + 4, :],
                                   psum[:, 4:6, :].rearrange("p b (h t) -> p (b h) t", h=2), ACT.Copy)\
                        .then_inc(S("m_k_out"), 1)
                    split_u(U_UKV + i + 2)
                for i in range(H + 3):
                    if i < H:
                        act.wait_ge(S("m_bias"), i + 1)
                        if i >= 3:
                            act.wait_ge(S("m_turned"), i - 2)
                        for t in range(TT):
                            act.activation(m_p[:, i % 3, t, :], psum[:, i % 3, t * SEQ:t * SEQ + SEQ], ACT.Exp,
                                           scale=M_SCALE, bias=soft[:, i, 1, t:t + 1],
                                           accum_out=soft[:, i, 2, t:t + 1]).then_inc(S("m_exp"), 1)
                    if 0 <= i - 2 < H:
                        h = i - 2
                        act.wait_ge(S("m_turned"), h + 1)
                        if h >= 2:
                            act.wait_ge(S("m_values"), h - 1)
                        act.activation(m_pt[:, h % 2], psum[:, 3 + h % 2, :].rearrange("p (k t) -> p k t", k=2),
                                       ACT.Copy).then_inc(S("m_pt"), 1)
                    if i >= 3:
                        h = i - 3
                        act.wait_ge(S("m_values"), h + 1)
                        act.activation(act_hi[:, h, :], psum[:, 5 + h % 2, 0:SEQ], ACT.Copy).then_inc(S("m_o_hi"), 1)
                for i in range(4):
                    split_u(U_MO + i + 2)

            def diff():
                for i in range(8):
                    act.wait_ge(S("used_u"), U_QK + i + 1)
                    act.activation((d_q if i < 4 else d_k)[:, 2 * (i % 4):2 * (i % 4) + 2, :],
                                   psum[:, i % 4, :].rearrange("p (h t) -> p h t", h=2), ACT.Copy)\
                        .then_inc(S("d_qk_out"), 1)
                    split_u(U_QK + i + 2)
                ch = Chain(act, S("act_chain_diff"))
                act.wait_ge(S("lam_sums"), 1)
                act.activation(lam[:, 258:260], lam[:, 256:258], ACT.Exp).then_inc(S("lam_exp"), 1)
                for i in range(4):
                    split_u(U_V + i + 2)
                for t in range(TT):
                    act.wait_ge(S("used_u"), U_V + 4)
                    act.activation(d_v[:, t, :].rearrange("p (a b) -> p a b", a=2), psum[:, 4 + 2 * t:6 + 2 * t, :],
                                   ACT.Copy).then_inc(S("d_v_out"), 1)
                for i in range(H + 3):
                    if i < H:
                        act.wait_ge(S("d_bias"), i + 1)
                        for m in range(4):
                            act.activation(d_x[:, i % 3, m, :], d_x[:, i % 3, m, :], ACT.Exp, scale=D_SCALE,
                                           bias=soft[:, i, 1, m:m + 1],
                                           accum_out=soft[:, i, 2, m:m + 1]).then_inc(S("d_exp"), 1)
                    if 0 <= i - 2 < H:
                        h = i - 2
                        act.wait_ge(S("d_turned"), h + 1)
                        if h >= 2:
                            act.wait_ge(S("d_values"), h - 1)
                        act.activation(d_at[:, h % 2], psum[:, 4 + h % 2, :].rearrange("p (k t) -> p k t", k=2),
                                       ACT.Copy).then_inc(S("d_at"), 1)
                    if i >= 3:
                        h = i - 3
                        act.wait_ge(S("d_values"), h + 1)
                        act.activation(d_o[:, :, h, :], psum[:, 6 + h % 2, 0:2 * P].rearrange("p (t d) -> p t d", t=2),
                                       ACT.Copy).then_inc(S("d_o_out"), 1)
                act.wait_ge(S("d_gain"), 1)
                for b in range(4):
                    act.wait_ge(S("d_tr"), b + 1)
                    act.activation(act_hi[:, 2 * b:2 * b + 2, :], psum[:, 4 + b, :].rearrange("p (k t) -> p k t", k=2),
                                   ACT.Copy, scale=lam[:, 261:262]).then_inc(S("d_hi"), 1)
                for i in range(4):
                    split_u(U_DO + i + 2)

            def mix():
                both = lambda v: v.rearrange("p (h t) -> p h t", h=2)
                flat = lambda v: v.rearrange("p a b -> p (a b)")
                for i in range(2):
                    act.wait_ge(S("used_u"), U_NQ + i + 1)
                    act.activation(n_q[:, 2 * i:2 * i + 2, :], both(psum[:, i, :]), ACT.Copy).then_inc(S("n_q_out"), 1)
                    split_u(U_NQ + i + 2)
                split_u(U_NC + 2)
                for i, u in enumerate((U_NS, U_NW)):
                    act.wait_ge(S("used_u"), u + 1)
                    for g in range(2):
                        for e in range(2):
                            act.activation(n_k[e * HD:e * HD + HD, 2 * i + g, :],
                                           psum[g * HD:g * HD + HD, 3 + 2 * i, 0:SEQ], ACT.Copy)\
                                .then_inc(S("n_k_out"), 1)
                    split_u(u + 2)
                act.wait_ge(S("used_u"), U_NG + 1)
                act.activation(n_g, psum[:, 7, 0:48].rearrange("p (t n) -> p t n", t=TT), ACT.Sigmoid)\
                    .then_inc(S("n_gates"), 1)
                split_u(U_NG + 2)
                for i in range(2):
                    act.wait_ge(S("used_u"), U_HQ + i + 1)
                    act.activation(h_q[:, 2 * i:2 * i + 2, :], both(psum[:, i, :]), ACT.Silu).then_inc(S("h_q_out"), 1)
                    split_u(U_HQ + i + 2)
                for i in range(2):
                    act.wait_ge(S("used_u"), U_HF + i + 1)
                    for sign, dst in ((1.0, h_f), (-1.0, h_k)):
                        act.activation(dst[:, 2 * i:2 * i + 2, :], both(psum[:, 2 + i, :]), ACT.Sigmoid, scale=sign)\
                            .then_inc(S("h_fk_out"), 1)
                    split_u(U_HF + i + 2)
                for i in range(3):
                    split_u(U_HI + i + 2)
                for v in range(2):
                    act.wait_ge(S("used_u"), U_HI + 4)
                    if v == 0:
                        act.wait_ge(S("c_x_done"), 16)
                    act.activation(flat(act_hi[:, 2 * v:2 * v + 2, :])[:, 0:480], c_x[:, v].rearrange("p i c -> p (i c)"),
                                   ACT.Copy).then_inc(S("c_hi"), 1)
                for t in range(TT):
                    act.activation(h_g[:, t, :], psum[:, 5 + 2 * t, :], ACT.Silu).then_inc(S("h_g_out"), 1)
                split_u(U_HI + 5)
                for v in range(2):
                    u = (U_CK, U_CV)[v]
                    split_u(u + 2)
                    act.wait_ge(S("used_u"), u + 2)
                    act.activation(c_h[:, v, :], psum[0:30, v, 0:256], ACT.Gelu_apprx_tanh).then_inc(S("c_h_out"), 1)
                    split_u(u + 3)
                act.wait_ge(S("c_h_tr"), 1)
                act.activation(c_ht, psum[:, 2, 0:120].rearrange("p (a b) -> p a b", a=4), ACT.Copy)\
                    .then_inc(S("c_ht_out"), 1)
                act.wait_ge(S("c_kv"), 1)
                act.activation(c_k, psum[:, 3, 0:30].rearrange("p (a b) -> p a b", a=2), ACT.Copy)\
                    .then_inc(S("c_kv_out"), 1)
                act.activation(c_v, psum[0:NB, 0, 0:P].rearrange("p (a b) -> p a b", a=2), ACT.Copy)\
                    .then_inc(S("c_kv_out"), 1)
                act.wait_ge(S("lb_shifted"), 1)
                act.activation(bound[:, 1, :], bound[:, 0, :], ACT.Exp).then_inc(S("lb_exp"), 1)
                for i in range(H + 2):
                    if i < H:
                        act.wait_ge(S("n_bias"), i + 1)
                        x = n_x[:, i % 2, :]
                        for m, (at, n) in enumerate(N_PARTS):
                            act.activation(x[:, at:at + n], x[:, at:at + n], ACT.Exp, scale=D_SCALE,
                                           bias=soft[:, i, 1, m:m + 1], accum_out=soft[:, i, 2, m:m + 1])\
                                .then_inc(S("n_exp"), 1)
                    if 1 <= i <= H:
                        h = i - 1
                        act.wait_ge(S("n_turned"), h + 1)
                        if h >= 2:
                            act.wait_ge(S("n_values"), h - 1)
                        act.activation(n_pt[:, h % 2, 0:384], psum[:, 4, 0:384], ACT.Copy).then_inc(S("n_pt_a"), 1)
                        act.activation(n_pt[0:NB, h % 2, 768:896], psum[0:NB, 4, 384:512], ACT.Copy)\
                            .then_inc(S("n_pt_a"), 1)
                    if i >= 2 and i % 2:
                        j = (i - 2) // 2
                        act.wait_ge(S("n_values"), 2 * j + 2)
                        act.activation(act_hi[:, j, :], psum[:, 6 + j % 2, 0:SEQ], ACT.Copy).then_inc(S("n_o_hi"), 1)
                act.wait_ge(S("h_level"), 9)
                act.activation(h_ax, psum[:, 4, :].rearrange("p (h t) -> p h t", h=HGH), ACT.Copy)\
                    .then_inc(S("h_ax_out"), 1)
                act.wait_ge(S("h_out"), 1)
                act.activation(h_sq, psum[:, 6:8, :].rearrange("p t (h d) -> p (t h) d", h=HGH), ACT.Square)\
                    .then_inc(S("h_squares"), 1)
                for b in range(2):
                    act.wait_ge(S("h_tr"), b + 1)
                    act.activation(act_hi[:, 4 + 2 * b:6 + 2 * b, :], both(psum[:, 4 + b, :]), ACT.Copy)\
                        .then_inc(S("h_hi"), 1)
                for i in range(4):
                    split_u(U_WO + i + 2)

            for u in range(2):
                split_u(u)
            norm(N_MLA)
            mla()
            post_sums(0, "used_u", U_MO + 4)
            norm(N_F0)
            ffn(0)
            post_sums(1, "used_d", FT)
            norm(N_DIFF)
            diff()
            post_sums(2, "used_u", U_DO + 4)
            norm(N_F1)
            ffn(1)
            post_sums(3, "used_d", 2 * FT)
            norm(N_F2)
            ffn(2)
            norm(N_MIX)
            mix()
            norm(N_F3)
            ffn(3)
            norm(N_FINAL)

        @block.vector
        def _(dve):
            def split_u(u, b=None):
                if b is not None:
                    dve.wait_ge(S("hi_u_done"), b * 2 + (u + 1))
                    v = [u_slot(x, u) for x in (lo_u, raw_u, hi_u)]
                else:
                    if u >= U_END:
                        return
                    dve.wait_ge(S("hi_u_done"), u + 1)
                    v = [unit_view(x, u) for x in (lo_u, raw_u, hi_u)]
                dve.tensor_tensor(v[0], v[1], v[2].bitcast(F32), ALU.subtract).then_inc(S("lo_u_done"), 1)

            def split_d(d, b=None):
                dve.wait_ge(S("hi_d_done"), d + 1 if b is None else b * 2 + (d + 1))
                dve.tensor_tensor(lo_d[:, d % 2, :], raw_d[:, d % 2, :], hi_d[:, d % 2, :].bitcast(F32),
                                  ALU.subtract).then_inc(S("lo_d_done"), 1)

            def mean_squares(r, n, over):
                dve.tensor_scalar(st[:, r, 0:n], st[:, r, 0:n], 1.0 / over, EPS, ALU.mult, ALU.add)\
                    .then_inc(S("ms"), 1)

            def norm(i):
                r = R_OF_NORM[i]
                dve.wait_ge(S("row_sums"), 2 * i + 2)
                mean_squares(r, 2, D)
                dve.wait_ge(S("rstd"), r + 1)
                for t in range(TT):
                    dve.tensor_scalar(normed[:, t, :], resid[:, t, :], st[:, r, t:t + 1], None, ALU.mult)\
                        .then_inc(S("normed"), 1)
                if i == N_FINAL:
                    dve.wait_ge(S("gain0"), 16 * 3)
                    for t in range(TT):
                        dve.wait_ge(S("normed"), 2 * i + t + 1)
                        dve.tensor_tensor(normed[:, t, :], normed[:, t, :], gain_row[:, 0, :], ALU.mult)\
                            .then_inc(S("final"), 1)
                    return
                for b in range(4):
                    dve.wait_ge(S("act_hi"), 8 * i + 2 * b + 2)
                    for k in (2 * b, 2 * b + 1):
                        v = V_OF_NORM[i] + k
                        dve.scalar_tensor_tensor(act_lo[:, k, :], psum[:, 4 + b, (k % 2) * SEQ:(k % 2) * SEQ + SEQ],
                                                 vecs[:, v:v + 1], act_hi[:, k, :].bitcast(F32), ALU.mult,
                                                 ALU.subtract).then_inc(S("act_lo"), 1)

            def post(j):
                r = R_OF_POST[j]
                dve.wait_ge(S("post_sums"), 2 * j + 2)
                mean_squares(r, 2, D)
                dve.wait_ge(S("rstd"), r + 1)
                dve.wait_ge(S(f"gain{j % 2}"), 16 * (j // 2 + 1))
                two = lambda v: v.rearrange("p (a b) -> p a b", a=2)
                for t in range(TT):
                    dve.scalar_tensor_tensor(two(normed[:, t, :]), psum[:, 2 * t:2 * t + 2, :], st[:, r, t:t + 1],
                                             two(gain_row[:, j % 2, :]), ALU.mult, ALU.mult)\
                        .then_inc(S("post_scaled"), 1)
                for t in range(TT):
                    dve.wait_ge(S("post_scaled"), 2 * j + t + 1)
                    dve.tensor_tensor(resid[:, t, :], resid[:, t, :], normed[:, t, :], ALU.add)\
                        .then_inc(S("resid_ready"), 1)

            def add(factor, name, n):
                dve.wait_ge(S(name), n)
                two = lambda v: v.rearrange("p (a b) -> p a b", a=2)
                for t in range(TT):
                    dve.scalar_tensor_tensor(two(resid[:, t, :]), psum[:, 2 * t:2 * t + 2, :], factor,
                                             two(resid[:, t, :]), ALU.mult, ALU.add).then_inc(S("resid_ready"), 1)

            def ffn(f):
                def tile(t, slot, n, b=None):
                    at = (lambda x: x) if b is None else (lambda x: b * 2 + x)
                    at2 = (lambda x: x) if b is None else (lambda x: b * 4 + x)
                    g, u = FT * f + t, U_OF_FFN[f] + t
                    if f < 2:
                        for tap, name in ((0, "tap_a"), (2, "tap_b")):
                            for s, buf in ((0, cg), (1, cv)):
                                dve.wait_ge(S("conv_mid" if tap == 0 else "tap_a"), at2(2 * g + s + 1))
                                w = at(V_CW + (f * 3 + tap) * 44 + s * FT + t)
                                o = slice(1, SEQ) if tap == 0 else slice(0, SEQ - 1)
                                x = slice(0, SEQ - 1) if tap == 0 else slice(1, SEQ)
                                dve.scalar_tensor_tensor(buf[0:n, slot, o], psum[0:n, 4 + 2 * slot + s, x],
                                                         vecs[0:n, bass.ds(w, 1)], buf[0:n, slot, o],
                                                         ALU.mult, ALU.add).then_inc(S(name), 1)
                    split_u(u + 2, b)
                    dve.wait_ge(S("gated"), at(g + 1))
                    if f < 2:
                        dve.wait_ge(S("tap_b"), at2(2 * g + 2))
                        val = cv[0:n, slot, :]
                    else:
                        dve.wait_ge(S("used_u"), at(u + 1))
                        val = psum[0:n, 5 + 2 * slot, 0:SEQ]
                    dve.tensor_tensor(hf[0:n, slot, :], gg[0:n, slot, :], val, ALU.mult).then_inc(S("hidden"), 1)
                    if b is not None or g >= 2:
                        dve.wait_ge(S("used_d"), at(g - 1))
                    dve.tensor_tensor(hid_hi[0:n, slot, :], gg[0:n, slot, :], val, ALU.mult)\
                        .then_inc(S("hid_hi_done"), 1)
                    dve.wait_ge(S("hidden"), at(g + 1))
                    dve.wait_ge(S("hid_hi_done"), at(g + 1))
                    dve.tensor_tensor(hid_lo[0:n, slot, :], hf[0:n, slot, :], hid_hi[0:n, slot, :].bitcast(F32),
                                      ALU.subtract).then_inc(S("hid_lo_done"), 1)
                    if b is not None or t + 1 < FT:
                        split_d(g + 1, b)

                split_d(FT * f)
                tile(0, 0, P)
                tile(1, 1, P)
                with dve.Fori(0, LOOPED) as b:
                    tile(2, 0, P, b)
                    tile(3, 1, P, b)
                tile(20, 0, P)
                tile(21, 1, width(f, 21))

            def mla():
                for u in range(2, 4):
                    split_u(u)
                ch = Chain(dve, S("dve_chain_mla"))
                dve.wait_ge(S("latent_sums"), 1)
                ch.link(dve.tensor_scalar(st[:, R_CQ, 0:2], st[:, R_CQ, 0:2], 1.0 / QL, EPS, ALU.mult, ALU.add))
                dve.tensor_scalar(st[:, R_CQ, 2:4], st[:, R_CQ, 2:4], 1.0 / KVL, EPS, ALU.mult, ALU.add)\
                    .then_inc(S("ms"), 1)
                dve.wait_ge(S("rope_in"), 32)
                raw = psum[:, 2:4, KVL:KVL + ROPE]
                ch.put(dve.tensor_tensor(kr3[:, 0], raw, ropek[:, 0], ALU.mult))
                ch.put(dve.tensor_tensor(kr3[:, 1, :, 0:32], raw[:, :, 32:64], ropek[:, 1, :, 32:64], ALU.mult))
                ch.put(dve.tensor_tensor(kr3[:, 1, :, 32:64], raw[:, :, 0:32], ropek[:, 1, :, 0:32], ALU.mult))
                ch.wait()
                dve.tensor_tensor(kr3[:, 2], kr3[:, 0], kr3[:, 1], ALU.add).then_inc(S("k_roped"), 1)
                dve.wait_ge(S("rstd"), R_CQ + 1)
                for t in range(TT):
                    dve.tensor_scalar(cq[:, t, :], psum[:, t, 0:QL], st[:, R_CQ, t:t + 1], None, ALU.mult)\
                        .then_inc(S("latents"), 1)
                for t in range(TT):
                    dve.tensor_scalar(ck[:, t, :], psum[:, 2 + t, 0:KVL], st[:, R_CQ, 2 + t:3 + t], None, ALU.mult)\
                        .then_inc(S("latents"), 1)
                for u in range(4, 6):
                    split_u(u)
                dve.wait_ge(S("latent_hi"), 5)
                for c in range(5):
                    b, o = (4 + c // 2, c % 2) if c < 3 else (6, c - 3)
                    v = V_QN + c if c < 3 else V_KVN + c - 3
                    dve.scalar_tensor_tensor(act_lo[:, c, :], psum[:, b, o * SEQ:o * SEQ + SEQ], vecs[:, v:v + 1],
                                             act_hi[:, c, :].bitcast(F32), ALU.mult, ALU.subtract)\
                        .then_inc(S("latent_lo"), 1)
                t1, t2 = qr2[:, 0], qr2[:, 1]
                both = lambda v: v.unsqueeze(1).broadcast_to([v.shape[0], 2, SEQ])
                for i in range(4):
                    dve.wait_ge(S("used_u"), U_UQ + i + 1)
                    if i:
                        dve.wait_ge(S("m_qr_out"), i)
                    raw = psum[0:ROPE, 2 * (i % 2) + 1, :].rearrange("p (h t) -> p h t", h=2)
                    ch.put(dve.tensor_tensor(t1, raw, both(ropeq[:, 0, :]), ALU.mult))
                    ch.put(dve.tensor_tensor(t2[0:32], raw[32:64], both(ropeq[32:64, 1, :]), ALU.mult))
                    dve.tensor_tensor(t2[32:64], raw[0:32], both(ropeq[0:32, 1, :]), ALU.mult)\
                        .then_inc(S("m_qr_read"), 1)
                    ch.wait()
                    dve.wait_ge(S("m_qr_read"), i + 1)
                    dve.tensor_tensor(m_qr[:, 2 * i:2 * i + 2, :], t1, t2, ALU.add).then_inc(S("m_qr_out"), 1)
                    split_u(U_UQ + i + 2)
                for i in range(2):
                    dve.wait_ge(S("used_u"), U_UKV + i + 1)
                    dve.tensor_copy(m_v[:, :, 4 * i:4 * i + 4, :], psum[:, 6:8, :].rearrange("p t (h d) -> p t h d", h=4))\
                        .then_inc(S("m_v_out"), 1)
                    split_u(U_UKV + i + 2)
                for i in range(H + 3):
                    if i < H:
                        dve.wait_ge(S("m_scores"), i + 1)
                        ch.link(dve.tensor_reduce(soft[:, i, 0, 0:2], psum[:, i % 3, :].rearrange("p (t k) -> p t k", t=2),
                                                  AX, ALU.max))
                        dve.tensor_scalar(soft[:, i, 1, 0:2], soft[:, i, 0, 0:2], -M_SCALE, None, ALU.mult)\
                            .then_inc(S("m_bias"), 1)
                    if 0 <= i - 1 < H:
                        h = i - 1
                        dve.wait_ge(S("m_exp"), 2 * h + 2)
                        ch.link(dve.reciprocal(soft[:, h, 3, 0:2], soft[:, h, 2, 0:2]))
                        for t in range(TT):
                            dve.tensor_scalar(m_p[:, h % 3, t, :], m_p[:, h % 3, t, :], soft[:, h, 3, t:t + 1], None,
                                              ALU.mult).then_inc(S("m_probs"), 1)
                    if i >= 3:
                        h = i - 3
                        dve.wait_ge(S("m_o_hi"), h + 1)
                        dve.tensor_tensor(act_lo[:, h, :], psum[:, 5 + h % 2, 0:SEQ], act_hi[:, h, :].bitcast(F32),
                                          ALU.subtract).then_inc(S("m_o_lo"), 1)
                for i in range(4):
                    split_u(U_MO + i + 2)

            def diff():
                ch = Chain(dve, S("dve_chain_diff"))
                dve.wait_ge(S("tables_in"), 16 * 9)
                pairs = lam[:, 0:256].rearrange("p (a b d) -> p a b d", a=2, b=2)
                prod = junk_d[:].rearrange("p (a d) -> p a d", a=2)
                ch.link(dve.tensor_tensor(prod, pairs[:, :, 0], pairs[:, :, 1], ALU.mult))
                dve.tensor_reduce(lam[:, 256:258], prod, AX, ALU.add).then_inc(S("lam_sums"), 1)
                for i in range(8):
                    split_u(U_QK + i + 2)
                for i in range(4):
                    split_u(U_V + i + 2)
                dve.wait_ge(S("lam_exp"), 1)
                ch.link(dve.tensor_tensor(lam[:, 260:261], lam[:, 258:259], lam[:, 259:260], ALU.subtract))
                ch.link(dve.tensor_scalar(lam[:, 260:261], lam[:, 260:261], LAM_INIT, None, ALU.add))
                dve.tensor_scalar(lam[:, 261:262], vecs[:, V_SUB:V_SUB + 1], 1.0 - LAM_INIT, None, ALU.mult)\
                    .then_inc(S("d_gain"), 1)
                for i in range(H + 3):
                    if i < H:
                        slope = 2.0 ** (-8.0 * (i + 1) / H)
                        if i >= 3:
                            dve.wait_ge(S("d_maps"), 2 * (i - 2))
                        for j in range(2):
                            dve.wait_ge(S("d_scores"), 2 * i + j + 1)
                            dve.scalar_tensor_tensor(d_x[:, i % 3, 2 * j:2 * j + 2, :], dist[:], -slope / D_SCALE,
                                                     psum[:, 2 * (i % 2) + j, :].rearrange("p (t k) -> p t k", t=2),
                                                     ALU.mult, ALU.add).then_inc(S("d_biased"), 1)
                        dve.wait_ge(S("d_biased"), 2 * i + 2)
                        ch.link(dve.tensor_reduce(soft[:, i, 0, 0:4], d_x[:, i % 3], AX, ALU.max))
                        dve.tensor_scalar(soft[:, i, 1, 0:4], soft[:, i, 0, 0:4], -D_SCALE, None, ALU.mult)\
                            .then_inc(S("d_bias"), 1)
                    if 0 <= i - 1 < H:
                        h = i - 1
                        dve.wait_ge(S("d_exp"), 4 * h + 4)
                        ch.link(dve.reciprocal(soft[:, h, 3, 0:4], soft[:, h, 2, 0:4]))
                        ch.link(dve.tensor_scalar(soft[:, h, 3, 2:4], soft[:, h, 3, 2:4], lam[:, 260:261], None, ALU.mult))
                        for t in range(TT):
                            n = ch.put(dve.tensor_scalar(d_x[:, h % 3, 2 + t, :], d_x[:, h % 3, 2 + t, :],
                                                         soft[:, h, 3, 2 + t:3 + t], None, ALU.mult))
                        if h >= 2:
                            dve.wait_ge(S("d_turned"), h - 1)
                        for t in range(TT):
                            ch.wait(n - 1 + t)
                            dve.scalar_tensor_tensor(d_a[:, h % 2, t, :], d_x[:, h % 3, t, :], soft[:, h, 3, t:t + 1],
                                                     d_x[:, h % 3, 2 + t, :], ALU.mult, ALU.subtract)\
                                .then_inc(S("d_maps"), 1)
                flat = d_o.rearrange("p t h d -> p (t h) d")
                sq = ar(6144, 2 * H, P)
                for t in range(TT):
                    dve.wait_ge(S("d_o_out"), H)
                    n = ch.put(dve.tensor_tensor(sq[:, t * H:t * H + H], flat[:, t * H:t * H + H],
                                                 flat[:, t * H:t * H + H], ALU.mult))
                ch.wait(n)
                ch.link(dve.tensor_reduce(st[:, R_SUB, :], sq, AX, ALU.add))
                mean_squares(R_SUB, 16, P)
                dve.wait_ge(S("rstd"), R_SUB + 1)
                for t in range(TT):
                    dve.tensor_tensor(flat[:, t * H:t * H + H], flat[:, t * H:t * H + H],
                                      st[:, R_SUB, t * H:t * H + H].unsqueeze(2).broadcast_to([P, H, P]), ALU.mult)\
                        .then_inc(S("d_normed"), 1)
                for b in range(4):
                    dve.wait_ge(S("d_hi"), b + 1)
                    dve.scalar_tensor_tensor(act_lo[:, 2 * b:2 * b + 2, :],
                                             psum[:, 4 + b, :].rearrange("p (k t) -> p k t", k=2), lam[:, 261:262],
                                             act_hi[:, 2 * b:2 * b + 2, :].bitcast(F32), ALU.mult, ALU.subtract)\
                        .then_inc(S("d_lo"), 1)
                for i in range(4):
                    split_u(U_DO + i + 2)

            def mix():
                ch = Chain(dve, S("dve_chain_mix"))
                both = lambda v: v.rearrange("p (h t) -> p h t", h=2)
                flat = lambda v: v.rearrange("p a b -> p (a b)")
                lb = vecs[:, V_LB:V_LB + 4]
                dve.tensor_tensor(bound[:, 0, :], lb, lb, ALU.subtract).then_inc(S("lb_shifted"), 1)
                for u in (U_NQ + 2, U_NQ + 3):
                    split_u(u)
                dve.wait_ge(S("used_u"), U_NC + 1)
                for v in range(2):
                    for g in range(2):
                        src = psum[g * HD:g * HD + HD, 2, v * SEQ:v * SEQ + SEQ].rearrange("p (c i l) -> p l i c", i=8, l=2)
                        for l in range(2):
                            r = slice(l * HD, l * HD + HD)
                            for half_block in range(2):
                                i0 = 8 * half_block
                                emb = vecs[r, V_POSK + 16 * v + i0:V_POSK + 16 * v + i0 + 8]
                                dve.tensor_tensor(c_x[r, v, i0:i0 + 8, g * NB:g * NB + NB],
                                                  src[:, l, :, half_block:half_block + NB],
                                                  emb.unsqueeze(2).broadcast_to([HD, 8, NB]), ALU.add)\
                                    .then_inc(S("c_x_done"), 1)
                split_u(U_NC + 2)
                for i, (u, dst) in enumerate(((U_NS, n_vs), (U_NW, n_vw))):
                    dve.wait_ge(S("used_u"), u + 1)
                    dve.tensor_copy(dst, psum[:, 4 + 2 * i, 0:2 * P].rearrange("p (t d) -> p t d", t=TT))\
                        .then_inc(S("n_v_out"), 1)
                    split_u(u + 2)
                dve.wait_ge(S("n_gates"), 1)
                cmp_gate = n_g.rearrange("p t (h b) -> p t h b", b=3)[:, :, :, 0]
                gates_masked = ch.put(dve.tensor_tensor(cmp_gate, cmp_gate, crows[:].unsqueeze(2).broadcast_to([P, TT, H]),
                                                        ALU.mult))
                for u in range(U_NG + 2, U_HI + 5):
                    split_u(u)
                for t in range(TT):
                    dve.wait_ge(S("used_u"), U_HI + 4)
                    dve.tensor_copy(h_v[:, t, :], psum[:, 4 + 2 * t, :]).then_inc(S("h_v_out"), 1)
                for v in range(2):
                    dve.wait_ge(S("c_hi"), v + 1)
                    dve.tensor_tensor(flat(act_lo[:, 2 * v:2 * v + 2, :])[:, 0:480], c_x[:, v].rearrange("p i c -> p (i c)"),
                                      flat(act_hi[:, 2 * v:2 * v + 2, :])[:, 0:480].bitcast(F32), ALU.subtract)\
                        .then_inc(S("c_lo"), 1)
                for u in range(U_HI + 5, U_WO + 2):
                    split_u(u)
                dve.wait_ge(S("h_g_out"), 2)
                gate = h_g.rearrange("p t (h d) -> p (t h) d", h=HGH)
                ch.put(dve.tensor_tensor(gate, gate, hgain[:].unsqueeze(1).broadcast_to([P, 8, P]), ALU.mult))
                dve.wait_ge(S("lb_exp"), 1)
                ch.link(dve.reciprocal(bound[:, 2, :], bound[:, 1, :]))
                ch.link(dve.tensor_tensor(bound[:, 3, :], bound[:, 1, :], bound[:, 2, :], ALU.mult))
                ch.link(dve.tensor_tensor(bound[:, 4, :], bound[:, 3, :], bound[:, 3, :], ALU.subtract))
                ch.link(dve.tensor_scalar(bound[:, 5, :], bound[:, 4, :], -1.0, 1.0, ALU.mult, ALU.add))
                for h in range(HGH):
                    dve.wait_ge(S("h_fk_out"), 2 * (h // 2) + 2)
                    ch.put(dve.tensor_scalar(h_f[:, h, :], h_f[:, h, :], bound[:, 5, h:h + 1], bound[:, 4, h:h + 1],
                                             ALU.mult, ALU.add))
                    ch.put(dve.tensor_scalar(h_k[:, h, :], h_k[:, h, :], bound[:, 5, h:h + 1], None, ALU.mult))
                ch.wait()
                ch.link(dve.tensor_scalar(h_f, h_f, 1e-30, None, ALU.max))
                dve.wait_ge(S("c_kv"), 1)
                ch.link(dve.memset(h_a, 0.0))
                dve.tensor_copy(bound[:, 0, :], bound[:, 4, :]).then_inc(S("h_ready"), 1)
                for i in range(H + 2):
                    if i < H:
                        slope = 2.0 ** (-8.0 * (i + 1) / H)
                        if i >= 2:
                            dve.wait_ge(S("n_turned"), i - 1)
                        dve.wait_ge(S("n_scores"), i + 1)
                        x = n_x[:, i % 2, :]
                        b = 2 * (i % 2)
                        for br in range(2):
                            dve.scalar_tensor_tensor(x[:, 384 * br:384 * br + 384], flat(causal[:]), -slope / D_SCALE,
                                                     psum[:, b + br, 0:384], ALU.mult, ALU.add).then_inc(S("n_biased"), 1)
                        dve.scalar_tensor_tensor(x[:, 768:798], flat(cdist[:]), -slope / D_SCALE, psum[:, b, 384:414],
                                                 ALU.mult, ALU.add).then_inc(S("n_biased"), 1)
                        dve.wait_ge(S("n_biased"), 3 * i + 3)
                        ch.put(dve.tensor_reduce(top[:, 0:6], x[:, 0:768].rearrange("p (m k) -> p m k", m=6), AX, ALU.max))
                        ch.link(dve.tensor_reduce(soft[:, i, 0, 0:2], x[:, 768:798].rearrange("p (m k) -> p m k", m=2),
                                                  AX, ALU.max))
                        t3 = top[:, 0:6].rearrange("p (b c) -> p b c", b=2)
                        mx = soft[:, i, 0, 2:6].rearrange("p (b t) -> p b t", b=2)
                        ch.put(dve.tensor_copy(mx[:, :, 0:1], t3[:, :, 0:1]))
                        ch.link(dve.tensor_tensor(mx[:, :, 1:2], t3[:, :, 1:2], t3[:, :, 2:3], ALU.max))
                        dve.tensor_scalar(soft[:, i, 1, 0:6], soft[:, i, 0, 0:6], -D_SCALE, None, ALU.mult)\
                            .then_inc(S("n_bias"), 1)
                    if 1 <= i <= H:
                        h = i - 1
                        dve.wait_ge(S("n_exp"), 6 * h + 6)
                        ch.link(dve.reciprocal(soft[:, h, 3, 0:6], soft[:, h, 2, 0:6]))
                        r = soft[:, h, 3, 0:6].rearrange("p (b t) -> p b t", b=3)
                        gates = n_g[:, :, 3 * h:3 * h + 3].rearrange("p t b -> p b t")
                        ch.link(dve.tensor_tensor(r, r, gates, ALU.mult))
                        x = n_x[:, h % 2, :]
                        for m, (at, n) in enumerate(N_PARTS):
                            dve.tensor_scalar(x[:, at:at + n], x[:, at:at + n], soft[:, h, 3, m:m + 1], None, ALU.mult)\
                                .then_inc(S("n_probs"), 1)
                        dve.wait_ge(S("n_turned"), h + 1)
                        if h >= 2:
                            dve.wait_ge(S("n_values"), h - 1)
                        dve.tensor_copy(n_pt[:, h % 2, 384:768], psum[:, 5, 0:384]).then_inc(S("n_pt_b"), 1)
                        dve.tensor_copy(n_pt[0:NB, h % 2, 896:1024], psum[0:NB, 5, 384:512]).then_inc(S("n_pt_b"), 1)
                    if i >= 2 and i % 2:
                        j = (i - 2) // 2
                        dve.wait_ge(S("n_o_hi"), j + 1)
                        dve.tensor_tensor(act_lo[:, j, :], psum[:, 6 + j % 2, 0:SEQ], act_hi[:, j, :].bitcast(F32),
                                          ALU.subtract).then_inc(S("n_o_lo"), 1)
                for l in range(8):
                    dve.wait_ge(S("h_level"), l + 1)
                    if l == 0:
                        dve.tensor_tensor(h_q, h_q, h_f, ALU.mult).then_inc(S("h_q_upd"), 1)
                    else:
                        m = 1 << (l - 1)
                        e = decay_of(m).rearrange("p (n s) -> p n s", s=2)
                        right = flat(h_q).rearrange("p (n s m) -> p n s m", s=2, m=m)[:, :, 1, :]
                        dve.wait_ge(S("h_q_upd"), l)
                        if l >= 2:
                            dve.wait_ge(S("h_e"), l - 1)
                        dve.tensor_tensor(right, right, e[:, :, 0:1].broadcast_to([P, 512 // m, m]), ALU.mult)\
                            .then_inc(S("h_q_upd"), 1)
                        if 2 * m <= 64:
                            dve.tensor_tensor(decay_of(2 * m), e[:, :, 0], e[:, :, 1], ALU.mult).then_inc(S("h_e"), 1)
                    if l:
                        dve.wait_ge(S("h_a_done"), l)
                    dve.copy_predicated(h_a, masks[:, l:l + 1, :].bitcast(U32).broadcast_to([P, 8, P]),
                                        psum[:, 2 * (l % 2):2 * (l % 2) + 2, :].rearrange("p a (b c) -> p (a b) c", b=4))\
                        .then_inc(S("h_a_done"), 1)
                dve.wait_ge(S("h_squares"), 1)
                ch.link(dve.tensor_reduce(st[:, R_HG, 0:8], h_sq, AX, ALU.add))
                mean_squares(R_HG, 8, P)
                dve.wait_ge(S("rstd"), R_HG + 1)
                o = h_o.rearrange("p t h d -> p (t h) d")
                for t in range(TT):
                    s = slice(4 * t, 4 * t + 4)
                    ch.put(dve.tensor_tensor(o[:, s], psum[:, 6 + t, :].rearrange("p (h d) -> p h d", h=HGH),
                                             st[:, R_HG, s].unsqueeze(2).broadcast_to([P, 4, P]), ALU.mult))
                for t in range(TT):
                    s = slice(4 * t, 4 * t + 4)
                    ch.wait(ch.n - 1 + t)
                    dve.tensor_tensor(o[:, s], o[:, s], gate[:, s], ALU.mult).then_inc(S("h_gated"), 1)
                for b in range(2):
                    dve.wait_ge(S("h_hi"), b + 1)
                    dve.tensor_tensor(act_lo[:, 4 + 2 * b:6 + 2 * b, :], both(psum[:, 4 + b, :]),
                                      act_hi[:, 4 + 2 * b:6 + 2 * b, :].bitcast(F32), ALU.subtract).then_inc(S("h_lo"), 1)
                for i in range(4):
                    split_u(U_WO + i + 2)

            dve.memset(zeros[:], 0.0).then_inc(S("zeros_set"), 1)
            for u in range(2):
                split_u(u)
            norm(N_MLA)
            mla()
            post(0)
            norm(N_F0)
            ffn(0)
            post(1)
            norm(N_DIFF)
            diff()
            post(2)
            norm(N_F1)
            ffn(1)
            post(3)
            norm(N_F2)
            ffn(2)
            add(0.5, "used_d", 3 * FT)
            norm(N_MIX)
            mix()
            add(1.0, "used_u", U_WO + 4)
            norm(N_F3)
            ffn(3)
            add(0.5, "used_d", 4 * FT)
            norm(N_FINAL)


_INS = ["x", "norm_g", "ffn_w_up", "ffn_conv_w", "ffn_conv_b", "ffn_w_down", "mla_w_dq", "mla_q_norm_g", "mla_w_uq",
        "mla_w_dkv", "mla_kv_norm_g", "mla_w_ukv", "mla_w_o", "diff_w_qkv", "diff_lambda", "diff_subln_g", "diff_w_o",
        "ffn1_norm_2", "ffn1_w_gu_2", "ffn1_w_down_2", "mix_norm_2", "w_in_2", "cmp_pos_k_2", "cmp_pos_v_2",
        "cmp_k_w1_2", "cmp_k_w2_2", "cmp_v_w1_2", "cmp_v_w2_2", "hgrn_lower_bound_2", "hgrn_out_norm_2", "w_out_2",
        "ffn2_norm_2", "ffn2_w_gu_2", "ffn2_w_down_2", "final_norm_2"]


def kernel(**inputs):
    import concourse.bacc as bacc
    from concourse.bass_utils import run_bass_kernel_spmd

    nc = bacc.Bacc("TRN2", target_bir_lowering=False, num_devices=1)
    arrays, aps = {}, {}

    def give(name, array):
        arrays[f"in_{name}"] = array
        aps[name] = nc.dram_tensor(f"in_{name}", array.shape, mybir.dt.from_np(array.dtype), kind="ExternalInput").ap()

    for name in _INS:
        x = np.ascontiguousarray(inputs[name])
        give(name, x)
    for name, table in constants().items():
        give(name, np.ascontiguousarray(table))
    out = nc.dram_tensor("out_0", (1, SEQ, D), F32, kind="ExternalOutput").ap()
    program(nc, aps, out)
    r = run_bass_kernel_spmd(nc, [arrays], core_ids=[0])
    return r.results[0]["out_0"]
```

```python
import math
from contextlib import ExitStack

import numpy as np

import concourse.bass as bass
from concourse import mybir

F32 = mybir.dt.float32
F32R = mybir.dt.float32r
BF16 = mybir.dt.bfloat16
U32 = mybir.dt.uint32
ACT = mybir.ActivationFunctionType
ALU = mybir.AluOpType
AX = mybir.AxisListType.X

P = 128
SEQ = 256
TT = SEQ // P
D = 1024
KC = D // P
EPS = 1e-6
BANK = 512

H = 8
NOPE, ROPE, VD = 128, 64, 128
QL, KVL = 384, 256
F1, F2 = 2816, 2752
FT = 22
LAM_INIT = 0.8 - 0.6 * math.exp(-0.3)
NSA_Q, HG = 512, 512
HD = 64
CMP = 32
STRIDE = 16
NB = SEQ // STRIDE - 1
HGH = 4
MASKED = 1e30

V_NORM = 0
V_FFN1 = V_NORM + 64
V_MIX = V_FFN1 + 8
V_FFN2 = V_MIX + 8
V_QN = V_FFN2 + 8
V_KVN = V_QN + 3
V_LB = V_KVN + 2
V_SUB = V_LB + 4
V_POSK = V_SUB + 1
V_POSV = V_POSK + 16
V_CW = V_POSV + 16
V_CB = V_CW + 264
V_ALL = V_CB + 88

C_Q, C_KC, C_VC, C_KS, C_VS, C_KW, C_VW, C_GL = 0, 512, 640, 768, 896, 1024, 1152, 1280
C_HQ, C_HF, C_HI = 1304, 1816, 2328

U_DQ = 0
U_DKV = U_DQ + 2
U_UQ = U_DKV + 2
U_UKV = U_UQ + 4
U_MO = U_UKV + 2
U_F0 = U_MO + 4
U_QK = U_F0 + FT
U_V = U_QK + 8
U_DO = U_V + 4
U_F1 = U_DO + 4
U_F2 = U_F1 + FT
U_NQ = U_F2 + FT
U_NC = U_NQ + 2
U_NK = U_NC + 1
U_NV = U_NK + 1
U_HQ = U_NV + 2
U_HF = U_HQ + 2
U_CK = U_HF + 2
U_CV = U_CK + 2
U_HI = U_CV + 2
U_WO = U_HI + 4
U_F3 = U_WO + 4
U_END = U_F3 + FT
U_OF_FFN = [U_F0, U_F1, U_F2, U_F3]
LOOPED = 9

N_MLA, N_F0, N_DIFF, N_F1, N_F2, N_MIX, N_F3, N_FINAL = range(8)


def constants():
    pos = np.arange(SEQ, dtype=np.float32)
    q = pos.reshape(TT, P).T[:, :, None]
    dist = np.abs(q - pos[None, None, :]).astype(np.float32)
    signed = q - pos[None, None, :]
    causal = np.where(signed >= 0, signed, MASKED).astype(np.float32)
    causal = np.concatenate([causal[:, 0, :P], causal[:, 1, :]], axis=1)
    ends = (np.arange(NB) * STRIDE + CMP - 1).astype(np.float32)
    cmp = q - ends[None, None, :]
    cmp = np.where(cmp >= 0, cmp, MASKED).astype(np.float32)
    rows = (q[:, :, 0] >= CMP - 1).astype(np.float32)
    inv = (np.float32(10000.0) ** (-np.arange(0, ROPE, 2, dtype=np.float32) / np.float32(ROPE))).astype(np.float32)
    ang = pos[:, None] * inv[None, :]
    cos, sin = np.cos(ang).astype(np.float32), np.sin(ang).astype(np.float32)
    cos2 = np.concatenate([cos, cos], 1)
    sin2 = np.concatenate([sin, -sin], 1)
    tok = lambda a: np.ascontiguousarray(a.reshape(TT, P, -1).transpose(1, 0, 2))
    s = np.arange(P)[:, None]
    t = np.arange(P)[None, :]
    masks = np.zeros((P, 8, P), np.float32)
    masks[:, 0, :] = s == t
    for i in range(7):
        m = 1 << i
        masks[:, i + 1, :] = (s // (2 * m) == t // (2 * m)) & (s % (2 * m) < m) & (t % (2 * m) >= m)
    return {
        "ident": np.eye(P, dtype=np.float32), "dist": dist.reshape(P, -1), "causal": causal,
        "cdist": cmp.reshape(P, -1), "crows": rows,
        "ropek": np.concatenate([tok(cos2), tok(sin2)], 1).reshape(P, -1),
        "ropeq": np.concatenate([cos2.T, sin2.T], 1), "masks": masks.reshape(P, -1),
    }


ROOTS = ([("norm0", 0), ("norm0", 1), ("latents", 0), ("post0", 0), ("post0", 1), ("norm1", 0), ("norm1", 1),
          ("post1", 0), ("post1", 1), ("norm2", 0), ("norm2", 1), ("heads", 0), ("heads", 1), ("post2", 0),
          ("post2", 1), ("norm3", 0), ("norm3", 1), ("post3", 0), ("post3", 1), ("norm4", 0), ("norm4", 1),
          ("norm5", 0), ("norm5", 1), ("hgrn", 0), ("norm6", 0), ("norm6", 1), ("norm7", 0), ("norm7", 1)])
ST_OF = {name: i for i, name in enumerate(dict.fromkeys(n for n, _ in ROOTS))}


def root_no(name, part=0):
    return ROOTS.index((name, part)) + 1


WARM = [(0, 0, 0), (0, 0, 0), (0, 0, 0), (0, 0, 0), (0, 0, 0), (0, 0, 0), (0, 0, 0)]
V_OF_NORM = [V_NORM, V_NORM + 16, V_NORM + 32, V_NORM + 48, V_FFN1, V_MIX, V_FFN2]
M_SCALE = (NOPE + ROPE) ** -0.5
D_SCALE = HD ** -0.5
N_PARTS = [(768, NB), (768 + NB, NB), (0, P), (P, 2 * P), (3 * P, P), (4 * P, 2 * P)]


class Chain:

    def __init__(self, eng, sem):
        self.eng, self.sem, self.n = eng, sem, 0

    def put(self, ins):
        ins.then_inc(self.sem, 1)
        self.n += 1
        return self.n

    def wait(self, n=None):
        self.eng.wait_ge(self.sem, self.n if n is None else n)

    def link(self, ins):
        self.put(ins)
        self.wait()


def program(nc, a, out):
    ctx = ExitStack()
    sems = {}

    def S(name):
        if name not in sems:
            sems[name] = ctx.enter_context(nc.semaphore(name))
        return sems[name]

    def sb(name, shape, dt=F32):
        return ctx.enter_context(nc.sbuf_tensor(name, shape, dt))

    with ctx:
        psum = ctx.enter_context(nc.psum_tensor("psum", [P, 8, BANK], F32))

        resid = sb("resid", [P, TT, D])
        normed = sb("normed", [P, TT, D])
        act_hi = sb("act_hi", [P, KC, SEQ], F32R)
        act_lo = sb("act_lo", [P, KC, SEQ], F32R)
        raw_u = sb("raw_u", [P, 2, 2048])
        hi_u = sb("hi_u", [P, 2, 2048], F32R)
        lo_u = sb("lo_u", [P, 2, 2048], F32R)
        raw_d = sb("raw_d", [P, 2, 1024])
        hi_d = sb("hi_d", [P, 2, 1024], F32R)
        lo_d = sb("lo_d", [P, 2, 1024], F32R)
        hid_hi = sb("hid_hi", [P, 2, SEQ], F32R)
        hid_lo = sb("hid_lo", [P, 2, SEQ], F32R)
        gain_row = sb("gain_row", [P, 2, D])
        vecs = sb("vecs", [P, V_ALL])
        ident = sb("ident", [P, P])
        zeros = sb("zeros", [P, BANK], BF16)
        half = sb("half", [P, 16])
        st = sb("st", [P, len(ST_OF), 16])
        junk = sb("junk", [P, D])
        soft = sb("soft", [P, 8, 4, 8])
        lam = sb("lam", [P, 272])
        junk_d = sb("junk_d", [P, P])
        bound = sb("bound", [P, 6, 4])
        top = sb("top", [P, 8])
        masks = sb("masks", [P, 8, P])
        cdist = sb("cdist", [P, TT, NB])
        crows = sb("crows", [P, TT])
        slopes = sb("slopes", [P, H, P], BF16)
        dist_b = sb("dist_b", [P, TT, SEQ], BF16)
        causal_b = sb("causal_b", [P, 3 * P + TT * NB], BF16)
        w2k = sb("w2k", [P, 2, HD])
        w2v = sb("w2v", [P, 2, HD])
        hgain = sb("hgain", [P, P])
        dist = sb("dist", [P, TT, SEQ])
        causal = sb("causal", [P, 3, P])
        arena = sb("arena", [P, 12288])

        def ar(at, *shape, p=P):
            n = int(np.prod(shape))
            v = arena[0:p, at:at + n]
            if len(shape) == 2:
                v = v.rearrange("p (a b) -> p a b", a=shape[0])
            if len(shape) == 3:
                v = v.rearrange("p (a b c) -> p a b c", a=shape[0], b=shape[1])
            return v

        vrows = ar(0, 6, P)
        VROWS = [(V_NORM, 98), (V_POSK, 32), (V_CW, 88), (V_CW + 88, 88), (V_CW + 176, 88), (V_CB, 88)]
        cg, cv, gg, hf = (ar(512 * i, 2, SEQ) for i in range(4))

        def u_slot(t, u):
            return t[:, u % 2, :]

        def cols(w, c0, n):
            return w[:, c0:c0 + n].rearrange("(k p) n -> p k n", p=P)

        def rows(w, k0, n):
            return w[k0 * P:(k0 + n) * P, :].rearrange("(k p) n -> p k n", p=P)

        w_up, w_down = a["ffn_w_up"], a["ffn_w_down"]
        gu = [None, None, a["ffn1_w_gu_2"][0], a["ffn2_w_gu_2"][0]]
        dn = [w_down[0], w_down[1], a["ffn1_w_down_2"][0], a["ffn2_w_down_2"][0]]
        gu[0], gu[1] = w_up[0], w_up[1]
        FW = [F1, F1, F2, F2]
        units = {}
        w_in = a["w_in_2"][0]
        for i in range(2):
            units[U_DQ + i] = rows(a["mla_w_dq"][0], 4 * i, 4)
            units[U_DKV + i] = rows(a["mla_w_dkv"][0], 4 * i, 4)
            units[U_UKV + i] = cols(a["mla_w_ukv"][0], 1024 * i, 1024)
            units[U_NQ + i] = cols(w_in, C_Q + 256 * i, 256)
            units[U_HQ + i] = cols(w_in, C_HQ + 256 * i, 256)
            units[U_HF + i] = cols(w_in, C_HF + 256 * i, 256)
            units[U_CK + i] = rows(a["cmp_k_w1_2"][0], 8 * i, 8)
            units[U_CV + i] = rows(a["cmp_v_w1_2"][0], 8 * i, 8)
        for i in range(4):
            units[U_UQ + i] = cols(a["mla_w_uq"][0], 384 * i, 384)
            units[U_MO + i] = rows(a["mla_w_o"][0], 2 * i, 2)
            units[U_V + i] = rows(a["diff_w_qkv"][0][:, 2048:3072], 2 * i, 2)
            units[U_DO + i] = rows(a["diff_w_o"][0], 2 * i, 2)
            units[U_HI + i] = rows(w_in[:, C_HI:C_HI + 1024], 2 * i, 2)
            units[U_WO + i] = rows(a["w_out_2"][0], 2 * i, 2)
        for i in range(8):
            units[U_QK + i] = cols(a["diff_w_qkv"][0], 256 * i, 256)
        units[U_NC] = cols(w_in, C_KC, 256)
        units[U_NK] = [cols(w_in, C_KS, P), cols(w_in, C_KW, P)]
        for i in range(2):
            units[U_NV + i] = [cols(w_in, c, n)[:, 4 * i:4 * i + 4] for c, n in ((C_VS, P), (C_VW, P + 24))]

        def width(f, t):
            return min(P, FW[f] - t * P) if isinstance(t, int) else P

        def unit_view(t, u):
            if isinstance(u, int) and u in units:
                parts = units[u] if isinstance(units[u], list) else [units[u]]
                k, n = parts[0].shape[1], sum(p.shape[2] for p in parts)
                return u_slot(t, u)[:, 0:k * n].rearrange("p (k n) -> p k n", k=k)
            return u_slot(t, u)

        def up_view(t, slot, s, n):
            return t[:, slot, 1024 * s:1024 * s + 1024].rearrange("p (k n) -> p k n", k=KC)[:, :, 0:n]

        m_q = ar(0, H, SEQ)
        m_qr = ar(2048, H, SEQ, p=ROPE)
        m_k = ar(4096, H, SEQ)
        m_v = ar(6144, TT, H, VD)
        m_kr = ar(8192, SEQ, p=ROPE)
        ropek = ar(8448, 2, TT, ROPE)
        ropeq = ar(8704, 2, SEQ, p=ROPE)
        m_p = ar(9216, 3, TT, SEQ)
        m_pt = ar(10752, 2, 2, SEQ)
        cq = normed[:].rearrange("p a b -> p (a b)")[:, 0:768].rearrange("p (t n) -> p t n", t=TT)
        ck = normed[:].rearrange("p a b -> p (a b)")[:, 768:1280].rearrange("p (t n) -> p t n", t=TT)
        kr3 = normed[:].rearrange("p a b -> p (a b)")[:, 1280:1664].rearrange("p (a t n) -> p a t n", a=3, t=TT)
        qr2 = normed[0:ROPE, :, :].rearrange("p a (b t) -> p a b t", b=4)[:, :, 0:2, :]
        d_q = ar(0, H, SEQ)
        d_k = ar(2048, H, SEQ)
        d_v = ar(4096, TT, D)
        d_x = ar(6144, 3, 4, SEQ)
        d_a = ar(9216, 2, TT, SEQ)
        d_at = ar(10240, 2, 2, SEQ)
        d_o = normed[:].rearrange("p t (h d) -> p t h d", h=H)
        d_sq = ar(11264, 2, 4, P)
        n_q = ar(0, 4, SEQ)
        n_k = ar(1024, 4, SEQ)
        n_vs = ar(2048, TT, P)
        n_vw = ar(2304, TT, P)
        n_g = ar(2560, TT, 24)
        h_q = ar(2624, HGH, SEQ)
        h_f = ar(3648, HGH, SEQ)
        h_k = ar(4672, HGH, SEQ)
        h_v = ar(5696, TT, 512)
        h_g = ar(6720, TT, 512)
        h_a = ar(7744, 8, P)
        h_ax = ar(8768, HGH, P)
        h_e = ar(9280, 1024)
        n_x = ar(10304, 2, 800)
        c_x = normed[:].rearrange("p a b -> p (a b)")[:, 0:960].rearrange("p (v i c) -> p v i c", v=2, i=16)
        c_xhi, c_xlo = (x[:, 0, 0:960].rearrange("p (v i c) -> p v i c", v=2, i=16) for x in (hi_d, lo_d))
        c_h = normed[0:30, 1, 0:512].rearrange("p (v n) -> p v n", v=2)
        c_ht = normed[:, 1, 512:632].rearrange("p (a b) -> p a b", a=4)
        c_k = ar(11904, 2, NB)
        c_v = ar(11936, 2, HD, p=NB)
        n_pt = normed[:]
        h_o = ar(0, TT, HGH, P)

        h_sq = ar(10304, 8, P)

        def decay_of(m):
            if m == 1:
                return h_f.rearrange("p h t -> p (h t)")
            at = 1024 - 2048 // m
            return h_e[:, at:at + 1024 // m]

        block = ctx.enter_context(nc.Block())

        @block.sync
        def _(sp):
            def load_unit(u):
                if u >= 2:
                    sp.wait_ge(S("hi_u_done"), u - 1)
                    sp.wait_ge(S("lo_u_done"), u - 1)
                if isinstance(units[u], list):
                    at = 0
                    for part in units[u]:
                        sp.dma_start(unit_view(raw_u, u)[:, :, at:at + part.shape[2]], part).then_inc(S(f"raw_u{u % 2}"), 16)
                        at += part.shape[2]
                    return
                k = units[u].shape[1]
                for k0, k1 in ((0, k // 2), (k // 2, k)):
                    sp.dma_start(unit_view(raw_u, u)[:, k0:k1], units[u][:, k0:k1]).then_inc(S(f"raw_u{u % 2}"), 16)

            def load_up(f, t, slot, n):
                u = t + U_OF_FFN[f]
                sp.wait_ge(S("hi_u_done"), u - 1)
                sp.wait_ge(S("lo_u_done"), u - 1)
                for s in range(2):
                    src = gu[f][:, bass.ds(t * P + s * FW[f], n)].rearrange("(k p) n -> p k n", p=P)
                    sp.dma_start(up_view(raw_u, slot, s, n), src).then_inc(S(f"raw_u{slot}"), 16)

            def load_down(f, t, slot, n):
                d = t + FT * f
                if f or not isinstance(t, int) or t >= 2:
                    sp.wait_ge(S("hi_d_done"), d - 1)
                    sp.wait_ge(S("lo_d_done"), d - 1)
                sp.dma_start(raw_d[0:n, slot, :], dn[f][bass.ds(t * P, n), :]).then_inc(S(f"raw_d{slot}"), 16)

            def ffn(f):
                for t in range(2):
                    load_up(f, t, t, P)
                    load_down(f, t, t, P)
                with sp.Fori(1, LOOPED + 1) as b:
                    for t in range(2):
                        load_up(f, b * 2 + t, t, P)
                        load_down(f, b * 2 + t, t, P)
                for t in range(2 * LOOPED + 2, FT):
                    load_up(f, t, t % 2, width(f, t))
                    load_down(f, t, t % 2, width(f, t))

            def load_gain(i):
                g = a["norm_g"]
                src = [g[0, 1], g[0, 3], g[1, 1], g[1, 3], a["final_norm_2"]][i]
                if i >= 2:
                    sp.wait_ge(S("resid_ready"), 2 * (i - 1))
                sp.dma_start(gain_row[:, i % 2, :], src.partition_broadcast(P)).then_inc(S(f"gain{i % 2}"), 16)

            for t in range(TT):
                sp.dma_start(resid[:, t, :], a["x"][0, t * P:t * P + P, :]).then_inc(S(f"x_in{t}"), 16)
            sp.dma_start(ident[:], a["ident"]).then_inc(S("ident_in"), 16)
            load_unit(0)
            rows_in = S("vrows_in")
            sp.dma_start(vrows[0:64, 0, :], a["norm_g"].rearrange("l n (k p) -> (l n k) p", p=P)).then_inc(rows_in, 16)
            at = 64
            for name, n in (("ffn1_norm_2", 8), ("mix_norm_2", 8), ("ffn2_norm_2", 8), ("mla_q_norm_g", 3),
                            ("mla_kv_norm_g", 2), ("hgrn_lower_bound_2", 4), ("diff_subln_g", 1)):
                sp.dma_start(vrows[at:at + n, 0, :],
                             a[name].rearrange("l (k p) -> (l k) p", p=P)).then_inc(rows_in, 16)
                at += n
            for i, name in enumerate(("cmp_pos_k_2", "cmp_pos_v_2")):
                sp.dma_start(vrows[16 * i:16 * i + 16, 1, :],
                             a[name][0].rearrange("(i l) d -> i (l d)", l=2)).then_inc(rows_in, 16)
            cw = a["ffn_conv_w"].rearrange("l j (k p) -> (l j k) p", p=P)
            for i in range(3):
                sp.dma_start(vrows[0:88, 2 + i, :], cw[88 * i:88 * i + 88, :]).then_inc(rows_in, 16)
            sp.dma_start(vrows[0:88, 5, :], a["ffn_conv_b"].rearrange("l (k p) -> (l k) p", p=P)).then_inc(rows_in, 16)
            load_unit(1)
            sp.dma_start(ropek, a["ropek"].rearrange("p (a t r) -> p a t r", a=2, t=TT)).then_inc(S("rope_in"), 16)
            sp.dma_start(ropeq, a["ropeq"].rearrange("p (a t) -> p a t", a=2)).then_inc(S("rope_in"), 16)
            load_gain(0)
            for u in range(2, U_F0):
                load_unit(u)
            load_gain(1)
            ffn(0)
            sp.dma_start(dist[:], a["dist"].rearrange("p (t k) -> p t k", t=TT)).then_inc(S("tables_in"), 16)
            sp.dma_start(causal[:], a["causal"].rearrange("p (t k) -> p t k", t=3)).then_inc(S("tables_in"), 16)
            sp.dma_start(lam[:, 0:256], a["diff_lambda"].rearrange("l a d -> (l a d)").partition_broadcast(P)).then_inc(S("tables_in"), 16)
            sp.dma_start(masks[:], a["masks"].rearrange("p (t k) -> p t k", t=8)).then_inc(S("tables_in"), 16)
            sp.dma_start(cdist[:], a["cdist"].rearrange("p (t k) -> p t k", t=TT)).then_inc(S("tables_in"), 16)
            sp.dma_start(crows[:], a["crows"]).then_inc(S("tables_in"), 16)
            sp.dma_start(w2k[:], a["cmp_k_w2_2"][0].rearrange("(c p) d -> p c d", p=P)).then_inc(S("tables_in"), 16)
            sp.dma_start(w2v[:], a["cmp_v_w2_2"][0].rearrange("(c p) d -> p c d", p=P)).then_inc(S("tables_in"), 16)
            sp.dma_start(hgain[:], a["hgrn_out_norm_2"][0].partition_broadcast(P)).then_inc(S("tables_in"), 16)
            load_gain(2)
            for u in range(U_QK, U_F1):
                load_unit(u)
            load_gain(3)
            ffn(1)
            load_gain(4)
            ffn(2)
            for u in range(U_NQ, U_F3):
                load_unit(u)
            ffn(3)
            for t in range(TT):
                sp.wait_ge(S("final"), t + 1)
                sp.dma_start(out[0, t * P:t * P + P, :], normed[:, t, :]).then_inc(S("stored"), 16)
            sp.wait_ge(S("stored"), 32)

        @block.gpsimd
        def _(pool):
            pool.memset(half[:], -0.5).then_inc(S("half_set"), 1)
            pool.wait_ge(S("half_set"), 1)

            def root(name, part, c0, n, over, ready, count):
                v = st[:, ST_OF[name], c0:c0 + n]
                pool.wait_ge(S(ready), count)
                pool.tensor_scalar(v, v, 1.0 / over, EPS, ALU.mult, ALU.add).then_inc(S("mean_squares"), 1)
                k[0] += 1
                pool.wait_ge(S("mean_squares"), k[0])
                return pool.tensor_tensor(v, v, half[:, 0:n], ALU.pow)

            k = [0]

            def norm_roots(i):
                for t in range(TT):
                    root(f"norm{i}", t, t, 1, D, "row_sums", 2 * i + t + 1).then_inc(S("rstd"), 1)

            def post_roots(j):
                for t in range(TT):
                    root(f"post{j}", t, t, 1, D, "post_sums", 2 * j + t + 1).then_inc(S("rstd"), 1)

            def hgrn():
                for l in range(1, 8):
                    m = 1 << (l - 1)
                    pool.wait_ge(S("h_level"), 2 * l + 2)
                    if l >= 2:
                        pool.wait_ge(S("h_e"), l - 1)
                        pool.wait_ge(S("h_k_upd"), l - 1)
                    e = decay_of(m).rearrange("p (n s) -> p n s", s=2)
                    left = h_k.rearrange("p h t -> p (h t)").rearrange("p (n s m) -> p n s m", s=2, m=m)[:, :, 0, :]
                    pool.tensor_tensor(left, left, e[:, :, 1:2].broadcast_to([P, 512 // m, m]), ALU.mult)\
                        .then_inc(S("h_k_upd"), 1)

            norm_roots(N_MLA)
            pool.wait_ge(S("ident_in"), 16)
            for h in range(H):
                slope = 2.0 ** (-8.0 * (h + 1) / H)
                pool.tensor_scalar(slopes[:, h, :], ident[:], -slope / D_SCALE, None, ALU.mult).then_inc(S("slopes"), 1)
            root("latents", 0, 0, 2, QL, "latent_sums", 1).then_inc(S("q_latent_root"), 1)
            root("latents", 0, 2, 2, KVL, "latent_sums", 1).then_inc(S("rstd"), 1)
            post_roots(0)
            norm_roots(N_F0)
            post_roots(1)
            norm_roots(N_DIFF)
            pool.wait_ge(S("tables_in"), 16 * 9)
            pool.tensor_copy(dist_b[:], dist[:]).then_inc(S("bias_tables"), 1)
            pool.tensor_copy(causal_b[:, 0:3 * P], causal[:].rearrange("p a b -> p (a b)")).then_inc(S("bias_tables"), 1)
            pool.tensor_copy(causal_b[:, 3 * P:], cdist[:].rearrange("p a b -> p (a b)")).then_inc(S("bias_tables"), 1)
            for g in range(2):
                root("heads", g, 8 * g, 8, P, "d_sums", 8 * g + 8).then_inc(S("rstd"), 1)
            post_roots(2)
            norm_roots(N_F1)
            post_roots(3)
            norm_roots(N_F2)
            norm_roots(N_MIX)
            pool.memset(h_a, 0.0).then_inc(S("h_a_zero"), 1)
            gate = h_g.rearrange("p t (h d) -> p (t h) d", h=HGH)
            pool.wait_ge(S("h_g_out"), 2)
            pool.tensor_tensor(gate, gate, hgain[:].unsqueeze(1).broadcast_to([P, 8, P]), ALU.mult)\
                .then_inc(S("h_g_gained"), 1)
            hgrn()
            root("hgrn", 0, 0, 8, P, "h_sums", 1).then_inc(S("rstd"), 1)
            norm_roots(N_F3)
            norm_roots(N_FINAL)

        @block.tensor
        def _(pe):
            def mm3(o, s_hi, s_lo, m_hi, m_lo, start, stop):
                pe.matmul(o, s_hi, m_hi, start=start, stop=False)
                pe.matmul(o, s_hi, m_lo, start=False, stop=False)
                return pe.matmul(o, s_lo, m_hi, start=False, stop=stop)

            def keep_warm(n):
                for _ in range(n):
                    pe.matmul(psum[:, 5, :], zeros[:, 0:P], zeros[:], start=True, stop=True)

            def unit_ready(u):
                pe.wait_ge(S("hi_u_done"), u + 1)
                pe.wait_ge(S("lo_u_done"), u + 1)

            def tok(t):
                return slice(t * P, t * P + P)

            def norm_transposes(i):
                for t in range(TT):
                    keep_warm(WARM[i][t])
                    pe.wait_ge(S("normed"), 2 * i + t + 1)
                    for b in range(4):
                        for k in (b, b + 4):
                            at = (k // 4) * SEQ + t * P
                            mm = pe.transpose(psum[:, b, at:at + P], normed[:, t, k * P:k * P + P], ident[:])
                        if t == 1:
                            mm.then_inc(S("norm_tr"), 1)
                keep_warm(WARM[i][2])

            def tokens_out(o, u, k0, w0, n, first, last, i=None):
                hi, lo = unit_view(hi_u, u), unit_view(lo_u, u)
                for k in range(hi.shape[1]):
                    if i is not None:
                        pe.wait_ge(S("act_lo"), 8 * i + k0 + k + 1)
                    for t in range(TT):
                        mm = mm3(o(t), act_hi[:, k0 + k, tok(t)], act_lo[:, k0 + k, tok(t)],
                                 hi[:, k, w0:w0 + n], lo[:, k, w0:w0 + n],
                                 first and k == 0, last and k == hi.shape[1] - 1)
                return mm

            def features_out(o, u, w0, n, c0=0, i=None):
                hi, lo = unit_view(hi_u, u), unit_view(lo_u, u)
                kn = hi.shape[1]
                for k in range(kn):
                    if i is not None:
                        pe.wait_ge(S("act_lo"), 8 * i + k + 1)
                    mm = mm3(o, hi[:, k, w0:w0 + n], lo[:, k, w0:w0 + n], act_hi[:, c0 + k, :], act_lo[:, c0 + k, :],
                             k == 0, k == kn - 1)
                return mm

            def wide(u0, chunk_ready, before={}):
                def part(i, k, t):
                    hi, lo = unit_view(hi_u, u0 + i), unit_view(lo_u, u0 + i)
                    for n in range(2):
                        mm = mm3(psum[:, 2 * t + n, :], act_hi[:, 2 * i + k, tok(t)], act_lo[:, 2 * i + k, tok(t)],
                                 hi[:, k, n * BANK:n * BANK + BANK], lo[:, k, n * BANK:n * BANK + BANK],
                                 i == 0 and k == 0, i == 3 and k == 1)
                    return mm

                for i in range(3):
                    if i in before:
                        before[i]()
                    unit_ready(u0 + i)
                    for k in range(2):
                        chunk_ready(2 * i + k)
                        for t in range(TT):
                            mm = part(i, k, t)
                    mm.then_inc(S("used_u"), 1)
                unit_ready(u0 + 3)
                for t in range(TT):
                    for k in range(2):
                        if t == 0:
                            chunk_ready(6 + k)
                        mm = part(3, k, t)
                    mm.then_inc(S("first_half" if t == 0 else "used_u"), 1)

            def ffn(f):
                i = [N_F0, N_F1, N_F2, N_F3][f]

                def up(t, slot, n, first=False):
                    g, u = t + FT * f, t + U_OF_FFN[f]
                    unit_ready(u)
                    if not isinstance(t, int) or t >= 2:
                        if f < 2:
                            pe.wait_ge(S("tap_b"), g * 2 - 2)
                        else:
                            pe.wait_ge(S("hid_hi_done"), g - 1)
                    for s in range(2):
                        hi, lo = up_view(hi_u, slot, s, n), up_view(lo_u, slot, s, n)
                        for k in range(KC):
                            if first and s == 0:
                                pe.wait_ge(S("act_lo"), 8 * i + k + 1)
                            mm = mm3(psum[0:n, 4 + 2 * slot + s, 0:SEQ], hi[:, k, :], lo[:, k, :],
                                     act_hi[:, k, :], act_lo[:, k, :], k == 0, k == KC - 1)
                        mm.then_inc(S("gate_up" if s == 0 else "used_u"), 1)

                def down(t, slot, n, last=False, tiles=range(TT)):
                    g = t + FT * f
                    pe.wait_ge(S("hi_d_done"), g + 1)
                    pe.wait_ge(S("lo_d_done"), g + 1)
                    pe.wait_ge(S("hid_lo_done"), g + 1)
                    for tk in tiles:
                        for c in range(2):
                            w = slice(c * BANK, c * BANK + BANK)
                            mm = mm3(psum[:, 2 * tk + c, :], hid_hi[0:n, slot, tok(tk)], hid_lo[0:n, slot, tok(tk)],
                                     hi_d[0:n, slot, w], lo_d[0:n, slot, w], False, last)
                    mm.then_inc(S("used_d" if TT - 1 in tiles else "first_part"), 1)

                up(0, 0, P, True)
                pe.wait_ge(S("zeros_set"), 1)
                for b in range(4):
                    pe.matmul(psum[:, b, :], zeros[:, 0:P], zeros[:], start=True, stop=False)
                up(1, 1, P)
                down(0, 0, P)
                with pe.Fori(0, LOOPED) as b:
                    up(b * 2 + 2, 0, P)
                    down(b * 2 + 1, 1, P)
                    up(b * 2 + 3, 1, P)
                    down(b * 2 + 2, 0, P)
                up(20, 0, P)
                down(19, 1, P)
                up(21, 1, width(f, 21))
                down(20, 0, P, tiles=[0])
                down(21, 1, width(f, 21), True, [0])
                down(20, 0, P, tiles=[1])
                down(21, 1, width(f, 21), True, [1])

            def mla():
                for i in range(2):
                    unit_ready(U_DQ + i)
                    mm = tokens_out(lambda t: psum[:, 4 + t, 0:QL], U_DQ + i, 4 * i, 0, QL, i == 0, i == 1, N_MLA)
                    mm.then_inc(S("used_u"), 1)
                for i in range(2):
                    unit_ready(U_DKV + i)
                    mm = tokens_out(lambda t: psum[:, 6 + t, 0:KVL + ROPE], U_DKV + i, 4 * i, 0, KVL + ROPE,
                                    i == 0, i == 1)
                    mm.then_inc(S("used_u"), 1)
                pe.wait_ge(S("latents"), 2)
                for c in range(3):
                    for t in range(TT):
                        pe.transpose(psum[:, c // 2, (c % 2) * SEQ + t * P:(c % 2) * SEQ + t * P + P],
                                     cq[:, t, c * P:c * P + P], ident[:])
                pe.wait_ge(S("latents"), 4)
                for c in range(2):
                    for t in range(TT):
                        pe.transpose(psum[:, 2, c * SEQ + t * P:c * SEQ + t * P + P],
                                     ck[:, t, c * P:c * P + P], ident[:])
                pe.wait_ge(S("k_roped"), 1)
                for t in range(TT):
                    mm = pe.transpose(psum[0:ROPE, 3, t * P:t * P + P], kr3[:, 2, t, :], ident[:])
                mm.then_inc(S("latent_tr"), 1)
                pe.wait_ge(S("latent_lo"), 5)
                for i in range(4):
                    u = U_UQ + i
                    unit_ready(u)
                    b = 4 + 2 * (i % 2)
                    if i >= 2:
                        pe.wait_ge(S("m_q_out"), i - 1)
                        pe.wait_ge(S("m_qr_read"), i - 1)
                    for h in range(2):
                        mm = features_out(psum[:, b, h * SEQ:h * SEQ + SEQ], u, h * 192, NOPE)
                    mm.then_inc(S("m_q_up"), 1)
                    for h in range(2):
                        mm = features_out(psum[0:ROPE, b + 1, h * SEQ:h * SEQ + SEQ], u, h * 192 + NOPE, ROPE)
                    mm.then_inc(S("used_u"), 1)
                for i in range(2):
                    u = U_UKV + i
                    unit_ready(u)
                    hi, lo = unit_view(hi_u, u), unit_view(lo_u, u)
                    if i == 0:
                        pe.wait_ge(S("m_kr_out"), 1)
                    else:
                        pe.wait_ge(S("m_k_out"), 1)
                        pe.wait_ge(S("m_v_out"), 1)
                    for h in range(4):
                        mm = features_out(psum[:, h // 2, (h % 2) * SEQ:(h % 2) * SEQ + SEQ], u, h * 256, NOPE, 3)
                    mm.then_inc(S("m_k_up"), 1)
                    for t in range(TT):
                        for k in range(2):
                            v_hi, v_lo = (x[:, k, :].rearrange("p (h n) -> p h n", h=4)[:, :, NOPE:] for x in (hi, lo))
                            mm = mm3(psum[:, 2 + t, :], act_hi[:, 3 + k, tok(t)], act_lo[:, 3 + k, tok(t)],
                                     v_hi, v_lo, k == 0, k == 1)
                    mm.then_inc(S("used_u"), 1)

                def scores(h):
                    if h >= 3:
                        pe.wait_ge(S("m_exp"), 2 * (h - 2))
                    for t in range(TT):
                        o = psum[:, h % 3, t * SEQ:t * SEQ + SEQ]
                        pe.matmul(o, m_q[:, h, tok(t)], m_k[:, h, :], start=True, stop=False)
                        mm = pe.matmul(o, m_qr[:, h, tok(t)], m_kr, start=False, stop=True)
                    mm.then_inc(S("m_scores"), 1)

                def turn(h):
                    pe.wait_ge(S("m_probs"), 2 * h + 2)
                    if h >= 2:
                        pe.wait_ge(S("m_pt"), h - 1)
                    for k in range(2):
                        for t in range(TT):
                            mm = pe.transpose(psum[:, 3 + h % 2, k * SEQ + t * P:k * SEQ + t * P + P],
                                              m_p[:, h % 3, t, k * P:k * P + P], ident[:])
                    mm.then_inc(S("m_turned"), 1)

                def values(h):
                    pe.wait_ge(S("m_pt"), h + 1)
                    if h >= 2:
                        pe.wait_ge(S("m_o_lo"), h - 1)
                    for k in range(2):
                        mm = pe.matmul(psum[:, 5 + h % 2, 0:SEQ], m_v[:, k, h, :], m_pt[:, h % 2, k, :],
                                       start=k == 0, stop=k == 1)
                    mm.then_inc(S("m_values"), 1)

                pe.wait_ge(S("m_q_out"), 4)
                pe.wait_ge(S("m_qr_out"), 4)
                pe.wait_ge(S("m_k_out"), 2)
                pe.wait_ge(S("m_v_out"), 2)
                for i in range(H + 3):
                    if i < H:
                        scores(i)
                    if 0 <= i - 2 < H:
                        turn(i - 2)
                    if i >= 3:
                        values(i - 3)
                wide(U_MO, lambda c: pe.wait_ge(S("m_o_lo"), c + 1))

            def diff():
                for i in range(8):
                    u = U_QK + i
                    unit_ready(u)
                    if i >= 4:
                        pe.wait_ge(S("d_qk_out"), i - 3)
                    for h in range(2):
                        mm = features_out(psum[:, 4 + i % 4, h * SEQ:h * SEQ + SEQ], u, h * P, P,
                                          i=N_DIFF if i == 0 and h == 0 else None)
                    mm.then_inc(S("used_u"), 1)

                def v_unit(i):
                    unit_ready(U_V + i)
                    for n in range(2):
                        mm = tokens_out(lambda t: psum[:, 2 * t + n, :], U_V + i, 2 * i, n * BANK, BANK, i == 0, i == 3)
                    mm.then_inc(S("used_u"), 1)

                def scores(h):
                    if h >= 2:
                        pe.wait_ge(S("d_exp"), 4 * (h - 1))
                    for j in range(2):
                        r, b = slice(j * HD, j * HD + HD), 4 + 2 * (h % 2) + j
                        pe.matmul(psum[:, b, :], slopes[:, h, :], dist_b[:].rearrange("p t k -> p (t k)"),
                                  start=True, stop=False)
                        for t in range(TT):
                            mm = pe.matmul(psum[:, b, t * SEQ:t * SEQ + SEQ], d_q[r, h, tok(t)], d_k[r, h, :],
                                           start=False, stop=t == 1)
                    mm.then_inc(S("d_scores"), 1)

                def turn(h):
                    pe.wait_ge(S("d_maps"), 2 * h + 2)
                    if h >= 2:
                        pe.wait_ge(S("d_at"), h - 1)
                    for k in range(2):
                        for t in range(TT):
                            mm = pe.transpose(psum[:, h % 2, k * SEQ + t * P:k * SEQ + t * P + P],
                                              d_a[:, h % 2, t, k * P:k * P + P], ident[:])
                    mm.then_inc(S("d_turned"), 1)

                def values(h):
                    pe.wait_ge(S("d_at"), h + 1)
                    if h >= 2:
                        pe.wait_ge(S("d_o_out"), 2 * (h - 1))
                    for t in range(TT):
                        for k in range(2):
                            mm = pe.matmul(psum[:, 2 + h % 2, t * P:t * P + P], d_at[:, h % 2, k, tok(t)],
                                           d_v[:, k, h * P:h * P + P], start=k == 0, stop=k == 1)
                    mm.then_inc(S("d_values"), 1)

                def heads_turn(g):
                    pe.wait_ge(S("d_normed"), 2 * g + 2)
                    for b in (2 * g, 2 * g + 1):
                        for k in range(2):
                            for t in range(TT):
                                mm = pe.transpose(psum[:, 4 + b, k * SEQ + t * P:k * SEQ + t * P + P],
                                                  d_o[:, t, 2 * b + k, :], ident[:])
                        mm.then_inc(S("d_tr"), 1)

                v_unit(0)
                pe.wait_ge(S("d_qk_out"), 8)
                pe.wait_ge(S("slopes"), 8)
                pe.wait_ge(S("bias_tables"), 3)
                scores(0)
                scores(1)
                for i in range(1, 4):
                    v_unit(i)
                pe.wait_ge(S("d_v_out"), 2)
                for i in range(H + 1):
                    if i + 2 < H:
                        scores(i + 2)
                    if i >= 1:
                        values(i - 1)
                    if i < H:
                        turn(i)
                    if i == H - 1:
                        heads_turn(0)
                pe.wait_ge(S("d_o_out"), 16)
                wide(U_DO, lambda c: pe.wait_ge(S("d_lo"), c // 2 + 1), {2: lambda: heads_turn(1)})

            def mix():
                for i in range(2):
                    unit_ready(U_NQ + i)
                    for h in range(2):
                        mm = features_out(psum[:, 4 + i, h * SEQ:h * SEQ + SEQ], U_NQ + i, h * P, P,
                                          i=N_MIX if i == 0 and h == 0 else None)
                    mm.then_inc(S("used_u"), 1)
                unit_ready(U_NC)
                for v in range(2):
                    mm = features_out(psum[:, 6, v * SEQ:v * SEQ + SEQ], U_NC, v * P, P)
                mm.then_inc(S("used_u"), 1)
                unit_ready(U_NK)
                for i in range(2):
                    mm = features_out(psum[:, i, 0:SEQ], U_NK, i * P, P)
                mm.then_inc(S("used_u"), 1)
                for i in range(2):
                    unit_ready(U_NV + i)
                    mm = tokens_out(lambda t: psum[:, 2 + t, 0:280], U_NV + i, 4 * i, 0, 280, i == 0, i == 1)
                    mm.then_inc(S("used_u"), 1)
                pe.wait_ge(S("n_q_out"), 2)
                for i in range(2):
                    unit_ready(U_HQ + i)
                    for h in range(2):
                        mm = features_out(psum[:, 4 + i, h * SEQ:h * SEQ + SEQ], U_HQ + i, h * P, P)
                    mm.then_inc(S("used_u"), 1)
                pe.wait_ge(S("n_k_out"), 8)
                for i in range(2):
                    unit_ready(U_HF + i)
                    for h in range(2):
                        mm = features_out(psum[:, i, h * SEQ:h * SEQ + SEQ], U_HF + i, h * P, P)
                    mm.then_inc(S("used_u"), 1)
                for v in range(2):
                    pe.wait_ge(S("c_lo"), v + 1)
                    for i in range(2):
                        u = (U_CK, U_CV)[v] + i
                        unit_ready(u)
                        hi, lo = unit_view(hi_u, u), unit_view(lo_u, u)
                        for k in range(8):
                            mm = mm3(psum[0:30, 6 + v, 0:256], c_xhi[:, v, 8 * i + k, :], c_xlo[:, v, 8 * i + k, :],
                                     hi[:, k, :], lo[:, k, :], i == 0 and k == 0, i == 1 and k == 7)
                        mm.then_inc(S("used_u"), 1)

                def values_and_gates(i):
                    unit_ready(U_HI + i)
                    for n in range(2):
                        mm = tokens_out(lambda t: psum[:, 2 * t + n, :], U_HI + i, 2 * i, n * BANK, BANK,
                                        i == 0, i == 3)
                    mm.then_inc(S("used_u"), 1)

                pe.wait_ge(S("n_v_out"), 2)
                pe.wait_ge(S("n_gates"), 1)
                pe.wait_ge(S("h_fk_out"), 4)
                values_and_gates(0)
                pe.wait_ge(S("h_q_out"), 2)
                pe.wait_ge(S("c_h_out"), 2)
                for v in range(2):
                    for c in range(2):
                        mm = pe.transpose(psum[:, 4, (2 * v + c) * 30:(2 * v + c) * 30 + 30],
                                          c_h[:, v, c * P:c * P + P], ident[0:30, 0:30])
                mm.then_inc(S("c_h_tr"), 1)
                values_and_gates(1)
                pe.wait_ge(S("c_ht_out"), 1)
                for e in range(2):
                    for g in range(2):
                        for c in range(2):
                            mm = pe.matmul(psum[e * HD:e * HD + HD, 5, g * NB:g * NB + NB], w2k[:, c, :],
                                           c_ht[:, c, g * NB:g * NB + NB], start=c == 0, stop=c == 1)
                for g in range(2):
                    for c in range(2):
                        mm = pe.matmul(psum[0:NB, 6, g * HD:g * HD + HD], c_ht[:, 2 + c, g * NB:g * NB + NB],
                                       w2v[:, c, :], start=c == 0, stop=c == 1)
                mm.then_inc(S("c_kv"), 1)
                values_and_gates(2)
                values_and_gates(3)

                def scores(h):
                    b, r, j, g = 4 + 2 * (h % 2), slice((h % 2) * HD, (h % 2) * HD + HD), h // 2, h // 4
                    if h >= 2:
                        pe.wait_ge(S("n_exp"), 6 * (h - 1))
                    for br in range(2):
                        k = n_k[r, 2 * br + g, :]
                        n = 3 * P + (0 if br else TT * NB)
                        pe.matmul(psum[:, b + br, 0:n], slopes[:, h, :], causal_b[:, 0:n], start=True, stop=False)
                        if br == 0:
                            for t in range(TT):
                                pe.matmul(psum[:, b, 3 * P + t * NB:3 * P + t * NB + NB], n_q[r, j, tok(t)],
                                          c_k[r, g, :], start=False, stop=False)
                        pe.matmul(psum[:, b + br, 0:P], n_q[r, j, tok(0)], k[:, 0:P], start=False, stop=False)
                        mm = pe.matmul(psum[:, b + br, P:3 * P], n_q[r, j, tok(1)], k, start=False, stop=True)
                    mm.then_inc(S("n_scores"), 1)

                def turn(h):
                    pe.wait_ge(S("n_probs"), 6 * h + 6)
                    if h >= 1:
                        pe.wait_ge(S("n_pt_a"), 2 * h)
                        pe.wait_ge(S("n_pt_b"), 2 * h)
                    x = n_x[:, h % 2, :]
                    for br in range(2):
                        for c in range(3):
                            pe.transpose(psum[:, br, c * P:c * P + P], x[:, (3 * br + c) * P:(3 * br + c + 1) * P],
                                         ident[:])
                        mm = pe.transpose(psum[0:NB, br, 3 * P:4 * P], x[:, 768 + br * NB:768 + br * NB + NB], ident[:])
                    mm.then_inc(S("n_turned"), 1)

                def values(h):
                    r, j, g = slice((h % 2) * HD, (h % 2) * HD + HD), h // 2, h // 4
                    pe.wait_ge(S("n_pt_a"), 2 * h + 2)
                    pe.wait_ge(S("n_pt_b"), 2 * h + 2)
                    if j >= 1:
                        pe.wait_ge(S("n_o_lo"), j)
                    o, pt, gs = psum[r, 2, 0:SEQ], n_pt[:, h % 2, :], slice(g * HD, g * HD + HD)
                    pe.matmul(o, c_v[:, g, :], pt[0:NB, 768:1024], start=True, stop=False)
                    pe.matmul(o, n_vs[:, 0, gs], pt[:, 0:256], start=False, stop=False)
                    pe.matmul(o, n_vw[:, 0, gs], pt[:, 384:640], start=False, stop=False)
                    pe.matmul(o[:, P:], n_vs[:, 1, gs], pt[:, 256:384], start=False, stop=False)
                    pe.matmul(o[:, P:], n_vw[:, 1, gs], pt[:, 640:768], start=False, stop=True)\
                        .then_inc(S("n_values"), 1)

                def level(l, t):
                    if t == 0 and l >= 1:
                        pe.wait_ge(S("h_q_upd"), l)
                    if t == 0 and l >= 2:
                        pe.wait_ge(S("h_k_upd"), l - 1)
                    if l or t:
                        pe.wait_ge(S("h_a_done"), 2 * l + t)
                    for h in range(HGH):
                        mm = pe.matmul(psum[:, 3, h * P:h * P + P], h_k[:, h, tok(t)], h_q[:, h, tok(t)],
                                       start=True, stop=True)
                    mm.then_inc(S("h_level"), 1)

                pe.wait_ge(S("c_kv_out"), 2)
                for i in range(H + 2):
                    if i < H:
                        scores(i)
                    if i == 0:
                        pe.wait_ge(S("h_ready"), 1)
                        pe.wait_ge(S("h_v_out"), 2)
                        pe.wait_ge(S("h_g_out"), 2)
                    if i < 8:
                        level(i, 0)
                    if i >= 2:
                        values(i - 2)
                    if i < 8:
                        level(i, 1)
                    if 1 <= i <= H:
                        turn(i - 1)
                pe.wait_ge(S("h_q_upd"), 8)
                pe.wait_ge(S("h_k_upd"), 7)
                pe.wait_ge(S("h_a_done"), 16)
                for h in range(HGH):
                    mm = pe.matmul(psum[:, 3, h * P:h * P + P], h_k[:, h, tok(0)], h_q[:, h, tok(1)],
                                   start=True, stop=True)
                mm.then_inc(S("h_level"), 1)
                v = [[h_v[:, t, h * P:h * P + P] for t in range(TT)] for h in range(HGH)]
                for h in range(HGH):
                    pe.matmul(psum[:, 4, h * P:h * P + P], h_a[:, h, :], v[h][0], start=True, stop=True)
                pe.wait_ge(S("h_ax_out"), 1)
                for h in range(HGH):
                    pe.matmul(psum[:, 5, h * P:h * P + P], h_ax[:, h, :], v[h][0], start=True, stop=False)
                    mm = pe.matmul(psum[:, 5, h * P:h * P + P], h_a[:, 4 + h, :], v[h][1], start=False, stop=True)
                mm.then_inc(S("h_out"), 1)

                def h_turn():
                    pe.wait_ge(S("h_gated"), 2)
                    for h in range(HGH):
                        for t in range(TT):
                            mm = pe.transpose(psum[:, 6 + h // 2, (h % 2) * SEQ + t * P:(h % 2) * SEQ + t * P + P],
                                              h_o[:, t, h, :], ident[:])
                        if h % 2:
                            mm.then_inc(S("h_tr"), 1)

                pe.wait_ge(S("n_o_lo"), 4)
                wide(U_WO, lambda c: pe.wait_ge(S("n_o_lo"), c + 1) if c < 4 else pe.wait_ge(S("h_lo"), (c - 2) // 2),
                     {2: h_turn})

            pe.wait_ge(S("ident_in"), 16)
            pe.wait_ge(S("vrows_in"), 16 * 14)
            for i, (at, n) in enumerate(VROWS):
                mm = pe.transpose(psum[:, 4, at:at + n], vrows[0:n, i, :], ident[0:n, 0:n])
            mm.then_inc(S("vecs_tr"), 1)
            norm_transposes(N_MLA)
            mla()
            norm_transposes(N_F0)
            ffn(0)
            norm_transposes(N_DIFF)
            diff()
            norm_transposes(N_F1)
            ffn(1)
            norm_transposes(N_F2)
            ffn(2)
            norm_transposes(N_MIX)
            mix()
            norm_transposes(N_F3)
            ffn(3)

        @block.scalar
        def _(act):
            def split_u(u):
                if isinstance(u, int):
                    if u >= U_END:
                        return
                    act.wait_ge(S(f"raw_u{u % 2}"), 32 * (u // 2 + 1))
                    if u >= 2:
                        act.wait_ge(S("used_u"), u - 1)
                    act.activation(unit_view(hi_u, u), unit_view(raw_u, u), ACT.Copy).then_inc(S("hi_u_done"), 1)

            def split_u_looped(b, u0):
                act.wait_ge(S(f"raw_u{u0 % 2}"), b * 32 + 32 * (u0 // 2 + 1))
                act.wait_ge(S("used_u"), b * 2 + (u0 - 1))
                act.activation(u_slot(hi_u, u0), u_slot(raw_u, u0), ACT.Copy).then_inc(S("hi_u_done"), 1)

            def split_d(d, b=None):
                act.wait_ge(S(f"raw_d{d % 2}"), 16 * (d // 2 + 1) if b is None else b * 16 + 16 * (d // 2 + 1))
                if b is not None:
                    act.wait_ge(S("used_d"), b * 2 + (d - 1))
                elif d >= 2:
                    act.wait_ge(S("used_d"), d - 1)
                act.activation(hi_d[:, d % 2, :], raw_d[:, d % 2, :], ACT.Copy).then_inc(S("hi_d_done"), 1)

            def norm(i):
                for t in range(TT):
                    if i == N_MLA:
                        act.wait_ge(S(f"x_in{t}"), 16)
                    else:
                        act.wait_ge(S("resid_ready"), 2 * (i - 1) + t + 1)
                    act.activation(junk[:], resid[:, t, :], ACT.Square, accum_out=st[:, ST_OF[f"norm{i}"], t:t + 1])\
                        .then_inc(S("row_sums"), 1)
                    act.wait_ge(S("row_sums"), 2 * i + t + 1)
                if i == N_FINAL:
                    return
                if i == N_MLA:
                    act.wait_ge(S("vecs_tr"), 1)
                    act.activation(vecs[:], psum[:, 4, 0:V_ALL], ACT.Copy).then_inc(S("vecs_ready"), 1)
                    act.wait_ge(S("vecs_ready"), 1)
                for k in range(KC):
                    act.wait_ge(S("norm_tr"), 4 * i + k % 4 + 1)
                    if k >= 4:
                        act.wait_ge(S("act_lo"), 8 * i + k - 3)
                    act.activation(act_hi[:, k, :], psum[:, k % 4, (k // 4) * SEQ:(k // 4) * SEQ + SEQ], ACT.Copy,
                                   scale=vecs[:, V_OF_NORM[i] + k:V_OF_NORM[i] + k + 1]).then_inc(S("act_hi"), 1)

            def post_sums(j, halves, whole, n):
                for t, (name, count) in enumerate(((halves, (j // 2 + 1) * (2 if j % 2 else 1)), (whole, n))):
                    act.wait_ge(S(name), count)
                    act.activation(junk[:].rearrange("p (a b) -> p a b", a=2), psum[:, 2 * t:2 * t + 2, :], ACT.Square,
                                   accum_out=st[:, ST_OF[f"post{j}"], t:t + 1]).then_inc(S("post_sums"), 1)
                    act.wait_ge(S("post_sums"), 2 * j + t + 1)

            def ffn(f):
                def tile(t, slot, n, b=None):
                    at = (lambda x: x) if b is None else (lambda x: b * 2 + x)
                    g, u = FT * f + t, U_OF_FFN[f] + t
                    looped_or_late = b is not None or g >= 2
                    act.wait_ge(S("gate_up"), at(g + 1))
                    if f < 2:
                        if looped_or_late:
                            act.wait_ge(S("hid_lo_done"), at(g - 1))
                        for s, buf in ((0, cg), (1, cv)):
                            if s:
                                act.wait_ge(S("used_u"), at(u + 1))
                            w = at(V_CW + (f * 3 + 1) * 44 + s * FT + t)
                            c = at(V_CB + f * 44 + s * FT + t)
                            act.activation(buf[0:n, slot, :], psum[0:n, 4 + 2 * slot + s, 0:SEQ], ACT.Identity,
                                           scale=vecs[0:n, bass.ds(w, 1)], bias=vecs[0:n, bass.ds(c, 1)])\
                                .then_inc(S("conv_mid"), 1)
                    else:
                        act.wait_ge(S("hid_hi_done"), at(g - 1))
                        act.activation(gg[0:n, slot, :], psum[0:n, 4 + 2 * slot, 0:SEQ], ACT.Silu)\
                            .then_inc(S("gated"), 1)
                    if b is None:
                        split_u(u + 2)
                    else:
                        split_u_looped(b, u + 2)
                    if f < 2:
                        act.wait_ge(S("tap_b"), b * 4 + 2 * g + 1 if b is not None else 2 * g + 1)
                        act.activation(gg[0:n, slot, :], cg[0:n, slot, :], ACT.Gelu_apprx_tanh).then_inc(S("gated"), 1)
                    if b is not None or t + 1 < FT:
                        split_d(g + 1, b)

                split_d(FT * f)
                tile(0, 0, P)
                tile(1, 1, P)
                with act.Fori(0, LOOPED) as b:
                    tile(2, 0, P, b)
                    tile(3, 1, P, b)
                tile(20, 0, P)
                tile(21, 1, width(f, 21))

            def mla():
                for u in range(2, 4):
                    split_u(u)
                ch = Chain(act, S("act_chain_mla"))
                act.wait_ge(S("used_u"), U_DQ + 2)
                for t in range(TT):
                    ch.link(act.activation(junk[:, 0:QL], psum[:, 4 + t, 0:QL], ACT.Square, accum_out=st[:, ST_OF["latents"], t:t + 1]))
                act.wait_ge(S("used_u"), U_DKV + 2)
                for t in range(TT):
                    ins = act.activation(junk[:, 0:KVL], psum[:, 6 + t, 0:KVL], ACT.Square,
                                         accum_out=st[:, ST_OF["latents"], 2 + t:3 + t])
                    if t == 0:
                        ch.link(ins)
                ins.then_inc(S("latent_sums"), 1)
                for u in range(4, 6):
                    split_u(u)
                act.wait_ge(S("latent_tr"), 1)
                for c in range(5):
                    b, o = (c // 2, c % 2) if c < 3 else (2, c - 3)
                    v = V_QN + c if c < 3 else V_KVN + c - 3
                    act.activation(act_hi[:, c, :], psum[:, b, o * SEQ:o * SEQ + SEQ], ACT.Copy,
                                   scale=vecs[:, v:v + 1]).then_inc(S("latent_hi"), 1)
                act.activation(m_kr, psum[0:ROPE, 3, 0:SEQ], ACT.Copy).then_inc(S("m_kr_out"), 1)
                for i in range(4):
                    act.wait_ge(S("m_q_up"), i + 1)
                    act.activation(m_q[:, 2 * i:2 * i + 2, :], psum[:, 4 + 2 * (i % 2), :].rearrange("p (h t) -> p h t", h=2),
                                   ACT.Copy).then_inc(S("m_q_out"), 1)
                    split_u(U_UQ + i + 2)
                for i in range(2):
                    act.wait_ge(S("m_k_up"), i + 1)
                    act.activation(m_k[:, 4 * i:4 * i + 4, :],
                                   psum[:, 0:2, :].rearrange("p b (h t) -> p (b h) t", h=2), ACT.Copy)\
                        .then_inc(S("m_k_out"), 1)
                    split_u(U_UKV + i + 2)
                for i in range(H + 3):
                    if i < H:
                        act.wait_ge(S("m_bias"), i + 1)
                        if i >= 3:
                            act.wait_ge(S("m_turned"), i - 2)
                        for t in range(TT):
                            act.activation(m_p[:, i % 3, t, :], psum[:, i % 3, t * SEQ:t * SEQ + SEQ], ACT.Exp,
                                           scale=M_SCALE, bias=soft[:, i, 1, t:t + 1],
                                           accum_out=soft[:, i, 2, t:t + 1]).then_inc(S("m_exp"), 1)
                    if 0 <= i - 2 < H:
                        h = i - 2
                        act.wait_ge(S("m_turned"), h + 1)
                        if h >= 2:
                            act.wait_ge(S("m_values"), h - 1)
                        act.activation(m_pt[:, h % 2], psum[:, 3 + h % 2, :].rearrange("p (k t) -> p k t", k=2),
                                       ACT.Copy).then_inc(S("m_pt"), 1)
                    if i >= 3:
                        h = i - 3
                        act.wait_ge(S("m_values"), h + 1)
                        act.activation(act_hi[:, h, :], psum[:, 5 + h % 2, 0:SEQ], ACT.Copy).then_inc(S("m_o_hi"), 1)
                for i in range(3):
                    split_u(U_MO + i + 2)

            def diff():
                for i in range(8):
                    split_u(U_QK + i + 2)
                    act.wait_ge(S("used_u"), U_QK + i + 1)
                    act.activation((d_q if i < 4 else d_k)[:, 2 * (i % 4):2 * (i % 4) + 2, :],
                                   psum[:, 4 + i % 4, :].rearrange("p (h t) -> p h t", h=2), ACT.Copy)\
                        .then_inc(S("d_qk_out"), 1)
                act.wait_ge(S("lam_sums"), 1)
                act.activation(lam[:, 258:260], lam[:, 256:258], ACT.Exp).then_inc(S("lam_exp"), 1)

                def exps(h):
                    act.wait_ge(S("d_bias"), h + 1)
                    if h >= 3:
                        act.wait_ge(S("d_maps"), 2 * (h - 2))
                    for m in range(4):
                        act.activation(d_x[:, h % 3, m, :], psum[:, 4 + 2 * (h % 2) + m // 2, (m % 2) * SEQ:(m % 2) * SEQ + SEQ],
                                       ACT.Exp, scale=D_SCALE, bias=soft[:, h, 1, m:m + 1],
                                       accum_out=soft[:, h, 2, m:m + 1]).then_inc(S("d_exp"), 1)

                def heads_hi(g):
                    for b in (2 * g, 2 * g + 1):
                        act.wait_ge(S("d_tr"), b + 1)
                        act.activation(act_hi[:, 2 * b:2 * b + 2, :], psum[:, 4 + b, :].rearrange("p (k t) -> p k t", k=2),
                                       ACT.Copy, scale=lam[:, 261:262]).then_inc(S("d_hi"), 1)

                split_u(U_V + 2)
                exps(0)
                split_u(U_V + 3)
                exps(1)
                split_u(U_V + 4)
                for t in range(TT):
                    act.wait_ge(S("used_u"), U_V + 4)
                    act.activation(d_v[:, t, :].rearrange("p (a b) -> p a b", a=2), psum[:, 2 * t:2 * t + 2, :],
                                   ACT.Copy).then_inc(S("d_v_out"), 1)
                act.wait_ge(S("d_gain"), 1)
                for i in range(H + 1):
                    if i + 2 < H:
                        exps(i + 2)
                    if i >= 1:
                        h = i - 1
                        act.wait_ge(S("d_values"), h + 1)
                        for t in range(TT):
                            act.activation(d_o[:, t, h, :], psum[:, 2 + h % 2, t * P:t * P + P], ACT.Copy,
                                           scale=soft[:, h, 3, t:t + 1]).then_inc(S("d_o_out"), 1)
                    if i < H:
                        act.wait_ge(S("d_turned"), i + 1)
                        if i >= 2:
                            act.wait_ge(S("d_values"), i - 1)
                        act.activation(d_at[:, i % 2], psum[:, i % 2, :].rearrange("p (k t) -> p k t", k=2),
                                       ACT.Copy).then_inc(S("d_at"), 1)
                    if i == 1:
                        split_u(U_V + 5)
                heads_hi(0)
                split_u(U_DO + 2)
                heads_hi(1)
                split_u(U_DO + 3)
                split_u(U_DO + 4)

            def mix():
                both = lambda v: v.rearrange("p (h t) -> p h t", h=2)
                act.wait_ge(S("lb_shifted"), 1)
                act.activation(bound[:, 1, :], bound[:, 0, :], ACT.Exp).then_inc(S("lb_exp"), 1)
                for i in range(2):
                    act.wait_ge(S("used_u"), U_NQ + i + 1)
                    split_u(U_NQ + i + 2)
                    act.activation(n_q[:, 2 * i:2 * i + 2, :], both(psum[:, 4 + i, :]), ACT.Copy).then_inc(S("n_q_out"), 1)
                split_u(U_NC + 2)
                act.wait_ge(S("used_u"), U_NK + 1)
                split_u(U_NK + 2)
                for i in range(2):
                    for g in range(2):
                        for e in range(2):
                            act.activation(n_k[e * HD:e * HD + HD, 2 * i + g, :],
                                           psum[g * HD:g * HD + HD, i, 0:SEQ], ACT.Copy)\
                                .then_inc(S("n_k_out"), 1)
                split_u(U_NV + 2)
                act.wait_ge(S("used_u"), U_NV + 2)
                act.activation(n_g, psum[:, 2:4, 256:280], ACT.Sigmoid).then_inc(S("n_gates"), 1)
                split_u(U_NV + 3)
                act.wait_ge(S("c_x_done"), 16)
                for v in range(2):
                    act.activation(c_xhi[:, v], c_x[:, v], ACT.Copy).then_inc(S("c_hi"), 1)
                for i in range(2):
                    act.wait_ge(S("used_u"), U_HQ + i + 1)
                    split_u(U_HQ + i + 2)
                    act.activation(h_q[:, 2 * i:2 * i + 2, :], both(psum[:, 4 + i, :]), ACT.Silu).then_inc(S("h_q_out"), 1)
                for i in range(2):
                    act.wait_ge(S("used_u"), U_HF + i + 1)
                    split_u(U_HF + i + 2)
                    for sign, dst in ((1.0, h_f), (-1.0, h_k)):
                        act.activation(dst[:, 2 * i:2 * i + 2, :], both(psum[:, i, :]), ACT.Sigmoid, scale=sign)\
                            .then_inc(S("h_fk_out"), 1)
                for v in range(2):
                    u = (U_CK, U_CV)[v]
                    split_u(u + 2)
                    split_u(u + 3)
                    act.wait_ge(S("used_u"), u + 2)
                    act.activation(c_h[:, v, :], psum[0:30, 6 + v, 0:256], ACT.Gelu_apprx_tanh).then_inc(S("c_h_out"), 1)
                split_u(U_HI + 2)
                act.wait_ge(S("c_h_tr"), 1)
                act.activation(c_ht, psum[:, 4, 0:120].rearrange("p (a b) -> p a b", a=4), ACT.Copy)\
                    .then_inc(S("c_ht_out"), 1)
                split_u(U_HI + 3)
                act.wait_ge(S("c_kv"), 1)
                act.activation(c_k, psum[:, 5, 0:30].rearrange("p (a b) -> p a b", a=2), ACT.Copy)\
                    .then_inc(S("c_kv_out"), 1)
                act.activation(c_v, psum[0:NB, 6, 0:P].rearrange("p (a b) -> p a b", a=2), ACT.Copy)\
                    .then_inc(S("c_kv_out"), 1)
                split_u(U_HI + 4)
                for t in range(TT):
                    act.wait_ge(S("used_u"), U_HI + 4)
                    act.activation(h_g[:, t, :], psum[:, 1 + 2 * t, :], ACT.Silu).then_inc(S("h_g_out"), 1)
                for i in range(H + 2):
                    if i < H:
                        act.wait_ge(S("n_bias"), i + 1)
                        if i >= 2:
                            act.wait_ge(S("n_turned"), i - 1)
                        for m, (at, n) in enumerate(N_PARTS):
                            branch, col = (0, 3 * P + m * NB) if m < 2 else ((m - 2) // 2, (m % 2) * P)
                            act.activation(n_x[:, i % 2, at:at + n], psum[:, 4 + 2 * (i % 2) + branch, col:col + n], ACT.Exp,
                                           scale=D_SCALE, bias=soft[:, i, 1, m:m + 1],
                                           accum_out=soft[:, i, 2, m:m + 1]).then_inc(S("n_exp"), 1)
                    if i == H:
                        split_u(U_HI + 5)
                    if 1 <= i <= H:
                        h = i - 1
                        act.wait_ge(S("n_turned"), h + 1)
                        if h >= 2:
                            act.wait_ge(S("n_values"), h - 1)
                        act.activation(n_pt[:, h % 2, 0:384], psum[:, 0, 0:384], ACT.Copy).then_inc(S("n_pt_a"), 1)
                        act.activation(n_pt[0:NB, h % 2, 768:896], psum[0:NB, 0, 384:512], ACT.Copy)\
                            .then_inc(S("n_pt_a"), 1)
                    if i >= 2 and i % 2:
                        j = (i - 2) // 2
                        act.wait_ge(S("n_values"), 2 * j + 2)
                        act.activation(act_hi[:, j, :], psum[:, 2, 0:SEQ], ACT.Copy).then_inc(S("n_o_hi"), 1)
                act.wait_ge(S("h_level"), 17)
                act.activation(h_ax, psum[:, 3, :].rearrange("p (h t) -> p h t", h=HGH), ACT.Copy)\
                    .then_inc(S("h_ax_out"), 1)
                act.wait_ge(S("h_out"), 1)
                act.activation(h_sq, psum[:, 4:6, :].rearrange("p t (h d) -> p (t h) d", h=HGH), ACT.Square)\
                    .then_inc(S("h_squares"), 1)
                split_u(U_WO + 2)
                for b in range(2):
                    act.wait_ge(S("h_tr"), b + 1)
                    act.activation(act_hi[:, 4 + 2 * b:6 + 2 * b, :], both(psum[:, 6 + b, :]), ACT.Copy)\
                        .then_inc(S("h_hi"), 1)
                for i in range(1, 3):
                    split_u(U_WO + i + 2)

            norm(N_MLA)
            for u in range(2):
                split_u(u)
            mla()
            post_sums(0, "first_half", "used_u", U_MO + 4)
            split_u(U_MO + 5)
            norm(N_F0)
            ffn(0)
            post_sums(1, "first_part", "used_d", FT)
            norm(N_DIFF)
            diff()
            post_sums(2, "first_half", "used_u", U_DO + 4)
            split_u(U_DO + 5)
            norm(N_F1)
            ffn(1)
            post_sums(3, "first_part", "used_d", 2 * FT)
            norm(N_F2)
            ffn(2)
            norm(N_MIX)
            mix()
            split_u(U_WO + 5)
            norm(N_F3)
            ffn(3)
            norm(N_FINAL)

        @block.vector
        def _(dve):
            def split_u(u, b=None):
                if b is not None:
                    dve.wait_ge(S("hi_u_done"), b * 2 + (u + 1))
                    v = [u_slot(x, u) for x in (lo_u, raw_u, hi_u)]
                else:
                    if u >= U_END:
                        return
                    dve.wait_ge(S("hi_u_done"), u + 1)
                    v = [unit_view(x, u) for x in (lo_u, raw_u, hi_u)]
                dve.tensor_tensor(v[0], v[1], v[2].bitcast(F32), ALU.subtract).then_inc(S("lo_u_done"), 1)

            def split_d(d, b=None):
                dve.wait_ge(S("hi_d_done"), d + 1 if b is None else b * 2 + (d + 1))
                dve.tensor_tensor(lo_d[:, d % 2, :], raw_d[:, d % 2, :], hi_d[:, d % 2, :].bitcast(F32),
                                  ALU.subtract).then_inc(S("lo_d_done"), 1)

            def norm(i):
                for t in range(TT):
                    dve.wait_ge(S("rstd"), root_no(f"norm{i}", t))
                    scale = st[:, ST_OF[f"norm{i}"], t:t + 1]
                    if i == N_FINAL:
                        dve.wait_ge(S("gain0"), 16 * 3)
                        dve.scalar_tensor_tensor(normed[:, t, :], resid[:, t, :], scale, gain_row[:, 0, :], ALU.mult,
                                                 ALU.mult).then_inc(S("final"), 1)
                    else:
                        dve.tensor_scalar(normed[:, t, :], resid[:, t, :], scale, None, ALU.mult)\
                            .then_inc(S("normed"), 1)
                if i == N_FINAL:
                    return
                for k in range(KC):
                    dve.wait_ge(S("act_hi"), 8 * i + k + 1)
                    v = V_OF_NORM[i] + k
                    dve.scalar_tensor_tensor(act_lo[:, k, :], psum[:, k % 4, (k // 4) * SEQ:(k // 4) * SEQ + SEQ],
                                             vecs[:, v:v + 1], act_hi[:, k, :].bitcast(F32), ALU.mult,
                                             ALU.subtract).then_inc(S("act_lo"), 1)

            def post(j):
                dve.wait_ge(S(f"gain{j % 2}"), 16 * (j // 2 + 1))
                two = lambda v: v.rearrange("p (a b) -> p a b", a=2)
                for t in range(TT):
                    dve.wait_ge(S("post_sums"), 2 * j + t + 1)
                    dve.tensor_tensor(two(normed[:, t, :]), psum[:, 2 * t:2 * t + 2, :], two(gain_row[:, j % 2, :]),
                                      ALU.mult).then_inc(S("post_gained"), 1)
                    dve.wait_ge(S("post_gained"), 2 * j + t + 1)
                    dve.wait_ge(S("rstd"), root_no(f"post{j}", t))
                    dve.scalar_tensor_tensor(resid[:, t, :], normed[:, t, :], st[:, ST_OF[f"post{j}"], t:t + 1],
                                             resid[:, t, :], ALU.mult, ALU.add).then_inc(S("resid_ready"), 1)

            def add(factor, waits):
                two = lambda v: v.rearrange("p (a b) -> p a b", a=2)
                for t in range(TT):
                    dve.wait_ge(S(waits[t][0]), waits[t][1])
                    dve.scalar_tensor_tensor(two(resid[:, t, :]), psum[:, 2 * t:2 * t + 2, :], factor,
                                             two(resid[:, t, :]), ALU.mult, ALU.add).then_inc(S("resid_ready"), 1)

            def ffn(f):
                def tile(t, slot, n, b=None):
                    at = (lambda x: x) if b is None else (lambda x: b * 2 + x)
                    at2 = (lambda x: x) if b is None else (lambda x: b * 4 + x)
                    g, u = FT * f + t, U_OF_FFN[f] + t
                    if f < 2:
                        for tap, name in ((0, "tap_a"), (2, "tap_b")):
                            for s, buf in ((0, cg), (1, cv)):
                                dve.wait_ge(S("conv_mid" if tap == 0 else "tap_a"), at2(2 * g + s + 1))
                                w = at(V_CW + (f * 3 + tap) * 44 + s * FT + t)
                                o = slice(1, SEQ) if tap == 0 else slice(0, SEQ - 1)
                                x = slice(0, SEQ - 1) if tap == 0 else slice(1, SEQ)
                                dve.scalar_tensor_tensor(buf[0:n, slot, o], psum[0:n, 4 + 2 * slot + s, x],
                                                         vecs[0:n, bass.ds(w, 1)], buf[0:n, slot, o],
                                                         ALU.mult, ALU.add).then_inc(S(name), 1)
                    split_u(u + 2, b)
                    dve.wait_ge(S("gated"), at(g + 1))
                    if f < 2:
                        dve.wait_ge(S("tap_b"), at2(2 * g + 2))
                        val = cv[0:n, slot, :]
                    else:
                        dve.wait_ge(S("used_u"), at(u + 1))
                        val = psum[0:n, 5 + 2 * slot, 0:SEQ]
                    dve.tensor_tensor(hf[0:n, slot, :], gg[0:n, slot, :], val, ALU.mult).then_inc(S("hidden"), 1)
                    if b is not None or g >= 2:
                        dve.wait_ge(S("used_d"), at(g - 1))
                    dve.tensor_tensor(hid_hi[0:n, slot, :], gg[0:n, slot, :], val, ALU.mult)\
                        .then_inc(S("hid_hi_done"), 1)
                    dve.wait_ge(S("hidden"), at(g + 1))
                    dve.wait_ge(S("hid_hi_done"), at(g + 1))
                    dve.tensor_tensor(hid_lo[0:n, slot, :], hf[0:n, slot, :], hid_hi[0:n, slot, :].bitcast(F32),
                                      ALU.subtract).then_inc(S("hid_lo_done"), 1)
                    if b is not None or t + 1 < FT:
                        split_d(g + 1, b)

                split_d(FT * f)
                tile(0, 0, P)
                tile(1, 1, P)
                with dve.Fori(0, LOOPED) as b:
                    tile(2, 0, P, b)
                    tile(3, 1, P, b)
                tile(20, 0, P)
                tile(21, 1, width(f, 21))

            def mla():
                for u in range(2, 4):
                    split_u(u)
                ch = Chain(dve, S("dve_chain_mla"))
                dve.wait_ge(S("latent_sums"), 1)
                dve.wait_ge(S("rope_in"), 32)
                raw = psum[:, 6:8, KVL:KVL + ROPE]
                ch.put(dve.tensor_tensor(kr3[:, 0], raw, ropek[:, 0], ALU.mult))
                ch.put(dve.tensor_tensor(kr3[:, 1, :, 0:32], raw[:, :, 32:64], ropek[:, 1, :, 32:64], ALU.mult))
                ch.put(dve.tensor_tensor(kr3[:, 1, :, 32:64], raw[:, :, 0:32], ropek[:, 1, :, 0:32], ALU.mult))
                ch.wait()
                dve.tensor_tensor(kr3[:, 2], kr3[:, 0], kr3[:, 1], ALU.add).then_inc(S("k_roped"), 1)
                dve.wait_ge(S("rstd"), root_no("latents"))
                for t in range(TT):
                    dve.tensor_scalar(cq[:, t, :], psum[:, 4 + t, 0:QL], st[:, ST_OF["latents"], t:t + 1], None, ALU.mult)\
                        .then_inc(S("latents"), 1)
                for t in range(TT):
                    dve.tensor_scalar(ck[:, t, :], psum[:, 6 + t, 0:KVL], st[:, ST_OF["latents"], 2 + t:3 + t], None, ALU.mult)\
                        .then_inc(S("latents"), 1)
                for u in range(4, 6):
                    split_u(u)
                dve.wait_ge(S("latent_hi"), 5)
                for c in range(5):
                    b, o = (c // 2, c % 2) if c < 3 else (2, c - 3)
                    v = V_QN + c if c < 3 else V_KVN + c - 3
                    dve.scalar_tensor_tensor(act_lo[:, c, :], psum[:, b, o * SEQ:o * SEQ + SEQ], vecs[:, v:v + 1],
                                             act_hi[:, c, :].bitcast(F32), ALU.mult, ALU.subtract)\
                        .then_inc(S("latent_lo"), 1)
                t1, t2 = qr2[:, 0], qr2[:, 1]
                both = lambda v: v.unsqueeze(1).broadcast_to([v.shape[0], 2, SEQ])
                for i in range(4):
                    dve.wait_ge(S("used_u"), U_UQ + i + 1)
                    if i:
                        dve.wait_ge(S("m_qr_out"), i)
                    raw = psum[0:ROPE, 4 + 2 * (i % 2) + 1, :].rearrange("p (h t) -> p h t", h=2)
                    ch.put(dve.tensor_tensor(t1, raw, both(ropeq[:, 0, :]), ALU.mult))
                    ch.put(dve.tensor_tensor(t2[0:32], raw[32:64], both(ropeq[32:64, 1, :]), ALU.mult))
                    dve.tensor_tensor(t2[32:64], raw[0:32], both(ropeq[0:32, 1, :]), ALU.mult)\
                        .then_inc(S("m_qr_read"), 1)
                    ch.wait()
                    dve.wait_ge(S("m_qr_read"), i + 1)
                    dve.tensor_tensor(m_qr[:, 2 * i:2 * i + 2, :], t1, t2, ALU.add).then_inc(S("m_qr_out"), 1)
                    split_u(U_UQ + i + 2)
                for i in range(2):
                    dve.wait_ge(S("used_u"), U_UKV + i + 1)
                    dve.tensor_copy(m_v[:, :, 4 * i:4 * i + 4, :], psum[:, 2:4, :].rearrange("p t (h d) -> p t h d", h=4))\
                        .then_inc(S("m_v_out"), 1)
                    split_u(U_UKV + i + 2)
                for i in range(H + 3):
                    if i < H:
                        dve.wait_ge(S("m_scores"), i + 1)
                        ch.link(dve.tensor_reduce(soft[:, i, 0, 0:2], psum[:, i % 3, :].rearrange("p (t k) -> p t k", t=2),
                                                  AX, ALU.max))
                        dve.tensor_scalar(soft[:, i, 1, 0:2], soft[:, i, 0, 0:2], -M_SCALE, None, ALU.mult)\
                            .then_inc(S("m_bias"), 1)
                    if 0 <= i - 1 < H:
                        h = i - 1
                        dve.wait_ge(S("m_exp"), 2 * h + 2)
                        ch.link(dve.reciprocal(soft[:, h, 3, 0:2], soft[:, h, 2, 0:2]))
                        for t in range(TT):
                            dve.tensor_scalar(m_p[:, h % 3, t, :], m_p[:, h % 3, t, :], soft[:, h, 3, t:t + 1], None,
                                              ALU.mult).then_inc(S("m_probs"), 1)
                    if i >= 3:
                        h = i - 3
                        dve.wait_ge(S("m_o_hi"), h + 1)
                        dve.tensor_tensor(act_lo[:, h, :], psum[:, 5 + h % 2, 0:SEQ], act_hi[:, h, :].bitcast(F32),
                                          ALU.subtract).then_inc(S("m_o_lo"), 1)
                for i in range(3):
                    split_u(U_MO + i + 2)

            def diff():
                ch = Chain(dve, S("dve_chain_diff"))
                dve.wait_ge(S("tables_in"), 16 * 9)
                pairs = lam[:, 0:256].rearrange("p (a b d) -> p a b d", a=2, b=2)
                prod = junk_d[:].rearrange("p (a d) -> p a d", a=2)
                ch.link(dve.tensor_tensor(prod, pairs[:, :, 0], pairs[:, :, 1], ALU.mult))
                dve.tensor_reduce(lam[:, 256:258], prod, AX, ALU.add).then_inc(S("lam_sums"), 1)
                for i in range(8):
                    split_u(U_QK + i + 2)
                dve.wait_ge(S("lam_exp"), 1)
                ch.link(dve.tensor_tensor(lam[:, 260:261], lam[:, 259:260], lam[:, 258:259], ALU.subtract))
                ch.link(dve.tensor_scalar(lam[:, 260:261], lam[:, 260:261], -LAM_INIT, None, ALU.add))
                dve.tensor_scalar(lam[:, 261:262], vecs[:, V_SUB:V_SUB + 1], 1.0 - LAM_INIT, None, ALU.mult)\
                    .then_inc(S("d_gain"), 1)

                def maxima(h):
                    dve.wait_ge(S("d_scores"), h + 1)
                    b = 4 + 2 * (h % 2)
                    ch.link(dve.tensor_reduce(soft[:, h, 0, 0:4].rearrange("p (j t) -> p j t", j=2),
                                              psum[:, b:b + 2, :].rearrange("p j (t k) -> p j t k", t=2), AX, ALU.max))
                    dve.tensor_scalar(soft[:, h, 1, 0:4], soft[:, h, 0, 0:4], -D_SCALE, None, ALU.mult)\
                        .then_inc(S("d_bias"), 1)

                def maps(h):
                    dve.wait_ge(S("d_exp"), 4 * h + 4)
                    ch.link(dve.reciprocal(soft[:, h, 3, 0:4], soft[:, h, 2, 0:4]))
                    ch.link(dve.scalar_tensor_tensor(soft[:, h, 3, 2:4], soft[:, h, 3, 2:4], lam[:, 260:261],
                                                     soft[:, h, 2, 0:2], ALU.mult, ALU.mult))
                    if h >= 2:
                        dve.wait_ge(S("d_turned"), h - 1)
                    for t in range(TT):
                        dve.scalar_tensor_tensor(d_a[:, h % 2, t, :], d_x[:, h % 3, 2 + t, :], soft[:, h, 3, 2 + t:3 + t],
                                                 d_x[:, h % 3, t, :], ALU.mult, ALU.add).then_inc(S("d_maps"), 1)

                def heads_sums(g):
                    for t in range(TT):
                        sq = d_sq[:, t]
                        heads = d_o[:, t, 4 * g:4 * g + 4, :]
                        dve.wait_ge(S("d_o_out"), 8 * g + 8)
                        if g:
                            dve.wait_ge(S("d_sums"), 4 * t + 4)
                        ch.link(dve.tensor_tensor(sq, heads, heads, ALU.mult))
                        c = 8 * g + 4 * t
                        dve.tensor_reduce(st[:, ST_OF["heads"], c:c + 4], sq, AX, ALU.add).then_inc(S("d_sums"), 4)

                def heads_normed(g):
                    dve.wait_ge(S("rstd"), root_no("heads", g))
                    for t in range(TT):
                        c = 8 * g + 4 * t
                        heads = d_o[:, t, 4 * g:4 * g + 4, :]
                        dve.tensor_tensor(heads, heads, st[:, ST_OF["heads"], c:c + 4].unsqueeze(2)
                                          .broadcast_to([P, 4, P]), ALU.mult).then_inc(S("d_normed"), 1)

                def heads_lo(g):
                    for b in (2 * g, 2 * g + 1):
                        dve.wait_ge(S("d_hi"), b + 1)
                        dve.scalar_tensor_tensor(act_lo[:, 2 * b:2 * b + 2, :],
                                                 psum[:, 4 + b, :].rearrange("p (k t) -> p k t", k=2), lam[:, 261:262],
                                                 act_hi[:, 2 * b:2 * b + 2, :].bitcast(F32), ALU.mult, ALU.subtract)\
                            .then_inc(S("d_lo"), 1)

                split_u(U_V + 2)
                maxima(0)
                split_u(U_V + 3)
                maxima(1)
                split_u(U_V + 4)
                for i in range(H):
                    maps(i)
                    if i + 2 < H:
                        maxima(i + 2)
                    if i == 1:
                        split_u(U_V + 5)
                    if i == 5:
                        heads_sums(0)
                    if i == 6:
                        heads_normed(0)
                heads_lo(0)
                heads_sums(1)
                heads_normed(1)
                split_u(U_DO + 2)
                heads_lo(1)
                split_u(U_DO + 3)
                split_u(U_DO + 4)

            def mix():
                ch = Chain(dve, S("dve_chain_mix"))
                both = lambda v: v.rearrange("p (h t) -> p h t", h=2)
                flat = lambda v: v.rearrange("p a b -> p (a b)")
                lb = vecs[:, V_LB:V_LB + 4]
                dve.tensor_tensor(bound[:, 0, :], lb, lb, ALU.subtract).then_inc(S("lb_shifted"), 1)
                for u in (U_NQ + 2, U_NQ + 3, U_NC + 2):
                    split_u(u)
                dve.wait_ge(S("used_u"), U_NC + 1)
                for v in range(2):
                    for g in range(2):
                        src = psum[g * HD:g * HD + HD, 6, v * SEQ:v * SEQ + SEQ].rearrange("p (c i l) -> p l i c", i=8, l=2)
                        for l in range(2):
                            r = slice(l * HD, l * HD + HD)
                            for half_block in range(2):
                                i0 = 8 * half_block
                                emb = vecs[r, V_POSK + 16 * v + i0:V_POSK + 16 * v + i0 + 8]
                                dve.tensor_tensor(c_x[r, v, i0:i0 + 8, g * NB:g * NB + NB],
                                                  src[:, l, :, half_block:half_block + NB],
                                                  emb.unsqueeze(2).broadcast_to([HD, 8, NB]), ALU.add)\
                                    .then_inc(S("c_x_done"), 1)
                for u in (U_NK + 2, U_NV + 2, U_NV + 3):
                    split_u(u)
                dve.wait_ge(S("n_gates"), 1)
                for i, dst in enumerate((n_vs, n_vw)):
                    dve.tensor_copy(dst, psum[:, 2:4, P * i:P * i + P]).then_inc(S("n_v_out"), 1)
                cmp_gate = n_g.rearrange("p t (h b) -> p t h b", b=3)[:, :, :, 0]
                ch.put(dve.tensor_tensor(cmp_gate, cmp_gate, crows[:].unsqueeze(2).broadcast_to([P, TT, H]), ALU.mult))
                for v in range(2):
                    dve.wait_ge(S("c_hi"), v + 1)
                    dve.tensor_tensor(c_xlo[:, v], c_x[:, v], c_xhi[:, v].bitcast(F32), ALU.subtract)\
                        .then_inc(S("c_lo"), 1)
                for u in range(U_HQ + 2, U_HI + 3):
                    split_u(u)
                dve.wait_ge(S("lb_exp"), 1)
                ch.link(dve.reciprocal(bound[:, 2, :], bound[:, 1, :]))
                ch.link(dve.tensor_tensor(bound[:, 3, :], bound[:, 1, :], bound[:, 2, :], ALU.mult))
                ch.link(dve.tensor_tensor(bound[:, 4, :], bound[:, 3, :], bound[:, 3, :], ALU.subtract))
                ch.link(dve.tensor_scalar(bound[:, 5, :], bound[:, 4, :], -1.0, 1.0, ALU.mult, ALU.add))
                for h in range(HGH):
                    if h == 2:
                        split_u(U_HI + 3)
                    dve.wait_ge(S("h_fk_out"), 2 * (h // 2) + 2)
                    ch.put(dve.tensor_scalar(h_f[:, h, :], h_f[:, h, :], bound[:, 5, h:h + 1], bound[:, 4, h:h + 1],
                                             ALU.mult, ALU.add))
                    ch.put(dve.tensor_scalar(h_k[:, h, :], h_k[:, h, :], bound[:, 5, h:h + 1], None, ALU.mult))
                split_u(U_HI + 4)
                ch.wait()
                dve.tensor_scalar(h_f, h_f, 1e-30, None, ALU.max).then_inc(S("h_ready"), 1)
                for t in range(TT):
                    dve.wait_ge(S("used_u"), U_HI + 4)
                    dve.tensor_copy(h_v[:, t, :], psum[:, 2 * t, :]).then_inc(S("h_v_out"), 1)
                gate = h_g.rearrange("p t (h d) -> p (t h) d", h=HGH)

                def take_level(l, t):
                    dve.wait_ge(S("h_level"), 2 * l + t + 1)
                    if l:
                        dve.wait_ge(S("h_a_done"), 2 * l + t - 1)
                    elif t == 0:
                        dve.wait_ge(S("h_a_zero"), 1)
                    dve.copy_predicated(h_a[:, 4 * t:4 * t + 4, :],
                                        masks[:, l:l + 1, :].bitcast(U32).broadcast_to([P, 4, P]),
                                        psum[:, 3, :].rearrange("p (b c) -> p b c", b=4)).then_inc(S("h_a_done"), 1)

                def decay_q(l):
                    if l == 0:
                        dve.tensor_tensor(h_q, h_q, h_f, ALU.mult).then_inc(S("h_q_upd"), 1)
                        return
                    m = 1 << (l - 1)
                    e = decay_of(m).rearrange("p (n s) -> p n s", s=2)
                    right = flat(h_q).rearrange("p (n s m) -> p n s m", s=2, m=m)[:, :, 1, :]
                    dve.wait_ge(S("h_q_upd"), l)
                    if l >= 2:
                        dve.wait_ge(S("h_e"), l - 1)
                    dve.tensor_tensor(right, right, e[:, :, 0:1].broadcast_to([P, 512 // m, m]), ALU.mult)\
                        .then_inc(S("h_q_upd"), 1)
                    if 2 * m <= 64:
                        dve.tensor_tensor(decay_of(2 * m), e[:, :, 0], e[:, :, 1], ALU.mult).then_inc(S("h_e"), 1)

                dve.wait_ge(S("h_ready"), 1)
                for i in range(H + 2):
                    if i < H:
                        dve.wait_ge(S("n_scores"), i + 1)
                        b = 4 + 2 * (i % 2)
                        mx = soft[:, i, 0, 2:6].rearrange("p (b t) -> p b t", b=2)
                        ch.put(dve.tensor_reduce(mx[:, :, 0:1], psum[:, b:b + 2, 0:P], AX, ALU.max))
                        ch.put(dve.tensor_reduce(mx[:, :, 1:2], psum[:, b:b + 2, P:3 * P], AX, ALU.max))
                        ch.link(dve.tensor_reduce(soft[:, i, 0, 0:2], psum[:, b, 384:414]
                                                  .rearrange("p (m k) -> p m k", m=2), AX, ALU.max))
                        dve.tensor_scalar(soft[:, i, 1, 0:6], soft[:, i, 0, 0:6], -D_SCALE, None, ALU.mult)\
                            .then_inc(S("n_bias"), 1)
                    if i == H:
                        split_u(U_HI + 5)
                    if i < 8:
                        take_level(i, 0)
                    if 1 <= i <= H:
                        h = i - 1
                        dve.wait_ge(S("n_exp"), 6 * h + 6)
                        ch.link(dve.reciprocal(soft[:, h, 3, 0:6], soft[:, h, 2, 0:6]))
                        r = soft[:, h, 3, 0:6].rearrange("p (b t) -> p b t", b=3)
                        gates = n_g[:, :, 3 * h:3 * h + 3].rearrange("p t b -> p b t")
                        ch.link(dve.tensor_tensor(r, r, gates, ALU.mult))
                        x = n_x[:, h % 2, :]
                        for m, (at, n) in enumerate(N_PARTS):
                            dve.tensor_scalar(x[:, at:at + n], x[:, at:at + n], soft[:, h, 3, m:m + 1], None, ALU.mult)\
                                .then_inc(S("n_probs"), 1)
                    if i < 8:
                        take_level(i, 1)
                        decay_q(i)
                    if 1 <= i <= H:
                        dve.wait_ge(S("n_turned"), h + 1)
                        if h >= 2:
                            dve.wait_ge(S("n_values"), h - 1)
                        dve.tensor_copy(n_pt[:, h % 2, 384:768], psum[:, 1, 0:384]).then_inc(S("n_pt_b"), 1)
                        dve.tensor_copy(n_pt[0:NB, h % 2, 896:1024], psum[0:NB, 1, 384:512]).then_inc(S("n_pt_b"), 1)
                    if i >= 2 and i % 2:
                        j = (i - 2) // 2
                        dve.wait_ge(S("n_o_hi"), j + 1)
                        dve.tensor_tensor(act_lo[:, j, :], psum[:, 2, 0:SEQ], act_hi[:, j, :].bitcast(F32),
                                          ALU.subtract).then_inc(S("n_o_lo"), 1)
                dve.wait_ge(S("h_g_gained"), 1)
                dve.wait_ge(S("h_squares"), 1)
                dve.tensor_reduce(st[:, ST_OF["hgrn"], 0:8], h_sq, AX, ALU.add).then_inc(S("h_sums"), 1)
                dve.wait_ge(S("rstd"), root_no("hgrn"))
                o = h_o.rearrange("p t h d -> p (t h) d")
                for t in range(TT):
                    s = slice(4 * t, 4 * t + 4)
                    ch.put(dve.tensor_tensor(o[:, s], psum[:, 4 + t, :].rearrange("p (h d) -> p h d", h=HGH),
                                             st[:, ST_OF["hgrn"], s].unsqueeze(2).broadcast_to([P, 4, P]), ALU.mult))
                for t in range(TT):
                    s = slice(4 * t, 4 * t + 4)
                    ch.wait(ch.n - 1 + t)
                    dve.tensor_tensor(o[:, s], o[:, s], gate[:, s], ALU.mult).then_inc(S("h_gated"), 1)
                split_u(U_WO + 2)
                for b in range(2):
                    dve.wait_ge(S("h_hi"), b + 1)
                    dve.tensor_tensor(act_lo[:, 4 + 2 * b:6 + 2 * b, :], both(psum[:, 6 + b, :]),
                                      act_hi[:, 4 + 2 * b:6 + 2 * b, :].bitcast(F32), ALU.subtract).then_inc(S("h_lo"), 1)
                for i in range(1, 3):
                    split_u(U_WO + i + 2)

            dve.memset(zeros[:], 0.0).then_inc(S("zeros_set"), 1)
            norm(N_MLA)
            for u in range(2):
                split_u(u)
            mla()
            post(0)
            norm(N_F0)
            split_u(U_MO + 5)
            ffn(0)
            post(1)
            norm(N_DIFF)
            diff()
            post(2)
            norm(N_F1)
            split_u(U_DO + 5)
            ffn(1)
            post(3)
            norm(N_F2)
            ffn(2)
            add(0.5, [("first_part", 6), ("used_d", 3 * FT)])
            norm(N_MIX)
            mix()
            add(1.0, [("first_half", 3), ("used_u", U_WO + 4)])
            norm(N_F3)
            split_u(U_WO + 5)
            ffn(3)
            add(0.5, [("first_part", 8), ("used_d", 4 * FT)])
            norm(N_FINAL)


_INS = ["x", "norm_g", "ffn_w_up", "ffn_conv_w", "ffn_conv_b", "ffn_w_down", "mla_w_dq", "mla_q_norm_g", "mla_w_uq",
        "mla_w_dkv", "mla_kv_norm_g", "mla_w_ukv", "mla_w_o", "diff_w_qkv", "diff_lambda", "diff_subln_g", "diff_w_o",
        "ffn1_norm_2", "ffn1_w_gu_2", "ffn1_w_down_2", "mix_norm_2", "w_in_2", "cmp_pos_k_2", "cmp_pos_v_2",
        "cmp_k_w1_2", "cmp_k_w2_2", "cmp_v_w1_2", "cmp_v_w2_2", "hgrn_lower_bound_2", "hgrn_out_norm_2", "w_out_2",
        "ffn2_norm_2", "ffn2_w_gu_2", "ffn2_w_down_2", "final_norm_2"]


def kernel(**inputs):
    import concourse.bacc as bacc
    from concourse.bass_utils import run_bass_kernel_spmd

    nc = bacc.Bacc("TRN2", target_bir_lowering=False, num_devices=1)
    arrays, aps = {}, {}

    def give(name, array):
        arrays[f"in_{name}"] = array
        aps[name] = nc.dram_tensor(f"in_{name}", array.shape, mybir.dt.from_np(array.dtype), kind="ExternalInput").ap()

    for name in _INS:
        x = np.ascontiguousarray(inputs[name])
        give(name, x)
    for name, table in constants().items():
        give(name, np.ascontiguousarray(table))
    out = nc.dram_tensor("out_0", (1, SEQ, D), F32, kind="ExternalOutput").ap()
    program(nc, aps, out)
    r = run_bass_kernel_spmd(nc, [arrays], core_ids=[0])
    return r.results[0]["out_0"]
```

```python
import math
from contextlib import ExitStack

import numpy as np

import concourse.bass as bass
from concourse import mybir

F32 = mybir.dt.float32
F32R = mybir.dt.float32r
BF16 = mybir.dt.bfloat16
U32 = mybir.dt.uint32
ACT = mybir.ActivationFunctionType
ALU = mybir.AluOpType
AX = mybir.AxisListType.X

P = 128
SEQ = 256
TT = SEQ // P
D = 1024
KC = D // P
EPS = 1e-6
BANK = 512

H = 8
NOPE, ROPE, VD = 128, 64, 128
QL, KVL = 384, 256
F1, F2 = 2816, 2752
FT = 22
LAM_INIT = 0.8 - 0.6 * math.exp(-0.3)
HD = 64
CMP = 32
STRIDE = 16
NB = SEQ // STRIDE - 1
HGH = 4
MASKED = 1e30

V_NORM = 0
V_FFN1 = V_NORM + 64
V_MIX = V_FFN1 + 8
V_FFN2 = V_MIX + 8
V_QN = V_FFN2 + 8
V_KVN = V_QN + 3
V_LB = V_KVN + 2
V_SUB = V_LB + 4
V_POSK = V_SUB + 1
V_POSV = V_POSK + 16
V_CW = V_POSV + 16
V_CB = V_CW + 264
V_ALL = V_CB + 88

C_Q, C_KC, C_VC, C_KS, C_VS, C_KW, C_VW, C_GL = 0, 512, 640, 768, 896, 1024, 1152, 1280
C_HQ, C_HF, C_HI = 1304, 1816, 2328

U_DQ = 0
U_DKV = U_DQ + 2
U_UQ = U_DKV + 2
U_UKV = U_UQ + 4
U_MO = U_UKV + 2
U_F0 = U_MO + 4
U_QK = U_F0 + FT
U_V = U_QK + 8
U_DO = U_V + 4
U_F1 = U_DO + 4
U_F2 = U_F1 + FT
U_NQ = U_F2 + FT
U_NC = U_NQ + 2
U_NK = U_NC + 1
U_NV = U_NK + 1
U_H = U_NV + 2
U_HI = U_H + 8
U_WO = U_HI + 4
U_F3 = U_WO + 4
U_END = U_F3 + FT
U_OF_FFN = [U_F0, U_F1, U_F2, U_F3]
LOOPED = 9

N_MLA, N_F0, N_DIFF, N_F1, N_F2, N_MIX, N_F3, N_FINAL = range(8)


def constants():
    pos = np.arange(SEQ, dtype=np.float32)
    q = pos.reshape(TT, P).T[:, :, None]
    dist = np.abs(q - pos[None, None, :]).astype(np.float32)
    signed = q - pos[None, None, :]
    causal = np.where(signed >= 0, signed, MASKED).astype(np.float32)
    causal = np.concatenate([causal[:, 0, :P], causal[:, 1, :]], axis=1)
    ends = (np.arange(NB) * STRIDE + CMP - 1).astype(np.float32)
    cmp = q - ends[None, None, :]
    cmp = np.where(cmp >= 0, cmp, MASKED).astype(np.float32)
    rows = (q[:, :, 0] >= CMP - 1).astype(np.float32)
    inv = (np.float32(10000.0) ** (-np.arange(0, ROPE, 2, dtype=np.float32) / np.float32(ROPE))).astype(np.float32)
    ang = pos[:, None] * inv[None, :]
    cos, sin = np.cos(ang).astype(np.float32), np.sin(ang).astype(np.float32)
    cos2 = np.concatenate([cos, cos], 1)
    sin2 = np.concatenate([sin, -sin], 1)
    tok = lambda a: np.ascontiguousarray(a.reshape(TT, P, -1).transpose(1, 0, 2))
    s = np.arange(P)[:, None]
    t = np.arange(P)[None, :]
    masks = np.zeros((P, 8, P), np.float32)
    masks[:, 0, :] = s == t
    for i in range(7):
        m = 1 << i
        masks[:, i + 1, :] = (s // (2 * m) == t // (2 * m)) & (s % (2 * m) < m) & (t % (2 * m) >= m)
    return {
        "ident": np.eye(P, dtype=np.float32), "dist": dist.reshape(P, -1), "causal": causal,
        "cdist": cmp.reshape(P, -1), "crows": rows,
        "ropek": np.concatenate([tok(cos2), tok(sin2)], 1).reshape(P, -1),
        "ropeq": np.concatenate([cos2.T, sin2.T], 1), "masks": masks.reshape(P, -1),
    }


ROOTS = ([("norm0", 0), ("norm0", 1), ("latents", 0), ("post0", 0), ("post0", 1), ("norm1", 0), ("norm1", 1),
          ("post1", 0), ("post1", 1), ("norm2", 0), ("norm2", 1), ("heads", 0), ("heads", 1), ("post2", 0),
          ("post2", 1), ("norm3", 0), ("norm3", 1), ("post3", 0), ("post3", 1), ("norm4", 0), ("norm4", 1),
          ("norm5", 0), ("norm5", 1), ("hgrn", 0), ("norm6", 0), ("norm6", 1), ("norm7", 0), ("norm7", 1)])
ST_OF = {name: i for i, name in enumerate(dict.fromkeys(n for n, _ in ROOTS))}


def root_no(name, part=0):
    return ROOTS.index((name, part)) + 1


WARM = [(0, 0, 0)] + 4 * [(19, 3, 1)] + 2 * [(12, 3, 1)]
WARM_DIFF = 6
FIRST = [0, U_F0, U_QK, U_F1, U_F2, U_NQ, U_F3]
HALVED = sorted(FIRST + list(range(U_NV, U_HI + 1)))
SECOND = [1, U_F0 + 1, U_QK + 1, U_F1 + 1, U_F2 + 1, U_NQ + 1, U_F3 + 1]
V_OF_NORM = [V_NORM, V_NORM + 16, V_NORM + 32, V_NORM + 48, V_FFN1, V_MIX, V_FFN2]
M_SCALE = (NOPE + ROPE) ** -0.5
D_SCALE = HD ** -0.5
N_PARTS = [(768, NB), (768 + NB, NB), (0, P), (P, 2 * P), (3 * P, P), (4 * P, 2 * P)]
N_DVE = 4


class Chain:

    def __init__(self, eng, sem):
        self.eng, self.sem, self.n = eng, sem, 0

    def put(self, ins):
        ins.then_inc(self.sem, 1)
        self.n += 1
        return self.n

    def wait(self, n=None):
        self.eng.wait_ge(self.sem, self.n if n is None else n)

    def link(self, ins):
        self.put(ins)
        self.wait()


def program(nc, a, out):
    ctx = ExitStack()
    sems = {}

    def S(name):
        if name not in sems:
            sems[name] = ctx.enter_context(nc.semaphore(name))
        return sems[name]

    def sb(name, shape, dt=F32):
        return ctx.enter_context(nc.sbuf_tensor(name, shape, dt))

    with ctx:
        psum = ctx.enter_context(nc.psum_tensor("psum", [P, 8, BANK], F32))

        resid = sb("resid", [P, TT, D])
        normed = sb("normed", [P, TT, D])
        act_hi = sb("act_hi", [P, KC, SEQ], F32R)
        act_lo = sb("act_lo", [P, KC, SEQ], F32R)
        raw_u = sb("raw_u", [P, 2, 2048])
        hi_u = sb("hi_u", [P, 2, 2048], F32R)
        lo_u = sb("lo_u", [P, 2, 2048], F32R)
        raw_d = sb("raw_d", [P, 2, 1024])
        hi_d = sb("hi_d", [P, 2, 1024], F32R)
        lo_d = sb("lo_d", [P, 2, 1024], F32R)
        hid_hi = sb("hid_hi", [P, 2, SEQ], F32R)
        hid_lo = sb("hid_lo", [P, 2, SEQ], F32R)
        gain_row = sb("gain_row", [P, 2, D])
        vecs = sb("vecs", [P, V_ALL])
        ident = sb("ident", [P, P])
        zeros = sb("zeros", [P, BANK], BF16)
        half = sb("half", [P, 16])
        st = sb("st", [P, len(ST_OF), 16])
        junk = sb("junk", [P, D])
        soft = sb("soft", [P, 8, 4, 8])
        lam = sb("lam", [P, 272])
        junk_d = sb("junk_d", [P, P])
        bound = sb("bound", [P, 6, 4])
        masks = sb("masks", [P, 8, P])
        cdist = sb("cdist", [P, TT, NB])
        crows = sb("crows", [P, TT])
        slopes = sb("slopes", [P, H, P], BF16)
        dist_b = sb("dist_b", [P, TT, SEQ], BF16)
        causal_b = sb("causal_b", [P, 3 * P + TT * NB], BF16)
        w2k = sb("w2k", [P, 2, HD])
        w2v = sb("w2v", [P, 2, HD])
        hgain = sb("hgain", [P, P])
        dist = sb("dist", [P, TT, SEQ])
        causal = sb("causal", [P, 3, P])
        arena = sb("arena", [P, 12288])

        def ar(at, *shape, p=P):
            n = int(np.prod(shape))
            v = arena[0:p, at:at + n]
            if len(shape) == 2:
                v = v.rearrange("p (a b) -> p a b", a=shape[0])
            if len(shape) == 3:
                v = v.rearrange("p (a b c) -> p a b c", a=shape[0], b=shape[1])
            return v

        vrows = ar(0, 7, P)
        VROWS = [(V_NORM, 64), (V_FFN1, 34), (V_POSK, 32), (V_CW, 88), (V_CW + 88, 88), (V_CW + 176, 88), (V_CB, 88)]
        cg, cv, gg, hf = (ar(512 * i, 2, SEQ) for i in range(4))

        def u_slot(t, u):
            return t[:, u % 2, :]

        def cols(w, c0, n):
            return w[:, c0:c0 + n].rearrange("(k p) n -> p k n", p=P)

        def rows(w, k0, n):
            return w[k0 * P:(k0 + n) * P, :].rearrange("(k p) n -> p k n", p=P)

        w_up, w_down = a["ffn_w_up"], a["ffn_w_down"]
        gu = [None, None, a["ffn1_w_gu_2"][0], a["ffn2_w_gu_2"][0]]
        dn = [w_down[0], w_down[1], a["ffn1_w_down_2"][0], a["ffn2_w_down_2"][0]]
        gu[0], gu[1] = w_up[0], w_up[1]
        FW = [F1, F1, F2, F2]
        units = {}
        w_in = a["w_in_2"][0]
        for i in range(2):
            units[U_DQ + i] = rows(a["mla_w_dq"][0], 4 * i, 4)
            units[U_DKV + i] = rows(a["mla_w_dkv"][0], 4 * i, 4)
            units[U_UKV + i] = cols(a["mla_w_ukv"][0], 1024 * i, 1024)
            units[U_NQ + i] = cols(w_in, C_Q + 256 * i, 256)
        for i in range(4):
            units[U_UQ + i] = cols(a["mla_w_uq"][0], 384 * i, 384)
            units[U_MO + i] = rows(a["mla_w_o"][0], 2 * i, 2)
            units[U_V + i] = rows(a["diff_w_qkv"][0][:, 2048:3072], 2 * i, 2)
            units[U_DO + i] = rows(a["diff_w_o"][0], 2 * i, 2)
            units[U_HI + i] = rows(w_in[:, C_HI:C_HI + 1024], 2 * i, 2)
            units[U_WO + i] = rows(a["w_out_2"][0], 2 * i, 2)
        for i in range(8):
            units[U_H + i] = (cols(w_in, (C_HQ, C_HF)[i // 4] + P * (i % 4), P),
                              rows(a[("cmp_k_w1_2", "cmp_v_w1_2")[i // 4]][0], 4 * (i % 4), 4))
            units[U_QK + i] = cols(a["diff_w_qkv"][0], 256 * i, 256)
        units[U_NC] = cols(w_in, C_KC, 256)
        units[U_NK] = [cols(w_in, C_KS, P), cols(w_in, C_KW, P)]
        for i in range(2):
            units[U_NV + i] = [cols(w_in, c, n)[:, 4 * i:4 * i + 4] for c, n in ((C_VS, P), (C_VW, P + 24))]

        def width(f, t):
            return min(P, FW[f] - t * P) if isinstance(t, int) else P

        def unit_view(t, u):
            if isinstance(u, int) and u in units:
                if isinstance(units[u], tuple):
                    return u_slot(t, u).rearrange("p (k n) -> p k n", k=2)
                parts = units[u] if isinstance(units[u], list) else [units[u]]
                k, n = parts[0].shape[1], sum(p.shape[2] for p in parts)
                return u_slot(t, u)[:, 0:k * n].rearrange("p (k n) -> p k n", k=k)
            return u_slot(t, u)

        def pair_views(t, u):
            v = unit_view(t, u)
            return v[:, 0, :].rearrange("p (k n) -> p k n", k=KC), v[:, 1, :].rearrange("p (k n) -> p k n", k=4)

        def up_view(t, slot, s, n):
            return t[:, slot, 1024 * s:1024 * s + 1024].rearrange("p (k n) -> p k n", k=KC)[:, :, 0:n]

        m_q = ar(0, H, SEQ)
        m_qr = ar(2048, H, SEQ, p=ROPE)
        m_k = ar(4096, H, SEQ)
        m_v = ar(6144, TT, H, VD)
        m_kr = ar(8192, SEQ, p=ROPE)
        ropek = ar(8448, 2, TT, ROPE)
        ropeq = ar(8704, 2, SEQ, p=ROPE)
        m_p = ar(9216, 3, TT, SEQ)
        m_pt = ar(10752, 2, 2, SEQ)
        cq = normed[:].rearrange("p a b -> p (a b)")[:, 0:768].rearrange("p (t n) -> p t n", t=TT)
        ck = normed[:].rearrange("p a b -> p (a b)")[:, 768:1280].rearrange("p (t n) -> p t n", t=TT)
        kr3 = normed[:].rearrange("p a b -> p (a b)")[:, 1280:1664].rearrange("p (a t n) -> p a t n", a=3, t=TT)
        qr2 = masks[0:ROPE, :, :].rearrange("p (a b) t -> p a (b t)", a=2).rearrange("p a (b t) -> p a b t", b=2)
        d_q = ar(0, H, SEQ)
        d_k = ar(2048, H, SEQ)
        d_v = ar(4096, TT, D)
        d_x = ar(6144, 3, 4, SEQ)
        d_a = ar(9216, 2, TT, SEQ)
        d_at = ar(10240, 2, 2, SEQ)
        d_o = normed[:].rearrange("p t (h d) -> p t h d", h=H)
        d_sq = hi_d[:].rearrange("p a (b d) -> p (a b) d", d=P)
        n_q = ar(0, 4, SEQ)
        n_k = ar(1024, 4, SEQ)
        n_vs = ar(2048, TT, P)
        n_vw = ar(2304, TT, P)
        n_g = ar(2560, TT, 24)
        h_q = ar(2624, HGH, SEQ)
        h_f = ar(3648, HGH, SEQ)
        h_k = ar(4672, HGH, SEQ)
        h_v = ar(5696, TT, 512)
        h_g = ar(6720, TT, 512)
        h_a = ar(7744, 8, P)
        h_ax = ar(8768, HGH, P)
        h_e = ar(9280, 1024)
        n_x = ar(10304, 2, 800)
        c_x = normed[:].rearrange("p a b -> p (a b)")[:, 0:960].rearrange("p (v i c) -> p v i c", v=2, i=16)
        c_xhi, c_xlo = (x[:, 0, 0:960].rearrange("p (v i c) -> p v i c", v=2, i=16) for x in (hi_d, lo_d))
        c_h = normed[0:30, 1, 0:512].rearrange("p (v n) -> p v n", v=2)
        c_ht = normed[:, 1, 512:632].rearrange("p (a b) -> p a b", a=4)
        c_k = ar(11904, 2, NB)
        c_v = ar(11936, 2, HD, p=NB)
        n_pt = normed[:]
        h_o = ar(0, TT, HGH, P)

        h_sq = ar(10304, 8, P)

        def decay_of(m):
            if m == 1:
                return h_f.rearrange("p h t -> p (h t)")
            at = 1024 - 2048 // m
            return h_e[:, at:at + 1024 // m]

        block = ctx.enter_context(nc.Block())

        @block.sync
        def _(sp):
            def load_unit(u):
                if u >= 2:
                    sp.wait_ge(S("hi_u_done"), u - 1)
                    sp.wait_ge(S("lo_u_done"), u - 1)
                if isinstance(units[u], list):
                    at = 0
                    for part in units[u]:
                        sp.dma_start(unit_view(raw_u, u)[:, :, at:at + part.shape[2]], part).then_inc(S(f"raw_u{u % 2}"), 16)
                        at += part.shape[2]
                    return
                if isinstance(units[u], tuple):
                    for dst, part in zip(pair_views(raw_u, u), units[u]):
                        sp.dma_start(dst, part).then_inc(S(f"raw_u{u % 2}"), 16)
                    return
                k = units[u].shape[1]
                for k0, k1 in ((0, k // 2), (k // 2, k)):
                    sp.dma_start(unit_view(raw_u, u)[:, k0:k1], units[u][:, k0:k1]).then_inc(S(f"raw_u{u % 2}"), 16)

            def load_up(f, t, slot, n):
                u = t + U_OF_FFN[f]
                sp.wait_ge(S("hi_u_done"), u - 1)
                sp.wait_ge(S("lo_u_done"), u - 1)
                for s in range(2):
                    src = gu[f][:, bass.ds(t * P + s * FW[f], n)].rearrange("(k p) n -> p k n", p=P)
                    dst = up_view(raw_u, slot, s, n)
                    if n < P:
                        dst = up_view(raw_u, slot, 0, 2 * n)[:, :, s * n:s * n + n]
                    sp.dma_start(dst, src).then_inc(S(f"raw_u{slot}"), 16)

            def load_down(f, t, slot, n):
                d = t + FT * f
                if f or not isinstance(t, int) or t >= 2:
                    sp.wait_ge(S("hi_d_done"), d - 1)
                    sp.wait_ge(S("lo_d_done"), d - 1)
                sp.dma_start(raw_d[0:n, slot, :], dn[f][bass.ds(t * P, n), :]).then_inc(S(f"raw_d{slot}"), 16)

            def ffn(f):
                for t in range(2):
                    load_up(f, t, t, P)
                    load_down(f, t, t, P)
                with sp.Fori(1, LOOPED + 1) as b:
                    for t in range(2):
                        load_up(f, b * 2 + t, t, P)
                        load_down(f, b * 2 + t, t, P)
                for t in range(2 * LOOPED + 2, FT):
                    load_up(f, t, t % 2, width(f, t))
                    load_down(f, t, t % 2, width(f, t))

            def load_gain(i):
                g = a["norm_g"]
                src = [g[0, 1], g[0, 3], g[1, 1], g[1, 3], a["final_norm_2"]][i]
                if i >= 2:
                    sp.wait_ge(S("resid_ready"), 2 * (i - 1))
                sp.dma_start(gain_row[:, i % 2, :], src.partition_broadcast(P)).then_inc(S(f"gain{i % 2}"), 16)

            for t in range(TT):
                sp.dma_start(resid[:, t, :], a["x"][0, t * P:t * P + P, :]).then_inc(S(f"x_in{t}"), 16)
            sp.dma_start(ident[:], a["ident"]).then_inc(S("ident_in"), 16)
            load_unit(0)
            load_unit(1)
            rows_in = S("vrows_in2")
            at = 0
            for name, n in (("ffn1_norm_2", 8), ("mix_norm_2", 8), ("ffn2_norm_2", 8), ("mla_q_norm_g", 3),
                            ("mla_kv_norm_g", 2), ("hgrn_lower_bound_2", 4), ("diff_subln_g", 1)):
                sp.dma_start(vrows[at:at + n, 1, :],
                             a[name].rearrange("l (k p) -> (l k) p", p=P)).then_inc(rows_in, 16)
                at += n
            for i, name in enumerate(("cmp_pos_k_2", "cmp_pos_v_2")):
                sp.dma_start(vrows[16 * i:16 * i + 16, 2, :],
                             a[name][0].rearrange("(i l) d -> i (l d)", l=2)).then_inc(rows_in, 16)
            cw = a["ffn_conv_w"].rearrange("l j (k p) -> (l j k) p", p=P)
            for i in range(3):
                sp.dma_start(vrows[0:88, 3 + i, :], cw[88 * i:88 * i + 88, :]).then_inc(rows_in, 16)
            sp.dma_start(vrows[0:88, 6, :], a["ffn_conv_b"].rearrange("l (k p) -> (l k) p", p=P)).then_inc(rows_in, 16)
            sp.dma_start(ropek, a["ropek"].rearrange("p (a t r) -> p a t r", a=2, t=TT)).then_inc(S("rope_in"), 16)
            sp.dma_start(ropeq, a["ropeq"].rearrange("p (a t) -> p a t", a=2)).then_inc(S("rope_in"), 16)
            load_gain(0)
            for u in range(2, U_F0):
                load_unit(u)
            load_gain(1)
            ffn(0)
            sp.dma_start(dist[:], a["dist"].rearrange("p (t k) -> p t k", t=TT)).then_inc(S("tables_in"), 16)
            sp.dma_start(causal[:], a["causal"].rearrange("p (t k) -> p t k", t=3)).then_inc(S("tables_in"), 16)
            sp.dma_start(lam[:, 0:256], a["diff_lambda"].rearrange("l a d -> (l a d)").partition_broadcast(P)).then_inc(S("tables_in"), 16)
            sp.dma_start(masks[:], a["masks"].rearrange("p (t k) -> p t k", t=8)).then_inc(S("tables_in"), 16)
            sp.dma_start(cdist[:], a["cdist"].rearrange("p (t k) -> p t k", t=TT)).then_inc(S("tables_in"), 16)
            sp.dma_start(crows[:], a["crows"]).then_inc(S("tables_in"), 16)
            sp.dma_start(w2k[:], a["cmp_k_w2_2"][0].rearrange("(c p) d -> p c d", p=P)).then_inc(S("tables_in"), 16)
            sp.dma_start(w2v[:], a["cmp_v_w2_2"][0].rearrange("(c p) d -> p c d", p=P)).then_inc(S("tables_in"), 16)
            sp.dma_start(hgain[:], a["hgrn_out_norm_2"][0].partition_broadcast(P)).then_inc(S("tables_in"), 16)
            load_gain(2)
            for u in range(U_QK, U_F1):
                load_unit(u)
            load_gain(3)
            ffn(1)
            load_gain(4)
            ffn(2)
            for u in range(U_NQ, U_F3):
                load_unit(u)
            ffn(3)
            for t in range(TT):
                sp.wait_ge(S("final"), t + 1)
                sp.dma_start(out[0, t * P:t * P + P, :], normed[:, t, :]).then_inc(S("stored"), 16)
            sp.wait_ge(S("stored"), 32)

        @block.gpsimd
        def _(pool):
            pool.memset(half[:], -0.5).then_inc(S("half_set"), 1)
            pool.wait_ge(S("half_set"), 1)

            def root(name, part, c0, n, over, ready, count):
                v = st[:, ST_OF[name], c0:c0 + n]
                pool.wait_ge(S(ready), count)
                pool.tensor_scalar(v, v, 1.0 / over, EPS, ALU.mult, ALU.add).then_inc(S("mean_squares"), 1)
                k[0] += 1
                pool.wait_ge(S("mean_squares"), k[0])
                return pool.tensor_tensor(v, v, half[:, 0:n], ALU.pow)

            k = [0]

            def norm_roots(i):
                for t in range(TT):
                    root(f"norm{i}", t, t, 1, D, "row_sums", 2 * i + t + 1).then_inc(S("rstd"), 1)

            def post_roots(j):
                for t in range(TT):
                    root(f"post{j}", t, t, 1, D, "post_sums", 2 * j + t + 1).then_inc(S("rstd"), 1)

            def hgrn():
                for l in range(1, 8):
                    m = 1 << (l - 1)
                    pool.wait_ge(S("h_level"), 2 * l + 2)
                    if l >= 2:
                        pool.wait_ge(S("h_e"), l - 1)
                        pool.wait_ge(S("h_k_upd"), l - 1)
                    e = decay_of(m).rearrange("p (n s) -> p n s", s=2)
                    left = h_k.rearrange("p h t -> p (h t)").rearrange("p (n s m) -> p n s m", s=2, m=m)[:, :, 0, :]
                    pool.tensor_tensor(left, left, e[:, :, 1:2].broadcast_to([P, 512 // m, m]), ALU.mult)\
                        .then_inc(S("h_k_upd"), 1)
                    if 2 * m <= 64:
                        pool.tensor_tensor(decay_of(2 * m), e[:, :, 0], e[:, :, 1], ALU.mult).then_inc(S("h_e"), 1)

            norm_roots(N_MLA)
            root("latents", 0, 0, 2, QL, "latent_sums", 1).then_inc(S("q_latent_root"), 1)
            root("latents", 0, 2, 2, KVL, "latent_sums", 2).then_inc(S("rstd"), 1)
            pool.wait_ge(S("ident_in"), 16)
            for h in range(H):
                slope = 2.0 ** (-8.0 * (h + 1) / H)
                pool.tensor_scalar(slopes[:, h, :], ident[:], -slope / D_SCALE, None, ALU.mult).then_inc(S("slopes"), 1)
            post_roots(0)
            norm_roots(N_F0)
            post_roots(1)
            norm_roots(N_DIFF)
            pool.wait_ge(S("tables_in"), 16 * 9)
            pool.tensor_copy(dist_b[:], dist[:]).then_inc(S("bias_tables"), 1)
            pool.tensor_copy(causal_b[:, 0:3 * P], causal[:].rearrange("p a b -> p (a b)")).then_inc(S("bias_tables"), 1)
            pool.tensor_copy(causal_b[:, 3 * P:], cdist[:].rearrange("p a b -> p (a b)")).then_inc(S("bias_tables"), 1)
            for g in range(2):
                root("heads", g, 8 * g, 8, P, "d_sums", 8 * g + 8).then_inc(S("rstd"), 1)
            post_roots(2)
            norm_roots(N_F1)
            post_roots(3)
            norm_roots(N_F2)
            norm_roots(N_MIX)
            pool.memset(h_a, 0.0).then_inc(S("h_a_zero"), 1)
            gate = h_g.rearrange("p t (h d) -> p (t h) d", h=HGH)
            pool.wait_ge(S("h_g_out"), 2)
            pool.tensor_tensor(gate, gate, hgain[:].unsqueeze(1).broadcast_to([P, 8, P]), ALU.mult)\
                .then_inc(S("h_g_gained"), 1)
            hgrn()
            root("hgrn", 0, 0, 8, P, "h_sums", 1).then_inc(S("rstd"), 1)
            norm_roots(N_F3)
            norm_roots(N_FINAL)

        @block.tensor
        def _(pe):
            def mm3(o, s_hi, s_lo, m_hi, m_lo, start, stop):
                pe.matmul(o, s_hi, m_hi, start=start, stop=False)
                pe.matmul(o, s_hi, m_lo, start=False, stop=False)
                return pe.matmul(o, s_lo, m_hi, start=False, stop=stop)

            def keep_warm(n, bank=5):
                for _ in range(n):
                    pe.matmul(psum[:, bank, :], zeros[:, 0:P], zeros[:], start=True, stop=True)

            def unit_ready(u):
                if isinstance(u, int) and u in HALVED:
                    pe.wait_ge(S("lo_u_half"), HALVED.index(u) + 1)
                pe.wait_ge(S("hi_u_done"), u + 1)
                pe.wait_ge(S("lo_u_done"), u + 1)

            def tok(t):
                return slice(t * P, t * P + P)

            def norm_transposes(i):
                for t in range(TT):
                    keep_warm(WARM[i][t])
                    pe.wait_ge(S("normed"), 2 * i + t + 1)
                    for b in range(4):
                        for k in (b, b + 4):
                            at = (k // 4) * SEQ + t * P
                            mm = pe.transpose(psum[:, b, at:at + P], normed[:, t, k * P:k * P + P], ident[:])
                        if t == 1:
                            mm.then_inc(S("norm_tr"), 1)
                keep_warm(WARM[i][2])

            def tokens_out(o, u, k0, w0, n, first, last, i=None):
                hi, lo = unit_view(hi_u, u), unit_view(lo_u, u)
                for k in range(hi.shape[1]):
                    if i is not None:
                        pe.wait_ge(S("act_lo"), 8 * i + k0 + k + 1)
                    for t in range(TT):
                        mm = mm3(o(t), act_hi[:, k0 + k, tok(t)], act_lo[:, k0 + k, tok(t)],
                                 hi[:, k, w0:w0 + n], lo[:, k, w0:w0 + n],
                                 first and k == 0, last and k == hi.shape[1] - 1)
                return mm

            def features_out(o, u, w0, n, c0=0, i=None):
                hi, lo = unit_view(hi_u, u), unit_view(lo_u, u)
                kn = hi.shape[1]
                for k in range(kn):
                    if i is not None:
                        pe.wait_ge(S("act_lo"), 8 * i + k + 1)
                    mm = mm3(o, hi[:, k, w0:w0 + n], lo[:, k, w0:w0 + n], act_hi[:, c0 + k, :], act_lo[:, c0 + k, :],
                             k == 0, k == kn - 1)
                return mm

            def wide(u0, chunk_ready, before={}):
                def part(i, k, t):
                    hi, lo = unit_view(hi_u, u0 + i), unit_view(lo_u, u0 + i)
                    for n in range(2):
                        mm = mm3(psum[:, 2 * t + n, :], act_hi[:, 2 * i + k, tok(t)], act_lo[:, 2 * i + k, tok(t)],
                                 hi[:, k, n * BANK:n * BANK + BANK], lo[:, k, n * BANK:n * BANK + BANK],
                                 i == 0 and k == 0, i == 3 and k == 1)
                    return mm

                for i in range(3):
                    unit_ready(u0 + i)
                    for k in range(2):
                        if 2 * i + k in before:
                            before[2 * i + k]()
                        chunk_ready(2 * i + k)
                        for t in range(TT):
                            mm = part(i, k, t)
                    mm.then_inc(S("used_u"), 1)
                unit_ready(u0 + 3)
                for t in range(TT):
                    for k in range(2):
                        if t == 0:
                            chunk_ready(6 + k)
                        mm = part(3, k, t)
                    mm.then_inc(S("first_half" if t == 0 else "used_u"), 1)

            def ffn(f):
                i = [N_F0, N_F1, N_F2, N_F3][f]

                def up(t, slot, n, first=False):
                    g, u = t + FT * f, t + U_OF_FFN[f]
                    unit_ready(u)
                    if not isinstance(t, int) or t >= 2:
                        if f < 2:
                            pe.wait_ge(S("tap_b"), g * 2 - 2)
                        else:
                            pe.wait_ge(S("hid_hi_done"), g - 1)
                    if n < P:
                        hi, lo = up_view(hi_u, slot, 0, 2 * n), up_view(lo_u, slot, 0, 2 * n)
                        for k in range(KC):
                            mm = mm3(psum[0:2 * n, 4 + 2 * slot, 0:SEQ], hi[:, k, :], lo[:, k, :],
                                     act_hi[:, k, :], act_lo[:, k, :], k == 0, k == KC - 1)
                        mm.then_inc(S("used_u"), 1)
                        return
                    views = [(up_view(hi_u, slot, s, n), up_view(lo_u, slot, s, n)) for s in range(2)]
                    order = [(s, k) for s in range(2) for k in range(KC)]
                    if first:
                        order = [(s, k) for k in range(KC) for s in range(2)]
                    for s, k in order:
                        if first and s == 0:
                            pe.wait_ge(S("act_lo"), 8 * i + k + 1)
                        hi, lo = views[s]
                        mm = mm3(psum[0:n, 4 + 2 * slot + s, 0:SEQ], hi[:, k, :], lo[:, k, :],
                                 act_hi[:, k, :], act_lo[:, k, :], k == 0, k == KC - 1)
                        if k == KC - 1:
                            mm.then_inc(S("gate_up" if s == 0 else "used_u"), 1)

                def down(t, slot, n, last=False, tiles=range(TT)):
                    g = t + FT * f
                    pe.wait_ge(S("hi_d_done"), g + 1)
                    pe.wait_ge(S("lo_d_done"), g + 1)
                    pe.wait_ge(S("hid_lo_done"), g + 1)
                    for tk in tiles:
                        for c in range(2):
                            w = slice(c * BANK, c * BANK + BANK)
                            mm = mm3(psum[:, 2 * tk + c, :], hid_hi[0:n, slot, tok(tk)], hid_lo[0:n, slot, tok(tk)],
                                     hi_d[0:n, slot, w], lo_d[0:n, slot, w], False, last)
                    mm.then_inc(S("used_d" if TT - 1 in tiles else "first_part"), 1)

                up(0, 0, P, True)
                pe.wait_ge(S("zeros_set"), 1)
                for b in range(4):
                    pe.matmul(psum[:, b, :], zeros[:, 0:P], zeros[:], start=True, stop=False)
                up(1, 1, P)
                down(0, 0, P)
                with pe.Fori(0, LOOPED) as b:
                    up(b * 2 + 2, 0, P)
                    down(b * 2 + 1, 1, P)
                    up(b * 2 + 3, 1, P)
                    down(b * 2 + 2, 0, P)
                up(20, 0, P)
                down(19, 1, P)
                up(21, 1, width(f, 21))
                down(20, 0, P)
                down(21, 1, width(f, 21), True, [0])
                down(21, 1, width(f, 21), True, [1])

            def mla():
                for i in range(2):
                    unit_ready(U_DQ + i)
                    mm = tokens_out(lambda t: psum[:, 4 + t, 0:QL], U_DQ + i, 4 * i, 0, QL, i == 0, i == 1, N_MLA)
                    mm.then_inc(S("used_u"), 1)
                pe.wait_ge(S("vrows_in2"), 16 * 13)
                for i, (at, n) in enumerate(VROWS[1:]):
                    mm = pe.transpose(psum[:, 3, at:at + n], vrows[0:n, 1 + i, :], ident[0:n, 0:n])
                mm.then_inc(S("vecs_tr"), 1)
                for i in range(2):
                    unit_ready(U_DKV + i)
                    mm = tokens_out(lambda t: psum[:, 6 + t, 0:KVL + ROPE], U_DKV + i, 4 * i, 0, KVL + ROPE,
                                    i == 0, i == 1)
                    mm.then_inc(S("used_u"), 1)
                    if i == 0:
                        pe.wait_ge(S("latents"), 2)
                        for c in range(3):
                            for t in range(TT):
                                mm = pe.transpose(psum[:, c // 2, (c % 2) * SEQ + t * P:(c % 2) * SEQ + t * P + P],
                                                  cq[:, t, c * P:c * P + P], ident[:])
                        mm.then_inc(S("latent_tr"), 1)
                pe.wait_ge(S("latent_lo"), 3)
                for i in range(4):
                    u = U_UQ + i
                    unit_ready(u)
                    b = 4 + 2 * (i % 2)
                    if i == 1:
                        pe.wait_ge(S("latents"), 4)
                        pe.wait_ge(S("k_roped"), 1)
                    if i >= 2:
                        pe.wait_ge(S("m_q_out"), i - 1)
                        pe.wait_ge(S("m_qr_read"), i - 1)
                    for h in range(2):
                        mm = features_out(psum[:, b, h * SEQ:h * SEQ + SEQ], u, h * 192, NOPE)
                    mm.then_inc(S("m_q_up"), 1)
                    for h in range(2):
                        mm = features_out(psum[0:ROPE, b + 1, h * SEQ:h * SEQ + SEQ], u, h * 192 + NOPE, ROPE)
                    mm.then_inc(S("used_u"), 1)
                    if i == 1:
                        pe.wait_ge(S("vecs_ready"), 2)
                        for c in range(2):
                            for t in range(TT):
                                pe.transpose(psum[:, 2, c * SEQ + t * P:c * SEQ + t * P + P],
                                             ck[:, t, c * P:c * P + P], ident[:])
                        for t in range(TT):
                            mm = pe.transpose(psum[0:ROPE, 3, t * P:t * P + P], kr3[:, 2, t, :], ident[:])
                        mm.then_inc(S("latent_tr"), 1)
                pe.wait_ge(S("latent_lo"), 5)
                for i in range(2):
                    u = U_UKV + i
                    unit_ready(u)
                    hi, lo = unit_view(hi_u, u), unit_view(lo_u, u)
                    if i == 0:
                        pe.wait_ge(S("m_kr_out"), 1)
                    else:
                        pe.wait_ge(S("m_q_out"), 4)
                        pe.wait_ge(S("m_qr_out"), 4)
                    for h in range(4):
                        mm = features_out(psum[:, 4 * i + h // 2, (h % 2) * SEQ:(h % 2) * SEQ + SEQ], u, h * 256, NOPE, 3)
                    mm.then_inc(S("m_k_up"), 1)
                    for t in range(TT):
                        for k in range(2):
                            v_hi, v_lo = (x[:, k, :].rearrange("p (h n) -> p h n", h=4)[:, :, NOPE:] for x in (hi, lo))
                            mm = mm3(psum[:, 4 * i + 2 + t, :], act_hi[:, 3 + k, tok(t)], act_lo[:, 3 + k, tok(t)],
                                     v_hi, v_lo, k == 0, k == 1)
                    mm.then_inc(S("used_u"), 1)

                def scores(h):
                    if h >= 3:
                        pe.wait_ge(S("m_exp"), 2 * (h - 2))
                    for t in range(TT):
                        o = psum[:, h % 3, t * SEQ:t * SEQ + SEQ]
                        pe.matmul(o, m_q[:, h, tok(t)], m_k[:, h, :], start=True, stop=False)
                        mm = pe.matmul(o, m_qr[:, h, tok(t)], m_kr, start=False, stop=True)
                    mm.then_inc(S("m_scores"), 1)

                def turn(h):
                    pe.wait_ge(S("m_probs"), 2 * h + 2)
                    if h >= 2:
                        pe.wait_ge(S("m_pt"), h - 1)
                    for k in range(2):
                        for t in range(TT):
                            mm = pe.transpose(psum[:, 3 + h % 2, k * SEQ + t * P:k * SEQ + t * P + P],
                                              m_p[:, h % 3, t, k * P:k * P + P], ident[:])
                    mm.then_inc(S("m_turned"), 1)

                def values(h):
                    pe.wait_ge(S("m_pt"), h + 1)
                    if h >= 2:
                        pe.wait_ge(S("m_o_lo"), h - 1)
                    for k in range(2):
                        mm = pe.matmul(psum[:, 5 + h % 2, 0:SEQ], m_v[:, k, h, :], m_pt[:, h % 2, k, :],
                                       start=k == 0, stop=k == 1)
                    mm.then_inc(S("m_values"), 1)

                pe.wait_ge(S("m_k_out"), 1)
                pe.wait_ge(S("m_v_out"), 1)
                for i in range(H + 3):
                    if i < H:
                        scores(i)
                    if i == 2:
                        pe.wait_ge(S("m_k_out"), 2)
                        pe.wait_ge(S("m_v_out"), 2)
                    if 0 <= i - 2 < H:
                        turn(i - 2)
                    if i >= 3:
                        values(i - 3)
                wide(U_MO, lambda c: pe.wait_ge(S("m_o_lo"), c + 1))

            def diff():
                for i in range(8):
                    u = U_QK + i
                    unit_ready(u)
                    if i >= 4:
                        pe.wait_ge(S("d_qk_out"), i - 3)
                    for h in range(2):
                        mm = features_out(psum[:, 4 + i % 4, h * SEQ:h * SEQ + SEQ], u, h * P, P,
                                          i=N_DIFF if i == 0 and h == 0 else None)
                    mm.then_inc(S("used_u"), 1)

                def v_unit(i):
                    unit_ready(U_V + i)
                    for n in range(2):
                        mm = tokens_out(lambda t: psum[:, 2 * t + n, :], U_V + i, 2 * i, n * BANK, BANK, i == 0, i == 3)
                    mm.then_inc(S("used_u"), 1)

                def scores(h):
                    if h >= 2:
                        pe.wait_ge(S("d_exp"), 4 * (h - 1))
                    for j in range(2):
                        r, b = slice(j * HD, j * HD + HD), 4 + 2 * (h % 2) + j
                        pe.matmul(psum[:, b, :], slopes[:, h, :], dist_b[:].rearrange("p t k -> p (t k)"),
                                  start=True, stop=False)
                        for t in range(TT):
                            mm = pe.matmul(psum[:, b, t * SEQ:t * SEQ + SEQ], d_q[r, h, tok(t)], d_k[r, h, :],
                                           start=False, stop=t == 1)
                    mm.then_inc(S("d_scores"), 1)

                def turn(h):
                    pe.wait_ge(S("d_maps"), 2 * h + 2)
                    if h >= 2:
                        pe.wait_ge(S("d_at"), h - 1)
                    for k in range(2):
                        for t in range(TT):
                            mm = pe.transpose(psum[:, h % 2, k * SEQ + t * P:k * SEQ + t * P + P],
                                              d_a[:, h % 2, t, k * P:k * P + P], ident[:])
                    mm.then_inc(S("d_turned"), 1)

                def values(h):
                    pe.wait_ge(S("d_at"), h + 1)
                    if h >= 2:
                        pe.wait_ge(S("d_sums"), 2 * (h - 1))
                    for t in range(TT):
                        for k in range(2):
                            mm = pe.matmul(psum[:, 2 + h % 2, t * P:t * P + P], d_at[:, h % 2, k, tok(t)],
                                           d_v[:, k, h * P:h * P + P], start=k == 0, stop=k == 1)
                    mm.then_inc(S("d_values"), 1)

                def heads_turn(g):
                    pe.wait_ge(S("d_normed"), 2 * g + 2)
                    for b in (2 * g, 2 * g + 1):
                        for k in range(2):
                            for t in range(TT):
                                mm = pe.transpose(psum[:, 4 + b, k * SEQ + t * P:k * SEQ + t * P + P],
                                                  d_o[:, t, 2 * b + k, :], ident[:])
                        mm.then_inc(S("d_tr"), 1)

                v_unit(0)
                pe.wait_ge(S("d_qk_out"), 8)
                pe.wait_ge(S("slopes"), 8)
                pe.wait_ge(S("bias_tables"), 3)
                scores(0)
                scores(1)
                for i in range(1, 4):
                    v_unit(i)
                for i in range(H + 1):
                    if i + 2 < H:
                        scores(i + 2)
                    if i == 0:
                        pe.wait_ge(S("d_exp"), 8)
                        keep_warm(WARM_DIFF, 6)
                        pe.wait_ge(S("d_v_out"), 2)
                    if i >= 1:
                        values(i - 1)
                    if i < H:
                        turn(i)
                    if i == H - 1:
                        heads_turn(0)
                pe.wait_ge(S("d_sums"), 16)
                wide(U_DO, lambda c: pe.wait_ge(S("d_lo"), c // 2 + 1), {2: lambda: heads_turn(1)})

            def mix():
                for i in range(2):
                    unit_ready(U_NQ + i)
                    for h in range(2):
                        mm = features_out(psum[:, 4 + i, h * SEQ:h * SEQ + SEQ], U_NQ + i, h * P, P,
                                          i=N_MIX if i == 0 and h == 0 else None)
                    mm.then_inc(S("used_u"), 1)
                unit_ready(U_NC)
                for v in range(2):
                    mm = features_out(psum[:, 6, v * SEQ:v * SEQ + SEQ], U_NC, v * P, P)
                mm.then_inc(S("used_u"), 1)
                unit_ready(U_NK)
                for i in range(2):
                    mm = features_out(psum[:, i, 0:SEQ], U_NK, i * P, P)
                mm.then_inc(S("used_u"), 1)
                for i in range(2):
                    unit_ready(U_NV + i)
                    mm = tokens_out(lambda t: psum[:, 2 + t, 0:280], U_NV + i, 4 * i, 0, 280, i == 0, i == 1)
                    mm.then_inc(S("used_u"), 1)
                for i in range(8):
                    if i == 0:
                        pe.wait_ge(S("n_q_out"), 2)
                    if i in (4, 6):
                        pe.wait_ge(S("h_q_out"), i // 2 - 1)
                    u = U_H + i
                    unit_ready(u)
                    (h_hi, c_hi), (h_lo, c_lo) = pair_views(hi_u, u), pair_views(lo_u, u)
                    at = (i % 2) * SEQ
                    for k in range(KC):
                        mm3(psum[:, 4 + (i // 2) % 2, at:at + SEQ], h_hi[:, k, :], h_lo[:, k, :],
                            act_hi[:, k, :], act_lo[:, k, :], k == 0, k == KC - 1)
                    v, quarter = i // 4, i % 4
                    pe.wait_ge(S("c_lo"), v + 1)
                    for k in range(4):
                        c = 4 * quarter + k
                        mm = mm3(psum[0:30, 6 + v, 0:256], c_xhi[:, v, c, :], c_xlo[:, v, c, :],
                                 c_hi[:, k, :], c_lo[:, k, :], c == 0, c == 15)
                    mm.then_inc(S("used_u"), 1)

                def values_and_gates(i):
                    unit_ready(U_HI + i)
                    for n in range(2):
                        mm = tokens_out(lambda t: psum[:, 2 * t + n, :], U_HI + i, 2 * i, n * BANK, BANK,
                                        i == 0, i == 3)
                    mm.then_inc(S("used_u"), 1)

                pe.wait_ge(S("n_k_out"), 8)
                pe.wait_ge(S("n_v_out"), 3)
                values_and_gates(0)
                pe.wait_ge(S("h_fk_out"), 4)
                pe.wait_ge(S("c_h_out"), 2)
                for v in range(2):
                    for c in range(2):
                        mm = pe.transpose(psum[:, 4, (2 * v + c) * 30:(2 * v + c) * 30 + 30],
                                          c_h[:, v, c * P:c * P + P], ident[0:30, 0:30])
                mm.then_inc(S("c_h_tr"), 1)
                values_and_gates(1)
                pe.wait_ge(S("c_ht_out"), 1)
                for e in range(2):
                    for g in range(2):
                        for c in range(2):
                            mm = pe.matmul(psum[e * HD:e * HD + HD, 5, g * NB:g * NB + NB], w2k[:, c, :],
                                           c_ht[:, c, g * NB:g * NB + NB], start=c == 0, stop=c == 1)
                for g in range(2):
                    for c in range(2):
                        mm = pe.matmul(psum[0:NB, 6, g * HD:g * HD + HD], c_ht[:, 2 + c, g * NB:g * NB + NB],
                                       w2v[:, c, :], start=c == 0, stop=c == 1)
                mm.then_inc(S("c_kv"), 1)
                values_and_gates(2)
                values_and_gates(3)

                def scores(h):
                    b, r, j, g = 4 + 2 * (h % 2), slice((h % 2) * HD, (h % 2) * HD + HD), h // 2, h // 4
                    if h >= 2:
                        pe.wait_ge(S("n_exp"), 6 * (h - 1))
                    for br in range(2):
                        k = n_k[r, 2 * br + g, :]
                        n = 3 * P + (0 if br else TT * NB)
                        pe.matmul(psum[:, b + br, 0:n], slopes[:, h, :], causal_b[:, 0:n], start=True, stop=False)
                        if br == 0:
                            for t in range(TT):
                                pe.matmul(psum[:, b, 3 * P + t * NB:3 * P + t * NB + NB], n_q[r, j, tok(t)],
                                          c_k[r, g, :], start=False, stop=False)
                        pe.matmul(psum[:, b + br, 0:P], n_q[r, j, tok(0)], k[:, 0:P], start=False, stop=False)
                        mm = pe.matmul(psum[:, b + br, P:3 * P], n_q[r, j, tok(1)], k, start=False, stop=True)
                    mm.then_inc(S("n_scores"), 1)

                def turn(h):
                    pe.wait_ge(S("n_probs"), N_DVE * (h + 1))
                    pe.wait_ge(S("n_probs_act"), (6 - N_DVE) * (h + 1))
                    if h >= 1:
                        pe.wait_ge(S("n_pt"), 3 * h)
                    x = n_x[:, h % 2, :]
                    for br in range(2):
                        for c in range(3):
                            pe.transpose(psum[:, br, c * P:c * P + P], x[:, (3 * br + c) * P:(3 * br + c + 1) * P],
                                         ident[:])
                        mm = pe.transpose(psum[0:NB, br, 3 * P:4 * P], x[:, 768 + br * NB:768 + br * NB + NB], ident[:])
                    mm.then_inc(S("n_turned"), 1)

                def values(h):
                    r, j, g = slice((h % 2) * HD, (h % 2) * HD + HD), h // 2, h // 4
                    pe.wait_ge(S("n_pt"), 3 * h + 3)
                    if j >= 1:
                        pe.wait_ge(S("n_o_lo"), j)
                    o, pt, gs = psum[r, 2, 0:SEQ], n_pt[:, h % 2, :], slice(g * HD, g * HD + HD)
                    pe.matmul(o, c_v[:, g, :], pt[0:NB, 768:1024], start=True, stop=False)
                    pe.matmul(o, n_vs[:, 0, gs], pt[:, 0:256], start=False, stop=False)
                    pe.matmul(o, n_vw[:, 0, gs], pt[:, 384:640], start=False, stop=False)
                    pe.matmul(o[:, P:], n_vs[:, 1, gs], pt[:, 256:384], start=False, stop=False)
                    pe.matmul(o[:, P:], n_vw[:, 1, gs], pt[:, 640:768], start=False, stop=True)\
                        .then_inc(S("n_values"), 1)

                def level(l, t):
                    if t == 0 and l >= 1:
                        pe.wait_ge(S("h_q_upd"), l)
                    if t == 0 and l >= 2:
                        pe.wait_ge(S("h_k_upd"), l - 1)
                    if l or t:
                        pe.wait_ge(S("h_a_done"), 2 * l + t)
                    for h in range(HGH):
                        mm = pe.matmul(psum[:, 3, h * P:h * P + P], h_k[:, h, tok(t)], h_q[:, h, tok(t)],
                                       start=True, stop=True)
                    mm.then_inc(S("h_level"), 1)

                pe.wait_ge(S("c_kv_out"), 2)
                for i in range(H + 2):
                    if i < H:
                        scores(i)
                    if i == 0:
                        pe.wait_ge(S("h_ready"), 1)
                        pe.wait_ge(S("h_v_out"), 2)
                        pe.wait_ge(S("h_g_out"), 2)
                    if 1 <= i <= 8:
                        level(i - 1, 1)
                    if i >= 2:
                        values(i - 2)
                    if 1 <= i <= H:
                        turn(i - 1)
                    if i < 8:
                        level(i, 0)
                pe.wait_ge(S("h_q_upd"), 8)
                pe.wait_ge(S("h_k_upd"), 7)
                pe.wait_ge(S("h_a_done"), 16)
                for h in range(HGH):
                    mm = pe.matmul(psum[:, 3, h * P:h * P + P], h_k[:, h, tok(0)], h_q[:, h, tok(1)],
                                   start=True, stop=True)
                mm.then_inc(S("h_level"), 1)
                v = [[h_v[:, t, h * P:h * P + P] for t in range(TT)] for h in range(HGH)]
                for h in range(HGH):
                    pe.matmul(psum[:, 4, h * P:h * P + P], h_a[:, h, :], v[h][0], start=True, stop=True)
                pe.wait_ge(S("h_ax_out"), 1)
                for h in range(HGH):
                    pe.matmul(psum[:, 5, h * P:h * P + P], h_ax[:, h, :], v[h][0], start=True, stop=False)
                    mm = pe.matmul(psum[:, 5, h * P:h * P + P], h_a[:, 4 + h, :], v[h][1], start=False, stop=True)
                mm.then_inc(S("h_out"), 1)

                def h_turn():
                    pe.wait_ge(S("h_gated"), 2)
                    for h in range(HGH):
                        for t in range(TT):
                            mm = pe.transpose(psum[:, 6 + h // 2, (h % 2) * SEQ + t * P:(h % 2) * SEQ + t * P + P],
                                              h_o[:, t, h, :], ident[:])
                        if h % 2:
                            mm.then_inc(S("h_tr"), 1)

                pe.wait_ge(S("n_o_lo"), 4)
                wide(U_WO, lambda c: pe.wait_ge(S("n_o_lo"), c + 1) if c < 4 else pe.wait_ge(S("h_lo"), (c - 2) // 2),
                     {3: h_turn})

            pe.wait_ge(S("ident_in"), 16)
            pe.wait_ge(S("vrows_in"), 16)
            at, n = VROWS[0]
            pe.transpose(psum[:, 4, at:at + n], vrows[0:n, 0, :], ident[0:n, 0:n]).then_inc(S("vecs_tr"), 1)
            pe.wait_ge(S("zeros_set"), 1)
            norm_transposes(N_MLA)
            mla()
            norm_transposes(N_F0)
            ffn(0)
            norm_transposes(N_DIFF)
            diff()
            norm_transposes(N_F1)
            ffn(1)
            norm_transposes(N_F2)
            ffn(2)
            norm_transposes(N_MIX)
            mix()
            norm_transposes(N_F3)
            ffn(3)

        @block.scalar
        def _(act):
            def split_u(u):
                if isinstance(u, int):
                    if u >= U_END:
                        return
                    act.wait_ge(S(f"raw_u{u % 2}"), 32 * (u // 2 + 1))
                    if u >= 2:
                        act.wait_ge(S("used_u"), u - 1)
                    if u in HALVED:
                        k = unit_view(hi_u, u).shape[1] // 2
                        for part, name in ((slice(0, k), "hi_u_half"), (slice(k, 2 * k), "hi_u_done")):
                            act.activation(unit_view(hi_u, u)[:, part], unit_view(raw_u, u)[:, part], ACT.Copy)\
                                .then_inc(S(name), 1)
                        return
                    act.activation(unit_view(hi_u, u), unit_view(raw_u, u), ACT.Copy).then_inc(S("hi_u_done"), 1)

            def split_u_looped(b, u0):
                act.wait_ge(S(f"raw_u{u0 % 2}"), b * 32 + 32 * (u0 // 2 + 1))
                act.wait_ge(S("used_u"), b * 2 + (u0 - 1))
                act.activation(u_slot(hi_u, u0), u_slot(raw_u, u0), ACT.Copy).then_inc(S("hi_u_done"), 1)

            def split_d(d, b=None):
                act.wait_ge(S(f"raw_d{d % 2}"), 16 * (d // 2 + 1) if b is None else b * 16 + 16 * (d // 2 + 1))
                if b is not None:
                    act.wait_ge(S("used_d"), b * 2 + (d - 1))
                elif d >= 2:
                    act.wait_ge(S("used_d"), d - 1)
                act.activation(hi_d[:, d % 2, :], raw_d[:, d % 2, :], ACT.Copy).then_inc(S("hi_d_done"), 1)

            def norm(i):
                for t in range(TT):
                    if i == N_MLA:
                        act.wait_ge(S(f"x_in{t}"), 16)
                    else:
                        act.wait_ge(S("resid_ready"), 2 * (i - 1) + t + 1)
                    act.activation(junk[:], resid[:, t, :], ACT.Square,
                                   accum_out=st[:, ST_OF[f"norm{i}"], t:t + 1])\
                        .then_inc(S("row_sums"), 1)
                    act.wait_ge(S("row_sums"), 2 * i + t + 1)
                if i == N_FINAL:
                    return
                if i != N_MLA:
                    split_u(SECOND[i])
                else:
                    act.wait_ge(S("vecs_tr"), 1)
                    act.activation(vecs[:, 0:64], psum[:, 4, 0:64], ACT.Copy).then_inc(S("vecs_ready"), 1)
                    split_u(0)
                    act.wait_ge(S("vecs_ready"), 1)
                for k in range(KC):
                    act.wait_ge(S("norm_tr"), 4 * i + k % 4 + 1)
                    if k >= 4:
                        act.wait_ge(S("act_lo"), 8 * i + k - 3)
                    act.activation(act_hi[:, k, :], psum[:, k % 4, (k // 4) * SEQ:(k // 4) * SEQ + SEQ], ACT.Copy,
                                   scale=vecs[:, V_OF_NORM[i] + k:V_OF_NORM[i] + k + 1]).then_inc(S("act_hi"), 1)
                    if i == N_MLA and k == 3:
                        split_u(SECOND[i])

            def post_sums(j, halves, whole, n):
                for t, (name, count) in enumerate(((halves, j // 2 + 1), (whole, n))):
                    act.wait_ge(S(name), count)
                    act.activation(junk[:].rearrange("p (a b) -> p a b", a=2), psum[:, 2 * t:2 * t + 2, :], ACT.Square,
                                   accum_out=st[:, ST_OF[f"post{j}"], t:t + 1]).then_inc(S("post_sums"), 1)
                    act.wait_ge(S("post_sums"), 2 * j + t + 1)

            def ffn(f):
                def tile(t, slot, n, b=None):
                    at = (lambda x: x) if b is None else (lambda x: b * 2 + x)
                    g, u = FT * f + t, U_OF_FFN[f] + t
                    looped_or_late = b is not None or g >= 2
                    if n < P:
                        act.wait_ge(S("used_u"), u + 1)
                    else:
                        act.wait_ge(S("gate_up"), at(g + 1 - (f == 3)))
                    if f < 2:
                        if looped_or_late:
                            act.wait_ge(S("hid_lo_done"), at(g - 1))
                        for s, buf in ((0, cg), (1, cv)):
                            if s:
                                act.wait_ge(S("used_u"), at(u + 1))
                            w = at(V_CW + (f * 3 + 1) * 44 + s * FT + t)
                            c = at(V_CB + f * 44 + s * FT + t)
                            act.activation(buf[0:n, slot, :], psum[0:n, 4 + 2 * slot + s, 0:SEQ], ACT.Identity,
                                           scale=vecs[0:n, bass.ds(w, 1)], bias=vecs[0:n, bass.ds(c, 1)])\
                                .then_inc(S("conv_mid"), 1)
                    else:
                        act.wait_ge(S("hid_hi_done"), at(g - 1))
                        r = slice(n, 2 * n) if n < P else slice(0, P)
                        act.activation(gg[r, slot, :], psum[0:n, 4 + 2 * slot, 0:SEQ], ACT.Silu)\
                            .then_inc(S("gated"), 1)
                    if b is not None:
                        split_u_looped(b, u + 2)
                    elif t < 20:
                        split_u(u + 2)
                    if f < 2:
                        act.wait_ge(S("tap_b"), b * 4 + 2 * g + 1 if b is not None else 2 * g + 1)
                        act.activation(gg[0:n, slot, :], cg[0:n, slot, :], ACT.Gelu_apprx_tanh).then_inc(S("gated"), 1)
                    if b is not None or t + 1 < FT:
                        split_d(g + 1, b)

                split_d(FT * f)
                tile(0, 0, P)
                tile(1, 1, P)
                with act.Fori(0, LOOPED) as b:
                    tile(2, 0, P, b)
                    tile(3, 1, P, b)
                tile(20, 0, P)
                tile(21, 1, width(f, 21))
                split_u(U_OF_FFN[f] + FT)

            def mla():
                split_u(2)
                split_u(3)
                ch = Chain(act, S("act_chain_mla"))
                act.wait_ge(S("used_u"), U_DQ + 2)
                for t in range(TT):
                    ins = act.activation(junk[:, 0:QL], psum[:, 4 + t, 0:QL], ACT.Square,
                                         accum_out=st[:, ST_OF["latents"], t:t + 1])
                    if t == 0:
                        ch.link(ins)
                ins.then_inc(S("latent_sums"), 1)
                act.wait_ge(S("vecs_tr"), 2)
                act.activation(vecs[:, 64:], psum[:, 3, 64:V_ALL], ACT.Copy).then_inc(S("vecs_ready"), 1)
                split_u(4)

                def latent_hi(chunks):
                    for c in chunks:
                        b, o = (c // 2, c % 2) if c < 3 else (2, c - 3)
                        v = V_QN + c if c < 3 else V_KVN + c - 3
                        act.activation(act_hi[:, c, :], psum[:, b, o * SEQ:o * SEQ + SEQ], ACT.Copy,
                                       scale=vecs[:, v:v + 1]).then_inc(S("latent_hi"), 1)

                act.wait_ge(S("vecs_ready"), 2)
                act.wait_ge(S("latent_tr"), 1)
                latent_hi(range(3))
                act.wait_ge(S("used_u"), U_DKV + 2)
                for t in range(TT):
                    ins = act.activation(junk[:, QL:QL + KVL], psum[:, 6 + t, 0:KVL], ACT.Square,
                                         accum_out=st[:, ST_OF["latents"], 2 + t:3 + t])
                    if t == 0:
                        ch.link(ins)
                ins.then_inc(S("latent_sums"), 1)
                split_u(5)
                for i in range(4):
                    if i == 2:
                        act.wait_ge(S("latent_tr"), 2)
                        latent_hi(range(3, 5))
                        act.activation(m_kr, psum[0:ROPE, 3, 0:SEQ], ACT.Copy).then_inc(S("m_kr_out"), 1)
                    act.wait_ge(S("m_q_up"), i + 1)
                    act.activation(m_q[:, 2 * i:2 * i + 2, :], psum[:, 4 + 2 * (i % 2), :].rearrange("p (h t) -> p h t", h=2),
                                   ACT.Copy).then_inc(S("m_q_out"), 1)
                    split_u(U_UQ + i + 2)
                for i in range(2):
                    act.wait_ge(S("m_k_up"), i + 1)
                    act.activation(m_k[:, 4 * i:4 * i + 4, :],
                                   psum[:, 4 * i:4 * i + 2, :].rearrange("p b (h t) -> p (b h) t", h=2), ACT.Copy)\
                        .then_inc(S("m_k_out"), 1)
                    if i == 0:
                        split_u(U_UKV + 2)
                for i in range(H + 3):
                    if i < H:
                        act.wait_ge(S("m_bias"), i + 1)
                        if i >= 3:
                            act.wait_ge(S("m_turned"), i - 2)
                        for t in range(TT):
                            act.activation(m_p[:, i % 3, t, :], psum[:, i % 3, t * SEQ:t * SEQ + SEQ], ACT.Exp,
                                           scale=M_SCALE, bias=soft[:, i, 1, t:t + 1],
                                           accum_out=soft[:, i, 2, t:t + 1]).then_inc(S("m_exp"), 1)
                    if 0 <= i - 2 < H:
                        h = i - 2
                        act.wait_ge(S("m_turned"), h + 1)
                        if h >= 2:
                            act.wait_ge(S("m_values"), h - 1)
                        act.activation(m_pt[:, h % 2], psum[:, 3 + h % 2, :].rearrange("p (k t) -> p k t", k=2),
                                       ACT.Copy).then_inc(S("m_pt"), 1)
                    if i >= 3:
                        h = i - 3
                        act.wait_ge(S("m_values"), h + 1)
                        act.activation(act_hi[:, h, :], psum[:, 5 + h % 2, 0:SEQ], ACT.Copy).then_inc(S("m_o_hi"), 1)
                    if i == H:
                        split_u(U_UKV + 3)
                for i in range(3):
                    split_u(U_MO + i + 2)

            def diff():
                for i in range(8):
                    split_u(U_QK + i + 2)
                    act.wait_ge(S("used_u"), U_QK + i + 1)
                    act.activation((d_q if i < 4 else d_k)[:, 2 * (i % 4):2 * (i % 4) + 2, :],
                                   psum[:, 4 + i % 4, :].rearrange("p (h t) -> p h t", h=2), ACT.Copy)\
                        .then_inc(S("d_qk_out"), 1)
                act.wait_ge(S("lam_sums"), 1)
                act.activation(lam[:, 258:260], lam[:, 256:258], ACT.Exp).then_inc(S("lam_exp"), 1)

                def exps(h):
                    act.wait_ge(S("d_bias"), h + 1)
                    if h >= 3:
                        act.wait_ge(S("d_maps"), 2 * (h - 2))
                    for m in range(4):
                        act.activation(d_x[:, h % 3, m, :], psum[:, 4 + 2 * (h % 2) + m // 2, (m % 2) * SEQ:(m % 2) * SEQ + SEQ],
                                       ACT.Exp, scale=D_SCALE, bias=soft[:, h, 1, m:m + 1],
                                       accum_out=soft[:, h, 2, m:m + 1]).then_inc(S("d_exp"), 1)

                def heads_hi(g):
                    for b in (2 * g, 2 * g + 1):
                        act.wait_ge(S("d_tr"), b + 1)
                        act.activation(act_hi[:, 2 * b:2 * b + 2, :], psum[:, 4 + b, :].rearrange("p (k t) -> p k t", k=2),
                                       ACT.Copy, scale=lam[:, 261:262]).then_inc(S("d_hi"), 1)

                split_u(U_V + 2)
                exps(0)
                split_u(U_V + 3)
                exps(1)
                split_u(U_V + 4)
                act.wait_ge(S("used_u"), U_V + 4)
                act.activation(d_v[:, 0, :].rearrange("p (a b) -> p a b", a=2), psum[:, 0:2, :], ACT.Copy)\
                    .then_inc(S("d_v_out"), 1)
                act.wait_ge(S("d_gain"), 1)
                for i in range(H + 1):
                    if i == H:
                        heads_hi(0)
                    if i >= 1:
                        h = i - 1
                        act.wait_ge(S("d_values"), h + 1)
                        for t in range(TT):
                            act.activation(d_o[:, t, h, :], psum[:, 2 + h % 2, t * P:t * P + P], ACT.Copy,
                                           scale=soft[:, h, 3, t:t + 1]).then_inc(S("d_o_out"), 1)
                        for t in range(TT):
                            c, left = 8 * (h // 4) + 4 * t + h % 4, d_sq[:, 2 * h + t, :]
                            act.activation(left, psum[:, 2 + h % 2, t * P:t * P + P], ACT.Square,
                                           scale=soft[:, h, 3, t:t + 1], accum_out=st[:, ST_OF["heads"], c:c + 1])\
                                .then_inc(S("d_sums"), 1)
                    if i < H:
                        act.wait_ge(S("d_turned"), i + 1)
                        if i >= 2:
                            act.wait_ge(S("d_values"), i - 1)
                        act.activation(d_at[:, i % 2], psum[:, i % 2, :].rearrange("p (k t) -> p k t", k=2),
                                       ACT.Copy).then_inc(S("d_at"), 1)
                    if i + 2 < H:
                        exps(i + 2)
                split_u(U_V + 5)
                split_u(U_DO + 2)
                heads_hi(1)
                split_u(U_DO + 3)
                split_u(U_DO + 4)

            def mix():
                both = lambda v: v.rearrange("p (h t) -> p h t", h=2)
                act.wait_ge(S("lb_shifted"), 1)
                act.activation(bound[:, 1, :], bound[:, 0, :], ACT.Exp).then_inc(S("lb_exp"), 1)
                for i in range(2):
                    act.wait_ge(S("used_u"), U_NQ + i + 1)
                    split_u(U_NQ + i + 2)
                    act.activation(n_q[:, 2 * i:2 * i + 2, :], both(psum[:, 4 + i, :]), ACT.Copy).then_inc(S("n_q_out"), 1)
                split_u(U_NC + 2)
                split_u(U_NK + 2)
                act.wait_ge(S("c_x_done"), 16)
                for v in range(2):
                    act.activation(c_xhi[:, v], c_x[:, v], ACT.Copy).then_inc(S("c_hi"), 1)
                split_u(U_NV + 2)
                for i in range(2):
                    for g in range(2):
                        for e in range(2):
                            act.activation(n_k[e * HD:e * HD + HD, 2 * i + g, :],
                                           psum[g * HD:g * HD + HD, i, 0:SEQ], ACT.Copy)\
                                .then_inc(S("n_k_out"), 1)
                split_u(U_NV + 3)
                for i in range(8):
                    if i == 7:
                        act.wait_ge(S("used_u"), U_H + 8)
                    else:
                        split_u(U_H + i + 2)
                    b = i // 2
                    if i in (1, 3):
                        act.activation(h_q[:, 2 * b:2 * b + 2, :], both(psum[:, 4 + b, :]), ACT.Silu)\
                            .then_inc(S("h_q_out"), 1)
                    if i == 5:
                        act.wait_ge(S("n_v_out"), 3)
                        act.activation(n_g, n_g, ACT.Sigmoid).then_inc(S("n_gates"), 1)
                    if i in (5, 7):
                        for sign, dst in ((1.0, h_f), (-1.0, h_k)):
                            act.activation(dst[:, 2 * b - 4:2 * b - 2, :], both(psum[:, 2 + b, :]), ACT.Sigmoid,
                                           scale=sign).then_inc(S("h_fk_out"), 1)
                split_u(U_HI + 1)
                for v in range(2):
                    act.activation(c_h[:, v, :], psum[0:30, 6 + v, 0:256], ACT.Gelu_apprx_tanh)\
                        .then_inc(S("c_h_out"), 1)
                split_u(U_HI + 2)
                act.wait_ge(S("c_h_tr"), 1)
                act.activation(c_ht, psum[:, 4, 0:120].rearrange("p (a b) -> p a b", a=4), ACT.Copy)\
                    .then_inc(S("c_ht_out"), 1)
                split_u(U_HI + 3)
                act.wait_ge(S("c_kv"), 1)
                act.activation(c_k, psum[:, 5, 0:30].rearrange("p (a b) -> p a b", a=2), ACT.Copy)\
                    .then_inc(S("c_kv_out"), 1)
                act.activation(c_v, psum[0:NB, 6, 0:P].rearrange("p (a b) -> p a b", a=2), ACT.Copy)\
                    .then_inc(S("c_kv_out"), 1)
                split_u(U_HI + 4)
                for t in range(TT):
                    act.wait_ge(S("used_u"), U_HI + 4)
                    act.activation(h_g[:, t, :], psum[:, 1 + 2 * t, :], ACT.Silu).then_inc(S("h_g_out"), 1)
                for i in range(H + 2):
                    if 1 <= i <= H:
                        h = i - 1
                        act.wait_ge(S("n_factors"), h + 1)
                        x = n_x[:, h % 2, :]
                        for m, (at, n) in list(enumerate(N_PARTS))[N_DVE:]:
                            act.activation(x[:, at:at + n], x[:, at:at + n], ACT.Copy, scale=soft[:, h, 3, m:m + 1])\
                                .then_inc(S("n_probs_act"), 1)
                    if i < H:
                        act.wait_ge(S("n_bias"), i + 1)
                        if i >= 2:
                            act.wait_ge(S("n_turned"), i - 1)
                        for m, (at, n) in enumerate(N_PARTS):
                            branch, col = (0, 3 * P + m * NB) if m < 2 else ((m - 2) // 2, (m % 2) * P)
                            act.activation(n_x[:, i % 2, at:at + n], psum[:, 4 + 2 * (i % 2) + branch, col:col + n], ACT.Exp,
                                           scale=D_SCALE, bias=soft[:, i, 1, m:m + 1],
                                           accum_out=soft[:, i, 2, m:m + 1]).then_inc(S("n_exp"), 1)
                    if i >= 2 and i % 2:
                        j = (i - 2) // 2
                        act.wait_ge(S("n_values"), 2 * j + 2)
                        act.activation(act_hi[:, j, :], psum[:, 2, 0:SEQ], ACT.Copy).then_inc(S("n_o_hi"), 1)
                    if 1 <= i <= H:
                        h = i - 1
                        act.wait_ge(S("n_turned"), h + 1)
                        if h >= 2:
                            act.wait_ge(S("n_values"), h - 1)
                        act.activation(n_pt[:, h % 2, 0:384], psum[:, 0, 0:384], ACT.Copy).then_inc(S("n_pt"), 1)
                        act.activation(n_pt[:, h % 2, 384:768], psum[:, 1, 0:384], ACT.Copy).then_inc(S("n_pt"), 1)
                        act.activation(n_pt[0:NB, h % 2, 768:1024].rearrange("p (t k) -> p t k", t=TT),
                                       psum[0:NB, 0:2, 384:512], ACT.Copy).then_inc(S("n_pt"), 1)
                    if i == H:
                        split_u(U_HI + 5)
                act.wait_ge(S("h_level"), 17)
                act.activation(h_ax, psum[:, 3, :].rearrange("p (h t) -> p h t", h=HGH), ACT.Copy)\
                    .then_inc(S("h_ax_out"), 1)
                act.wait_ge(S("h_out"), 1)
                act.activation(h_sq, psum[:, 4:6, :].rearrange("p t (h d) -> p (t h) d", h=HGH), ACT.Square)\
                    .then_inc(S("h_squares"), 1)
                split_u(U_WO + 2)
                for b in range(2):
                    act.wait_ge(S("h_tr"), b + 1)
                    act.activation(act_hi[:, 4 + 2 * b:6 + 2 * b, :], both(psum[:, 6 + b, :]), ACT.Copy)\
                        .then_inc(S("h_hi"), 1)
                for i in range(1, 3):
                    split_u(U_WO + i + 2)

            act.dma_start(vrows[0:64, 0, :], a["norm_g"].rearrange("l n (k p) -> (l n k) p", p=P)).then_inc(S("vrows_in"), 16)
            norm(N_MLA)
            mla()
            post_sums(0, "first_half", "used_u", U_MO + 4)
            norm(N_F0)
            ffn(0)
            post_sums(1, "first_part", "used_d", FT)
            norm(N_DIFF)
            diff()
            post_sums(2, "first_half", "used_u", U_DO + 4)
            norm(N_F1)
            ffn(1)
            post_sums(3, "first_part", "used_d", 2 * FT)
            norm(N_F2)
            ffn(2)
            norm(N_MIX)
            mix()
            norm(N_F3)
            ffn(3)
            norm(N_FINAL)

        @block.vector
        def _(dve):
            def split_half(u, part):
                if part == 0:
                    dve.wait_ge(S("hi_u_half"), HALVED.index(u) + 1)
                else:
                    dve.wait_ge(S("hi_u_done"), u + 1)
                v = [unit_view(x, u) for x in (lo_u, raw_u, hi_u)]
                k = v[0].shape[1] // 2
                r = slice(part * k, part * k + k)
                dve.tensor_tensor(v[0][:, r], v[1][:, r], v[2][:, r].bitcast(F32), ALU.subtract)\
                    .then_inc(S("lo_u_done" if part else "lo_u_half"), 1)

            def split_u(u, b=None):
                if b is not None:
                    dve.wait_ge(S("hi_u_done"), b * 2 + (u + 1))
                    v = [u_slot(x, u) for x in (lo_u, raw_u, hi_u)]
                else:
                    if u >= U_END:
                        return
                    if u in HALVED:
                        split_half(u, 0)
                        split_half(u, 1)
                        return
                    dve.wait_ge(S("hi_u_done"), u + 1)
                    v = [unit_view(x, u) for x in (lo_u, raw_u, hi_u)]
                dve.tensor_tensor(v[0], v[1], v[2].bitcast(F32), ALU.subtract).then_inc(S("lo_u_done"), 1)

            def split_d(d, b=None):
                dve.wait_ge(S("hi_d_done"), d + 1 if b is None else b * 2 + (d + 1))
                dve.tensor_tensor(lo_d[:, d % 2, :], raw_d[:, d % 2, :], hi_d[:, d % 2, :].bitcast(F32),
                                  ALU.subtract).then_inc(S("lo_d_done"), 1)

            def norm(i):
                for t in range(TT):
                    dve.wait_ge(S("rstd"), root_no(f"norm{i}", t))
                    scale = st[:, ST_OF[f"norm{i}"], t:t + 1]
                    if i == N_FINAL:
                        dve.wait_ge(S("gain0"), 16 * 3)
                        dve.scalar_tensor_tensor(normed[:, t, :], resid[:, t, :], scale, gain_row[:, 0, :], ALU.mult,
                                                 ALU.mult).then_inc(S("final"), 1)
                    else:
                        dve.tensor_scalar(normed[:, t, :], resid[:, t, :], scale, None, ALU.mult)\
                            .then_inc(S("normed"), 1)
                        if i != N_MLA:
                            split_half(FIRST[i], t)
                if i == N_FINAL:
                    return
                if i == N_MLA:
                    split_u(FIRST[i])
                for k in range(KC):
                    dve.wait_ge(S("act_hi"), 8 * i + k + 1)
                    v = V_OF_NORM[i] + k
                    dve.scalar_tensor_tensor(act_lo[:, k, :], psum[:, k % 4, (k // 4) * SEQ:(k // 4) * SEQ + SEQ],
                                             vecs[:, v:v + 1], act_hi[:, k, :].bitcast(F32), ALU.mult,
                                             ALU.subtract).then_inc(S("act_lo"), 1)
                    if k == (3 if i == N_MLA else KC - 1):
                        split_u(SECOND[i])

            def post(j):
                dve.wait_ge(S(f"gain{j % 2}"), 16 * (j // 2 + 1))
                two = lambda v: v.rearrange("p (a b) -> p a b", a=2)
                for t in range(TT):
                    dve.wait_ge(S("post_sums"), 2 * j + t + 1)
                    dve.tensor_tensor(two(normed[:, t, :]), psum[:, 2 * t:2 * t + 2, :], two(gain_row[:, j % 2, :]),
                                      ALU.mult).then_inc(S("post_gained"), 1)
                    dve.wait_ge(S("post_gained"), 2 * j + t + 1)
                    dve.wait_ge(S("rstd"), root_no(f"post{j}", t))
                    dve.scalar_tensor_tensor(resid[:, t, :], normed[:, t, :], st[:, ST_OF[f"post{j}"], t:t + 1],
                                             resid[:, t, :], ALU.mult, ALU.add).then_inc(S("resid_ready"), 1)

            def add(factor, waits):
                two = lambda v: v.rearrange("p (a b) -> p a b", a=2)
                for t in range(TT):
                    dve.wait_ge(S(waits[t][0]), waits[t][1])
                    dve.scalar_tensor_tensor(two(resid[:, t, :]), psum[:, 2 * t:2 * t + 2, :], factor,
                                             two(resid[:, t, :]), ALU.mult, ALU.add).then_inc(S("resid_ready"), 1)

            def ffn(f):
                def tile(t, slot, n, b=None):
                    at = (lambda x: x) if b is None else (lambda x: b * 2 + x)
                    at2 = (lambda x: x) if b is None else (lambda x: b * 4 + x)
                    g, u = FT * f + t, U_OF_FFN[f] + t
                    if f < 2:
                        for tap, name in ((0, "tap_a"), (2, "tap_b")):
                            for s, buf in ((0, cg), (1, cv)):
                                dve.wait_ge(S("conv_mid" if tap == 0 else "tap_a"), at2(2 * g + s + 1))
                                w = at(V_CW + (f * 3 + tap) * 44 + s * FT + t)
                                o = slice(1, SEQ) if tap == 0 else slice(0, SEQ - 1)
                                x = slice(0, SEQ - 1) if tap == 0 else slice(1, SEQ)
                                dve.scalar_tensor_tensor(buf[0:n, slot, o], psum[0:n, 4 + 2 * slot + s, x],
                                                         vecs[0:n, bass.ds(w, 1)], buf[0:n, slot, o],
                                                         ALU.mult, ALU.add).then_inc(S(name), 1)
                    if b is not None or t < 20:
                        split_u(u + 2, b)
                    dve.wait_ge(S("gated"), at(g + 1))
                    if f < 2:
                        dve.wait_ge(S("tap_b"), at2(2 * g + 2))
                        gate, val = gg[0:n, slot, :], cv[0:n, slot, :]
                    elif n < P:
                        gate, val = gg[n:2 * n, slot, :], psum[n:2 * n, 4 + 2 * slot, 0:SEQ]
                    else:
                        dve.wait_ge(S("used_u"), at(u + 1))
                        gate, val = gg[:, slot, :], psum[:, 5 + 2 * slot, 0:SEQ]
                    dve.tensor_tensor(hf[0:n, slot, :], gate, val, ALU.mult).then_inc(S("hidden"), 1)
                    if b is not None or g >= 2:
                        dve.wait_ge(S("used_d"), at(g - 1))
                    dve.tensor_tensor(hid_hi[0:n, slot, :], gate, val, ALU.mult)\
                        .then_inc(S("hid_hi_done"), 1)
                    dve.wait_ge(S("hidden"), at(g + 1))
                    dve.wait_ge(S("hid_hi_done"), at(g + 1))
                    dve.tensor_tensor(hid_lo[0:n, slot, :], hf[0:n, slot, :], hid_hi[0:n, slot, :].bitcast(F32),
                                      ALU.subtract).then_inc(S("hid_lo_done"), 1)
                    if b is not None or t + 1 < FT:
                        split_d(g + 1, b)

                split_d(FT * f)
                tile(0, 0, P)
                tile(1, 1, P)
                with dve.Fori(0, LOOPED) as b:
                    tile(2, 0, P, b)
                    tile(3, 1, P, b)
                tile(20, 0, P)
                tile(21, 1, width(f, 21))

            def mla():
                split_u(2)
                ch = Chain(dve, S("dve_chain_mla"))
                split_u(3)
                dve.wait_ge(S("q_latent_root"), 1)
                for t in range(TT):
                    dve.tensor_scalar(cq[:, t, :], psum[:, 4 + t, 0:QL], st[:, ST_OF["latents"], t:t + 1], None, ALU.mult)\
                        .then_inc(S("latents"), 1)
                split_u(4)

                def latent_lo(chunks):
                    for c in chunks:
                        b, o = (c // 2, c % 2) if c < 3 else (2, c - 3)
                        v = V_QN + c if c < 3 else V_KVN + c - 3
                        dve.wait_ge(S("latent_hi"), 3 if c < 3 else 5)
                        dve.scalar_tensor_tensor(act_lo[:, c, :], psum[:, b, o * SEQ:o * SEQ + SEQ], vecs[:, v:v + 1],
                                                 act_hi[:, c, :].bitcast(F32), ALU.mult, ALU.subtract)\
                            .then_inc(S("latent_lo"), 1)

                latent_lo(range(3))
                dve.wait_ge(S("latent_sums"), 2)
                dve.wait_ge(S("rope_in"), 32)
                raw = psum[:, 6:8, KVL:KVL + ROPE]
                ch.put(dve.tensor_tensor(kr3[:, 0], raw, ropek[:, 0], ALU.mult))
                ch.put(dve.tensor_tensor(kr3[:, 1, :, 0:32], raw[:, :, 32:64], ropek[:, 1, :, 32:64], ALU.mult))
                ch.put(dve.tensor_tensor(kr3[:, 1, :, 32:64], raw[:, :, 0:32], ropek[:, 1, :, 0:32], ALU.mult))
                ch.wait()
                dve.tensor_tensor(kr3[:, 2], kr3[:, 0], kr3[:, 1], ALU.add).then_inc(S("k_roped"), 1)
                dve.wait_ge(S("rstd"), root_no("latents"))
                for t in range(TT):
                    dve.tensor_scalar(ck[:, t, :], psum[:, 6 + t, 0:KVL], st[:, ST_OF["latents"], 2 + t:3 + t], None, ALU.mult)\
                        .then_inc(S("latents"), 1)
                split_u(5)
                t1, t2 = qr2[:, 0], qr2[:, 1]
                both = lambda v: v.unsqueeze(1).broadcast_to([v.shape[0], 2, SEQ])
                for i in range(4):
                    if i == 2:
                        latent_lo(range(3, 5))
                    dve.wait_ge(S("used_u"), U_UQ + i + 1)
                    if i:
                        dve.wait_ge(S("m_qr_out"), i)
                    raw = psum[0:ROPE, 4 + 2 * (i % 2) + 1, :].rearrange("p (h t) -> p h t", h=2)
                    ch.put(dve.tensor_tensor(t1, raw, both(ropeq[:, 0, :]), ALU.mult))
                    ch.put(dve.tensor_tensor(t2[0:32], raw[32:64], both(ropeq[32:64, 1, :]), ALU.mult))
                    dve.tensor_tensor(t2[32:64], raw[0:32], both(ropeq[0:32, 1, :]), ALU.mult)\
                        .then_inc(S("m_qr_read"), 1)
                    ch.wait()
                    dve.wait_ge(S("m_qr_read"), i + 1)
                    dve.tensor_tensor(m_qr[:, 2 * i:2 * i + 2, :], t1, t2, ALU.add).then_inc(S("m_qr_out"), 1)
                    split_u(U_UQ + i + 2)
                for i in range(2):
                    dve.wait_ge(S("used_u"), U_UKV + i + 1)
                    dve.tensor_copy(m_v[:, :, 4 * i:4 * i + 4, :], psum[:, 4 * i + 2:4 * i + 4, :].rearrange("p t (h d) -> p t h d", h=4))\
                        .then_inc(S("m_v_out"), 1)
                    if i == 0:
                        split_u(U_UKV + 2)
                for i in range(H + 3):
                    if i < H:
                        dve.wait_ge(S("m_scores"), i + 1)
                        ch.link(dve.tensor_reduce(soft[:, i, 0, 0:2], psum[:, i % 3, :].rearrange("p (t k) -> p t k", t=2),
                                                  AX, ALU.max))
                        dve.tensor_scalar(soft[:, i, 1, 0:2], soft[:, i, 0, 0:2], -M_SCALE, None, ALU.mult)\
                            .then_inc(S("m_bias"), 1)
                    if 0 <= i - 1 < H:
                        h = i - 1
                        dve.wait_ge(S("m_exp"), 2 * h + 2)
                        ch.link(dve.reciprocal(soft[:, h, 3, 0:2], soft[:, h, 2, 0:2]))
                        for t in range(TT):
                            dve.tensor_scalar(m_p[:, h % 3, t, :], m_p[:, h % 3, t, :], soft[:, h, 3, t:t + 1], None,
                                              ALU.mult).then_inc(S("m_probs"), 1)
                    if i >= 3:
                        h = i - 3
                        dve.wait_ge(S("m_o_hi"), h + 1)
                        dve.tensor_tensor(act_lo[:, h, :], psum[:, 5 + h % 2, 0:SEQ], act_hi[:, h, :].bitcast(F32),
                                          ALU.subtract).then_inc(S("m_o_lo"), 1)
                    if i == H:
                        split_u(U_UKV + 3)
                for i in range(2):
                    split_u(U_MO + i + 2)

            def diff():
                ch = Chain(dve, S("dve_chain_diff"))
                dve.wait_ge(S("tables_in"), 16 * 9)
                pairs = lam[:, 0:256].rearrange("p (a b d) -> p a b d", a=2, b=2)
                prod = junk_d[:].rearrange("p (a d) -> p a d", a=2)
                ch.link(dve.tensor_tensor(prod, pairs[:, :, 0], pairs[:, :, 1], ALU.mult))
                dve.tensor_reduce(lam[:, 256:258], prod, AX, ALU.add).then_inc(S("lam_sums"), 1)
                for i in range(8):
                    split_u(U_QK + i + 2)
                dve.wait_ge(S("lam_exp"), 1)
                ch.link(dve.tensor_tensor(lam[:, 260:261], lam[:, 259:260], lam[:, 258:259], ALU.subtract))
                ch.link(dve.tensor_scalar(lam[:, 260:261], lam[:, 260:261], -LAM_INIT, None, ALU.add))
                dve.tensor_scalar(lam[:, 261:262], vecs[:, V_SUB:V_SUB + 1], 1.0 - LAM_INIT, None, ALU.mult)\
                    .then_inc(S("d_gain"), 1)

                def maxima(h):
                    dve.wait_ge(S("d_scores"), h + 1)
                    b = 4 + 2 * (h % 2)
                    ch.link(dve.tensor_reduce(soft[:, h, 0, 0:4].rearrange("p (j t) -> p j t", j=2),
                                              psum[:, b:b + 2, :].rearrange("p j (t k) -> p j t k", t=2), AX, ALU.max))
                    dve.tensor_scalar(soft[:, h, 1, 0:4], soft[:, h, 0, 0:4], -D_SCALE, None, ALU.mult)\
                        .then_inc(S("d_bias"), 1)

                def maps(h):
                    dve.wait_ge(S("d_exp"), 4 * h + 4)
                    ch.link(dve.reciprocal(soft[:, h, 3, 0:4], soft[:, h, 2, 0:4]))
                    ch.link(dve.scalar_tensor_tensor(soft[:, h, 3, 2:4], soft[:, h, 3, 2:4], lam[:, 260:261],
                                                     soft[:, h, 2, 0:2], ALU.mult, ALU.mult))
                    if h >= 2:
                        dve.wait_ge(S("d_turned"), h - 1)
                    for t in range(TT):
                        dve.scalar_tensor_tensor(d_a[:, h % 2, t, :], d_x[:, h % 3, 2 + t, :], soft[:, h, 3, 2 + t:3 + t],
                                                 d_x[:, h % 3, t, :], ALU.mult, ALU.add).then_inc(S("d_maps"), 1)

                def heads_normed(g):
                    dve.wait_ge(S("rstd"), root_no("heads", g))
                    for t in range(TT):
                        c = 8 * g + 4 * t
                        heads = d_o[:, t, 4 * g:4 * g + 4, :]
                        dve.tensor_tensor(heads, heads, st[:, ST_OF["heads"], c:c + 4].unsqueeze(2)
                                          .broadcast_to([P, 4, P]), ALU.mult).then_inc(S("d_normed"), 1)

                def heads_lo(g):
                    for b in (2 * g, 2 * g + 1):
                        dve.wait_ge(S("d_hi"), b + 1)
                        dve.scalar_tensor_tensor(act_lo[:, 2 * b:2 * b + 2, :],
                                                 psum[:, 4 + b, :].rearrange("p (k t) -> p k t", k=2), lam[:, 261:262],
                                                 act_hi[:, 2 * b:2 * b + 2, :].bitcast(F32), ALU.mult, ALU.subtract)\
                            .then_inc(S("d_lo"), 1)

                split_u(U_V + 2)
                maxima(0)
                split_u(U_V + 3)
                maxima(1)
                split_u(U_V + 4)
                dve.wait_ge(S("used_u"), U_V + 4)
                dve.tensor_copy(d_v[:, 1, :].rearrange("p (a b) -> p a b", a=2), psum[:, 2:4, :])\
                    .then_inc(S("d_v_out"), 1)
                for i in range(H):
                    maps(i)
                    if i + 2 < H:
                        maxima(i + 2)
                    if i == 6:
                        heads_normed(0)
                heads_lo(0)
                split_u(U_V + 5)
                heads_normed(1)
                split_u(U_DO + 2)
                heads_lo(1)
                split_u(U_DO + 3)

            def mix():
                ch = Chain(dve, S("dve_chain_mix"))
                both = lambda v: v.rearrange("p (h t) -> p h t", h=2)
                flat = lambda v: v.rearrange("p a b -> p (a b)")
                lb = vecs[:, V_LB:V_LB + 4]
                dve.tensor_tensor(bound[:, 0, :], lb, lb, ALU.subtract).then_inc(S("lb_shifted"), 1)
                for u in (U_NQ + 2, U_NQ + 3, U_NC + 2):
                    split_u(u)
                dve.wait_ge(S("used_u"), U_NC + 1)
                for v in range(2):
                    for g in range(2):
                        src = psum[g * HD:g * HD + HD, 6, v * SEQ:v * SEQ + SEQ].rearrange("p (c i l) -> p l i c", i=8, l=2)
                        for l in range(2):
                            r = slice(l * HD, l * HD + HD)
                            for half_block in range(2):
                                i0 = 8 * half_block
                                emb = vecs[r, V_POSK + 16 * v + i0:V_POSK + 16 * v + i0 + 8]
                                dve.tensor_tensor(c_x[r, v, i0:i0 + 8, g * NB:g * NB + NB],
                                                  src[:, l, :, half_block:half_block + NB],
                                                  emb.unsqueeze(2).broadcast_to([HD, 8, NB]), ALU.add)\
                                    .then_inc(S("c_x_done"), 1)
                split_u(U_NK + 2)
                for v in range(2):
                    dve.wait_ge(S("c_hi"), v + 1)
                    dve.tensor_tensor(c_xlo[:, v], c_x[:, v], c_xhi[:, v].bitcast(F32), ALU.subtract)\
                        .then_inc(S("c_lo"), 1)
                split_u(U_NV + 2)
                dve.wait_ge(S("used_u"), U_NV + 2)
                for i, dst in enumerate((n_vs, n_vw, n_g)):
                    n = dst.shape[2]
                    dve.tensor_copy(dst, psum[:, 2:4, P * i:P * i + n]).then_inc(S("n_v_out"), 1)
                split_u(U_NV + 3)
                for u in range(U_H + 2, U_HI + 3):
                    split_u(u)
                dve.wait_ge(S("n_gates"), 1)
                cmp_gate = n_g.rearrange("p t (h b) -> p t h b", b=3)[:, :, :, 0]
                ch.put(dve.tensor_tensor(cmp_gate, cmp_gate, crows[:].unsqueeze(2).broadcast_to([P, TT, H]), ALU.mult))
                dve.wait_ge(S("lb_exp"), 1)
                ch.link(dve.reciprocal(bound[:, 2, :], bound[:, 1, :]))
                ch.link(dve.tensor_tensor(bound[:, 3, :], bound[:, 1, :], bound[:, 2, :], ALU.mult))
                ch.link(dve.tensor_tensor(bound[:, 4, :], bound[:, 3, :], bound[:, 3, :], ALU.subtract))
                ch.link(dve.tensor_scalar(bound[:, 5, :], bound[:, 4, :], -1.0, 1.0, ALU.mult, ALU.add))
                for h in range(HGH):
                    if h == 2:
                        split_u(U_HI + 3)
                    dve.wait_ge(S("h_fk_out"), 2 * (h // 2) + 2)
                    ch.put(dve.tensor_scalar(h_f[:, h, :], h_f[:, h, :], bound[:, 5, h:h + 1], bound[:, 4, h:h + 1],
                                             ALU.mult, ALU.add))
                    ch.put(dve.tensor_scalar(h_k[:, h, :], h_k[:, h, :], bound[:, 5, h:h + 1], None, ALU.mult))
                split_u(U_HI + 4)
                ch.wait()
                dve.tensor_scalar(h_f, h_f, 1e-30, None, ALU.max).then_inc(S("h_ready"), 1)
                for t in range(TT):
                    dve.wait_ge(S("used_u"), U_HI + 4)
                    dve.tensor_copy(h_v[:, t, :], psum[:, 2 * t, :]).then_inc(S("h_v_out"), 1)
                gate = h_g.rearrange("p t (h d) -> p (t h) d", h=HGH)

                def take_level(l, t):
                    dve.wait_ge(S("h_level"), 2 * l + t + 1)
                    if l:
                        dve.wait_ge(S("h_a_done"), 2 * l + t - 1)
                    elif t == 0:
                        dve.wait_ge(S("h_a_zero"), 1)
                    dve.copy_predicated(h_a[:, 4 * t:4 * t + 4, :],
                                        masks[:, l:l + 1, :].bitcast(U32).broadcast_to([P, 4, P]),
                                        psum[:, 3, :].rearrange("p (b c) -> p b c", b=4)).then_inc(S("h_a_done"), 1)

                def decay_q(l):
                    if l == 0:
                        dve.tensor_tensor(h_q, h_q, h_f, ALU.mult).then_inc(S("h_q_upd"), 1)
                        return
                    m = 1 << (l - 1)
                    e = decay_of(m).rearrange("p (n s) -> p n s", s=2)
                    right = flat(h_q).rearrange("p (n s m) -> p n s m", s=2, m=m)[:, :, 1, :]
                    dve.wait_ge(S("h_q_upd"), l)
                    if l >= 2:
                        dve.wait_ge(S("h_e"), l - 1)
                    dve.tensor_tensor(right, right, e[:, :, 0:1].broadcast_to([P, 512 // m, m]), ALU.mult)\
                        .then_inc(S("h_q_upd"), 1)

                dve.wait_ge(S("h_ready"), 1)
                for i in range(H + 2):
                    if 1 <= i <= 8:
                        take_level(i - 1, 0)
                    if 1 <= i <= H:
                        h = i - 1
                        dve.wait_ge(S("n_exp"), 6 * h + 6)
                        ch.link(dve.reciprocal(soft[:, h, 3, 0:6], soft[:, h, 2, 0:6]))
                        r = soft[:, h, 3, 0:6].rearrange("p (b t) -> p b t", b=3)
                        gates = n_g[:, :, 3 * h:3 * h + 3].rearrange("p t b -> p b t")
                        dve.tensor_tensor(r, r, gates, ALU.mult).then_inc(S("n_factors"), 1)
                        dve.wait_ge(S("n_factors"), h + 1)
                        x = n_x[:, h % 2, :]
                        for m, (at, n) in enumerate(N_PARTS[:N_DVE]):
                            dve.tensor_scalar(x[:, at:at + n], x[:, at:at + n], soft[:, h, 3, m:m + 1], None, ALU.mult)\
                                .then_inc(S("n_probs"), 1)
                    if i < H:
                        dve.wait_ge(S("n_scores"), i + 1)
                        b = 4 + 2 * (i % 2)
                        mx = soft[:, i, 0, 2:6].rearrange("p (b t) -> p b t", b=2)
                        ch.put(dve.tensor_reduce(mx[:, :, 0:1], psum[:, b:b + 2, 0:P], AX, ALU.max))
                        ch.put(dve.tensor_reduce(mx[:, :, 1:2], psum[:, b:b + 2, P:3 * P], AX, ALU.max))
                        ch.link(dve.tensor_reduce(soft[:, i, 0, 0:2], psum[:, b, 384:414]
                                                  .rearrange("p (m k) -> p m k", m=2), AX, ALU.max))
                        dve.tensor_scalar(soft[:, i, 1, 0:6], soft[:, i, 0, 0:6], -D_SCALE, None, ALU.mult)\
                            .then_inc(S("n_bias"), 1)
                    if 1 <= i <= 8:
                        take_level(i - 1, 1)
                        decay_q(i - 1)
                    if i >= 2 and i % 2:
                        j = (i - 2) // 2
                        dve.wait_ge(S("n_o_hi"), j + 1)
                        dve.tensor_tensor(act_lo[:, j, :], psum[:, 2, 0:SEQ], act_hi[:, j, :].bitcast(F32),
                                          ALU.subtract).then_inc(S("n_o_lo"), 1)
                split_u(U_HI + 5)
                dve.wait_ge(S("h_g_gained"), 1)
                dve.wait_ge(S("h_squares"), 1)
                dve.tensor_reduce(st[:, ST_OF["hgrn"], 0:8], h_sq, AX, ALU.add).then_inc(S("h_sums"), 1)
                dve.wait_ge(S("rstd"), root_no("hgrn"))
                o = h_o.rearrange("p t h d -> p (t h) d")
                for t in range(TT):
                    s = slice(4 * t, 4 * t + 4)
                    ch.put(dve.tensor_tensor(o[:, s], psum[:, 4 + t, :].rearrange("p (h d) -> p h d", h=HGH),
                                             st[:, ST_OF["hgrn"], s].unsqueeze(2).broadcast_to([P, 4, P]), ALU.mult))
                for t in range(TT):
                    s = slice(4 * t, 4 * t + 4)
                    ch.wait(ch.n - 1 + t)
                    dve.tensor_tensor(o[:, s], o[:, s], gate[:, s], ALU.mult).then_inc(S("h_gated"), 1)
                split_u(U_WO + 2)
                for b in range(2):
                    dve.wait_ge(S("h_hi"), b + 1)
                    dve.tensor_tensor(act_lo[:, 4 + 2 * b:6 + 2 * b, :], both(psum[:, 6 + b, :]),
                                      act_hi[:, 4 + 2 * b:6 + 2 * b, :].bitcast(F32), ALU.subtract).then_inc(S("h_lo"), 1)
                split_u(U_WO + 3)

            dve.memset(zeros[:], 0.0).then_inc(S("zeros_set"), 1)
            norm(N_MLA)
            mla()
            post(0)
            norm(N_F0)
            ffn(0)
            post(1)
            norm(N_DIFF)
            diff()
            post(2)
            norm(N_F1)
            ffn(1)
            post(3)
            norm(N_F2)
            ffn(2)
            add(0.5, [("first_part", 3), ("used_d", 3 * FT)])
            norm(N_MIX)
            mix()
            add(1.0, [("first_half", 3), ("used_u", U_WO + 4)])
            norm(N_F3)
            ffn(3)
            add(0.5, [("first_part", 4), ("used_d", 4 * FT)])
            norm(N_FINAL)


_INS = ["x", "norm_g", "ffn_w_up", "ffn_conv_w", "ffn_conv_b", "ffn_w_down", "mla_w_dq", "mla_q_norm_g", "mla_w_uq",
        "mla_w_dkv", "mla_kv_norm_g", "mla_w_ukv", "mla_w_o", "diff_w_qkv", "diff_lambda", "diff_subln_g", "diff_w_o",
        "ffn1_norm_2", "ffn1_w_gu_2", "ffn1_w_down_2", "mix_norm_2", "w_in_2", "cmp_pos_k_2", "cmp_pos_v_2",
        "cmp_k_w1_2", "cmp_k_w2_2", "cmp_v_w1_2", "cmp_v_w2_2", "hgrn_lower_bound_2", "hgrn_out_norm_2", "w_out_2",
        "ffn2_norm_2", "ffn2_w_gu_2", "ffn2_w_down_2", "final_norm_2"]


def kernel(**inputs):
    import concourse.bacc as bacc
    from concourse.bass_utils import run_bass_kernel_spmd

    nc = bacc.Bacc("TRN2", target_bir_lowering=False, num_devices=1)
    arrays, aps = {}, {}

    def give(name, array):
        arrays[f"in_{name}"] = array
        aps[name] = nc.dram_tensor(f"in_{name}", array.shape, mybir.dt.from_np(array.dtype), kind="ExternalInput").ap()

    for name in _INS:
        x = np.ascontiguousarray(inputs[name])
        give(name, x)
    for name, table in constants().items():
        give(name, np.ascontiguousarray(table))
    out = nc.dram_tensor("out_0", (1, SEQ, D), F32, kind="ExternalOutput").ap()
    program(nc, aps, out)
    r = run_bass_kernel_spmd(nc, [arrays], core_ids=[0])
    return r.results[0]["out_0"]
```
